# Optimizing a Trainium2 kernel written in Bass

```python
import jax, jax.numpy as jnp
from jax import lax
import numpy as np

D_MODEL = 1024
BATCH = 1
SEQ = 1024
DEPTH = 1
DEC_BATCH = 8
DEC_SEQ = 1
PAST_LEN = 8192
PAGE_SIZE = 128

HEAD_DIM = 64
N_Q_HEADS = 8
N_KV_HEADS = 2
Q_PER_KV = N_Q_HEADS // N_KV_HEADS
ATTN_WIDTH = N_Q_HEADS * HEAD_DIM
KV_WIDTH = N_KV_HEADS * HEAD_DIM
WINDOW = 128
ROPE_THETA = 10000.0
GMLP_WIDTH = D_MODEL - ATTN_WIDTH
GMLP_GROUPS = 8
GMLP_GROUP_DIM = GMLP_WIDTH // GMLP_GROUPS
CHUNK = 128
MIX_WIDTH = ATTN_WIDTH + GMLP_WIDTH
Q_END = ATTN_WIDTH
K_END = Q_END + KV_WIDTH
V_END = K_END + KV_WIDTH
U_END = V_END + GMLP_WIDTH
IN_PROJ_WIDTH = U_END + GMLP_WIDTH
N_GROUPS = 4
EXPERTS_PER_GROUP = 8
N_EXPERTS = N_GROUPS * EXPERTS_PER_GROUP
TOP_K = 2
D_EXPERT = 256
EPS = 1e-6
NEG_INF = -1e30

kernel_name = "hymba_swa_sink_gmlp_hier_moe_step"

def rmsnorm(x, g):
    xf = x.astype(jnp.float32)
    y = xf * lax.rsqrt(jnp.mean(xf * xf, axis=-1, keepdims=True) + EPS)
    return (y * g.astype(jnp.float32)).astype(x.dtype)

def layernorm(x, g, b):
    xf = x.astype(jnp.float32)
    mu = jnp.mean(xf, axis=-1, keepdims=True)
    xc = xf - mu
    y = xc * lax.rsqrt(jnp.mean(xc * xc, axis=-1, keepdims=True) + EPS)
    return (y * g.astype(jnp.float32) + b.astype(jnp.float32)).astype(x.dtype)

def rope(x, pos):
    half = HEAD_DIM // 2
    inv_freq = ROPE_THETA ** (-jnp.arange(half, dtype=jnp.float32) * 2.0 / HEAD_DIM)
    ang = pos.astype(jnp.float32)[:, None] * inv_freq[None, :]
    cos = jnp.cos(ang)[:, None, :]
    sin = jnp.sin(ang)[:, None, :]
    xf = x.astype(jnp.float32)
    x1, x2 = xf[..., :half], xf[..., half:]
    return jnp.concatenate([x1 * cos - x2 * sin, x2 * cos + x1 * sin], axis=-1).astype(x.dtype)

def sink_softmax(scores, mask, sinks_kg):
    s = jnp.where(mask, scores, NEG_INF)
    sink = jnp.broadcast_to(sinks_kg.astype(jnp.float32)[:, :, None, None], s.shape[:-1] + (1,))
    p = jax.nn.softmax(jnp.concatenate([s, sink], axis=-1), axis=-1)
    return p[..., :-1]

def mix_inputs(x, norm_g, w_in):
    b, s = x.shape[:2]
    z = rmsnorm(x, norm_g) @ w_in
    q = z[..., :Q_END].reshape(b, s, N_Q_HEADS, HEAD_DIM)
    k = z[..., Q_END:K_END].reshape(b, s, N_KV_HEADS, HEAD_DIM)
    v = z[..., K_END:V_END].reshape(b, s, N_KV_HEADS, HEAD_DIM)
    u = jax.nn.gelu(z[..., V_END:U_END], approximate=False)
    vg = jax.nn.gelu(z[..., U_END:], approximate=False)
    return q, k, v, u, vg

def swa_prompt(q, k, v, sinks):
    b, s = q.shape[:2]
    nb = s // WINDOW
    qb = q.reshape(b, nb, WINDOW, N_KV_HEADS, Q_PER_KV, HEAD_DIM)
    kb = k.reshape(b, nb, WINDOW, N_KV_HEADS, HEAD_DIM)
    vb = v.reshape(b, nb, WINDOW, N_KV_HEADS, HEAD_DIM)
    pad = ((0, 0), (1, 0), (0, 0), (0, 0), (0, 0))
    kk = jnp.concatenate([jnp.pad(kb, pad)[:, :-1], kb], axis=2)
    vv = jnp.concatenate([jnp.pad(vb, pad)[:, :-1], vb], axis=2)
    scores = jnp.einsum('bnqkgd,bnskd->bnkgqs', qb, kk,
                        preferred_element_type=jnp.float32) * (HEAD_DIM ** -0.5)
    blk = jnp.arange(nb, dtype=jnp.int32)[:, None, None] * WINDOW
    qpos = blk + jnp.arange(WINDOW, dtype=jnp.int32)[None, :, None]
    kpos = blk - WINDOW + jnp.arange(2 * WINDOW, dtype=jnp.int32)[None, None, :]
    diff = qpos - kpos
    mask = (diff >= 0) & (diff <= WINDOW) & (kpos >= 0)
    p = sink_softmax(scores, mask[None, :, None, None], sinks.reshape(N_KV_HEADS, Q_PER_KV))
    o = jnp.einsum('bnkgqs,bnskd->bnqkgd', p.astype(vv.dtype), vv)
    return o.reshape(b, s, ATTN_WIDTH)

def swa_sample(q, k_new, v_new, k_cache, v_cache, sinks):
    db, s = q.shape[:2]
    kk = jnp.concatenate([k_cache, k_new], axis=1)
    vv = jnp.concatenate([v_cache, v_new], axis=1)
    qg = q.reshape(db, s, N_KV_HEADS, Q_PER_KV, HEAD_DIM)
    scores = jnp.einsum('bqkgd,bskd->bkgqs', qg, kk,
                        preferred_element_type=jnp.float32) * (HEAD_DIM ** -0.5)
    qpos = WINDOW + jnp.arange(s, dtype=jnp.int32)[:, None]
    kpos = jnp.arange(kk.shape[1], dtype=jnp.int32)[None, :]
    diff = qpos - kpos
    mask = (diff >= 0) & (diff <= WINDOW)
    p = sink_softmax(scores, mask[None, None, None], sinks.reshape(N_KV_HEADS, Q_PER_KV))
    o = jnp.einsum('bkgqs,bskd->bqkgd', p.astype(vv.dtype), vv)
    return o.reshape(db, s, ATTN_WIDTH)

def causal_spatial(w_s):
    tril = jnp.tril(jnp.ones((CHUNK, CHUNK), dtype=bool))
    return jnp.where(tril[None], w_s, jnp.zeros_like(w_s))

def gmlp_prompt(u, vn, w_s, b_s):
    b, s = u.shape[:2]
    vc = vn.reshape(b, s // CHUNK, CHUNK, GMLP_GROUPS, GMLP_GROUP_DIM)
    sp = jnp.einsum('gts,bnsgd->bntgd', causal_spatial(w_s), vc) + b_s.T[None, None, :, :, None]
    return u * sp.reshape(b, s, GMLP_WIDTH)

def gmlp_sample(u, vn, w_s, b_s):
    db, s = u.shape[:2]
    vc = vn.reshape(db, s, GMLP_GROUPS, GMLP_GROUP_DIM)
    wm = causal_spatial(w_s)[:, :s, :s]
    sp = jnp.einsum('gts,bsgd->btgd', wm, vc) + b_s[:, :s].T[None, :, :, None]
    return u * sp.reshape(db, s, GMLP_WIDTH)

def hier_moe(h, w_rg, b_rg, w_re, b_re, w_gate, w_up, w_down):
    shape = h.shape
    t = h.reshape(-1, D_MODEL)
    n = t.shape[0]
    g_logits = jnp.einsum('td,dg->tg', t, w_rg, preferred_element_type=jnp.float32) + b_rg.astype(jnp.float32)
    g_prob = jax.nn.softmax(g_logits, axis=-1)
    g_idx = jnp.argmax(g_logits, axis=-1)
    g_w = jnp.take_along_axis(g_prob, g_idx[:, None], axis=-1)
    e_logits = jnp.einsum('td,dge->tge', t, w_re, preferred_element_type=jnp.float32) + b_re.astype(jnp.float32)
    e_sel = jnp.take_along_axis(e_logits, g_idx[:, None, None], axis=1)[:, 0]
    e_prob = jax.nn.softmax(e_sel, axis=-1)
    top_w, top_i = lax.top_k(e_prob, TOP_K)
    top_w = top_w / jnp.sum(top_w, axis=-1, keepdims=True)
    within = jnp.sum(jax.nn.one_hot(top_i, EXPERTS_PER_GROUP, dtype=jnp.float32) * top_w[..., None], axis=1)
    combine = (jax.nn.one_hot(g_idx, N_GROUPS, dtype=jnp.float32)[:, :, None]
               * within[:, None, :] * g_w[:, :, None]).reshape(n, N_EXPERTS)
    y = jnp.zeros((n, D_MODEL), jnp.float32)
    for e in range(N_EXPERTS):
        hid = jax.nn.silu(t @ w_gate[e]) * (t @ w_up[e])
        y = y + combine[:, e:e + 1] * (hid @ w_down[e]).astype(jnp.float32)
    return y.astype(h.dtype).reshape(shape)

def setup_inputs(seed: int = 0) -> dict:
    key = jax.random.key(seed)
    ks = jax.random.split(key, 24)
    f32 = jnp.float32
    nrm = lambda k, shp, sc: jax.random.normal(k, shp, f32) * sc
    return {
        "x_prompt": nrm(ks[0], (BATCH, SEQ, D_MODEL), 1.0),
        "x_sample": nrm(ks[1], (DEC_BATCH, DEC_SEQ, D_MODEL), 1.0),
        "cache_swa_k": nrm(ks[2], (DEPTH, DEC_BATCH, WINDOW, N_KV_HEADS, HEAD_DIM), 1.0),
        "cache_swa_v": nrm(ks[3], (DEPTH, DEC_BATCH, WINDOW, N_KV_HEADS, HEAD_DIM), 1.0),
        "norm_mix_g": 1.0 + nrm(ks[4], (DEPTH, D_MODEL), 0.02),
        "w_in": nrm(ks[5], (DEPTH, D_MODEL, IN_PROJ_WIDTH), D_MODEL ** -0.5),
        "attn_sinks": nrm(ks[6], (DEPTH, N_Q_HEADS), 0.5),
        "gmlp_ln_g": 1.0 + nrm(ks[7], (DEPTH, GMLP_WIDTH), 0.02),
        "gmlp_ln_b": nrm(ks[8], (DEPTH, GMLP_WIDTH), 0.02),
        "gmlp_w_s": nrm(ks[9], (DEPTH, GMLP_GROUPS, CHUNK, CHUNK), CHUNK ** -0.5),
        "gmlp_b_s": 1.0 + nrm(ks[10], (DEPTH, GMLP_GROUPS, CHUNK), 0.1),
        "w_out": nrm(ks[11], (DEPTH, MIX_WIDTH, D_MODEL), MIX_WIDTH ** -0.5),
        "norm_ffn_g": 1.0 + nrm(ks[12], (DEPTH, D_MODEL), 0.02),
        "router_group_w": nrm(ks[13], (DEPTH, D_MODEL, N_GROUPS), D_MODEL ** -0.5),
        "router_group_b": nrm(ks[14], (DEPTH, N_GROUPS), 0.01),
        "router_expert_w": nrm(ks[15], (DEPTH, D_MODEL, N_GROUPS, EXPERTS_PER_GROUP), D_MODEL ** -0.5),
        "router_expert_b": nrm(ks[16], (DEPTH, N_GROUPS, EXPERTS_PER_GROUP), 0.01),
        "expert_w_gate": nrm(ks[17], (DEPTH, N_EXPERTS, D_MODEL, D_EXPERT), D_MODEL ** -0.5),
        "expert_w_up": nrm(ks[18], (DEPTH, N_EXPERTS, D_MODEL, D_EXPERT), D_MODEL ** -0.5),
        "expert_w_down": nrm(ks[19], (DEPTH, N_EXPERTS, D_EXPERT, D_MODEL), D_EXPERT ** -0.5),
        "final_norm_g": 1.0 + nrm(ks[20], (D_MODEL,), 0.02),
    }

def reference(x_prompt, x_sample, cache_swa_k, cache_swa_v, norm_mix_g, w_in, attn_sinks,
              gmlp_ln_g, gmlp_ln_b, gmlp_w_s, gmlp_b_s, w_out, norm_ffn_g,
              router_group_w, router_group_b, router_expert_w, router_expert_b,
              expert_w_gate, expert_w_up, expert_w_down, final_norm_g):
    xp, xs = x_prompt, x_sample
    s_p = xp.shape[1]
    s_s = xs.shape[1]
    pos_p = jnp.arange(s_p, dtype=jnp.int32)
    pos_s = PAST_LEN + jnp.arange(s_s, dtype=jnp.int32)
    kp_l, vp_l, ks_l, vs_l, gs_l = [], [], [], [], []
    for l in range(DEPTH):
        moe_args = (router_group_w[l], router_group_b[l], router_expert_w[l], router_expert_b[l],
                    expert_w_gate[l], expert_w_up[l], expert_w_down[l])
        q, k, v, u, vg = mix_inputs(xp, norm_mix_g[l], w_in[l])
        q = rope(q, pos_p)
        k = rope(k, pos_p)
        att = swa_prompt(q, k, v, attn_sinks[l])
        vn = layernorm(vg, gmlp_ln_g[l], gmlp_ln_b[l])
        gm = gmlp_prompt(u, vn, gmlp_w_s[l], gmlp_b_s[l])
        xp = xp + jnp.concatenate([att, gm], axis=-1) @ w_out[l]
        xp = xp + hier_moe(rmsnorm(xp, norm_ffn_g[l]), *moe_args)
        kp_l.append(k[:, s_p - WINDOW:])
        vp_l.append(v[:, s_p - WINDOW:])
        q, k, v, u, vg = mix_inputs(xs, norm_mix_g[l], w_in[l])
        q = rope(q, pos_s)
        k = rope(k, pos_s)
        att = swa_sample(q, k, v, cache_swa_k[l], cache_swa_v[l], attn_sinks[l])
        vn = layernorm(vg, gmlp_ln_g[l], gmlp_ln_b[l])
        gm = gmlp_sample(u, vn, gmlp_w_s[l], gmlp_b_s[l])
        xs = xs + jnp.concatenate([att, gm], axis=-1) @ w_out[l]
        xs = xs + hier_moe(rmsnorm(xs, norm_ffn_g[l]), *moe_args)
        ks_l.append(k)
        vs_l.append(v)
        gs_l.append(vn)
    y_prompt = rmsnorm(xp, final_norm_g)
    y_sample = rmsnorm(xs, final_norm_g)
    new_k_prompt = jnp.stack(kp_l, axis=0)
    new_v_prompt = jnp.stack(vp_l, axis=0)
    new_k_sample = jnp.stack(ks_l, axis=0)
    new_v_sample = jnp.stack(vs_l, axis=0)
    new_gmlp_v_sample = jnp.stack(gs_l, axis=0)
    return (y_prompt, y_sample, new_k_prompt, new_v_prompt, new_k_sample, new_v_sample, new_gmlp_v_sample)


_drawn_inputs = setup_inputs


def setup_inputs(seed=0):
    import zlib

    import numpy as np

    out = dict(_drawn_inputs(seed))
    spreads = {}
    factors = {'attn_sinks': 8.0,
     'gmlp_ln_g': 7.819,
     'gmlp_ln_b': 8.267,
     'router_group_b': 12.631,
     'router_expert_b': 3.974,
     'final_norm_g': 8.738,
     'norm_ffn_g': 2.668}
    for name, (base, spread) in spreads.items():
        noise = np.random.default_rng([zlib.crc32(name.encode()), seed]).standard_normal(out[name].shape)
        drawn = base * np.exp(spread * noise) if base else spread * noise
        out[name] = __import__('jax').numpy.asarray(drawn.astype(out[name].dtype))
    for name, factor in factors.items():
        out[name] = (out[name] * factor).astype(out[name].dtype)
    return out
```

```python
from contextlib import ExitStack

import concourse.bass as bass
from concourse import mybir

F32 = mybir.dt.float32
F32R = mybir.dt.float32r
BF16 = mybir.dt.bfloat16
I32 = mybir.dt.int32
U32 = mybir.dt.uint32
ALU = mybir.AluOpType
ACT = mybir.ActivationFunctionType
AX = mybir.AxisListType.X

P = 128
D = 1024
DC = D // P
N_PROMPT = 1024
N_SAMPLE = 8
N_TOK = N_PROMPT + N_SAMPLE
T_P = N_PROMPT // P
T = T_P + 1
HD = 64
NQ = 8
NKV = 2
QPK = NQ // NKV
ATT = NQ * HD
GW = 512
NG = 8
Z_COLS = 1792
WIN = 128
NGRP = 4
EPG = 8
NE = 32
FE = 256
EPS = 1e-6
SCALE = HD ** -0.5
NEG = -1e30
SLOTS = 128
PAST = 8192
OV_LINKS = 5
N_CHUNK = -(-N_TOK // SLOTS)
OOB = 100000.0
KC = 256
N_WI = Z_COLS // KC
Z_GROUPS = [(0, 512, 2), (512, 256, 3), (768, 512, 5), (1280, 512, 7)]

C_ID = 0
C_MF = C_ID + P
C_MR = C_MF + 2 * P
C_IO = C_MR + 2 * P
C_TR = C_IO + P
C_PR = C_TR + P
C_SEL = C_PR + 1
C_INV = C_SEL + N_SAMPLE
C_TILE = C_INV + T
C_CS = C_TILE + T
C_END = C_CS + T * HD


class Region:

    def __init__(self, nc, base, start, end):
        self.nc, self.base, self.at, self.end = nc, base, start, end

    def take(self, name, shape, dt):
        n = 1
        for s in shape[1:]:
            n *= s
        size = -(-n * (2 if dt == BF16 else 4) // 32) * 32
        got = self.nc.alloc_sbuf_tensor_at(name, shape, dt, offset=self.base + self.at)
        self.at += size
        assert self.at <= self.end, (name, self.at, self.end)
        return got


class Chain:

    def __init__(self, eng, sem):
        self.eng, self.sem, self.n = eng, sem, 0

    def __call__(self, ins):
        ins.then_inc(self.sem, 1)
        self.n = self.n + 1
        self.eng.wait_ge(self.sem, self.n)


def build(nc, x_rows, cache_k, cache_v, mix_g, w_in, sinks_b, sink_rows, ln_g, ln_b, w_s, b_sT, b_s, w_out, ffn_g,
          w_rg, b_r, w_re, w_gate, w_up, w_down, fin_g, consts,
          y_rows, k_prompt, v_prompt, k_sample, v_sample, g_sample):
    mix_d = nc.dram_tensor("mix_d", [T * P, D], F32).ap()
    h_d = nc.dram_tensor("h_d", [T * P, D], F32).ap()
    y_d = nc.dram_tensor("y_d", [2 * T * P, D], F32).ap()

    ctx = ExitStack()
    with ctx:
        def bank(name, n=1):
            return ctx.enter_context(nc.psum_tensor(name, [P, n * 512], F32))

        def sem(name):
            return ctx.enter_context(nc.semaphore(name))

        psT = [bank("psT0"), bank("psT1")]
        psZ = [bank("psZ0"), bank("psZ1")]
        psS = bank("psS", 2)
        psO = bank("psO")
        psG = bank("psG")

        base = 16512
        r1 = Region(nc, base, 0, 114688)
        r2 = Region(nc, base, 114688, 147456)
        r3 = Region(nc, base, 147456, 212800)
        cst = r3.take("cst", [P, C_END], F32)
        w_of = r3.take("w_of", [P, 2, T], F32)
        small = r3.take("small", [P, 64], F32)
        wi_hi = r1.take("wi_hi", [P, DC, Z_COLS], F32R)
        wi_lo = r1.take("wi_lo", [P, DC, Z_COLS], F32R)
        w_stage = [r2.take(f"w_stage{n}", [P, DC * KC], F32) for n in range(3)]
        x_t = r2.take("x_t", [P, D], F32)
        q_ro = r2.take("q_ro", [P, ATT], F32)
        qT = r2.take("qT", [P, QPK, P], F32)
        a1 = r3.at
        mix_t = r3.take("mix_t", [P, D], F32)
        xT_hi = r3.take("xT_hi", [P, DC, P], F32R)
        xT_lo = r3.take("xT_lo", [P, DC, P], F32R)
        k_ro = r3.take("k_ro", [P, P], F32)
        kT = r3.take("kT", [P, 2 * P], F32)
        v_t = r3.take("v_t", [P, 2, P], F32)
        v_new = r3.take("v_new", [P, P], F32)
        u_t = r3.take("u_t", [P, GW], F32)
        vg_t = r3.take("vg_t", [P, GW], F32)
        vn_t = r3.take("vn_t", [P, GW], F32)
        s_at = r3.at
        s_t = [r3.take(f"s_t{g}", [P, QPK, 2 * P], F32) for g in range(2)]
        s_end = r3.at
        r_tmp = Region(nc, base, s_at, s_end)
        ws_raw = r_tmp.take("ws_raw", [P, NG, P], F32)
        kc_t = r_tmp.take("kc_t", [P, N_SAMPLE, P], F32)
        pT = r3.take("pT", [P, 2 * QPK, P], F32)
        lng = r3.take("lng", [P, GW], F32)
        lnb = r3.take("lnb", [P, GW], F32)
        wsT = r3.take("wsT", [P, NG, P], F32)
        rope_a = r3.take("rope_a", [P, ATT], F32)
        rope_b = r3.take("rope_b", [P, ATT], F32)
        junk = r3.take("junk", [P, D], BF16)
        kcT = r3.take("kcT", [P, N_SAMPLE, P], F32)
        csr = r3.take("csr", [P, HD], F32)
        sink_t = r3.take("sink_t", [P, NQ], F32)
        bsT = r3.take("bsT", [P, NG], F32)
        gmix = r3.take("gmix", [P, DC], F32)
        st = r3.take("st", [P, 64], F32)
        sinkr = r3.take("sinkr", [P, 1], F32)
        w00 = r3.take("w00", [P, NG], F32)
        b00 = r3.take("b00", [P, NG], F32)
        r_s = Region(nc, base, 114688, 114688 + 8192)
        vc_t = r_s.take("vc_t", [P, N_SAMPLE, P], F32)
        sT_s = r_s.take("sT_s", [P, NKV, 32], F32)
        prod = r_s.take("prod", [P, 64], F32)
        s_s = r_s.take("s_s", [64, 132], F32)
        pT_s = r_s.take("pT_s", [P, 64], F32)
        selp = r_s.take("selp", [64, N_SAMPLE], F32)
        d_s = r_s.take("d_s", [N_SAMPLE, 64], F32)
        oT_s = r_s.take("oT_s", [P, N_SAMPLE, QPK], F32)
        q1 = Region(nc, base, 0, 114688)
        wo_hi = q1.take("wo_hi", [P, DC, D], F32R)
        wo_lo = q1.take("wo_lo", [P, DC, D], F32R)
        x1a = Region(nc, base, 114688, 147456).take("x1a", [P, T_P, D], F32)
        s2 = Region(nc, base, a1, 212800)
        x1b = s2.take("x1b", [P, D], F32)
        m_t = [s2.take(f"m_t{b}", [P, D], F32) for b in range(2)]
        mT_hi = [s2.take(f"mT_hi{b}", [P, DC, P], F32R) for b in range(2)]
        mT_lo = [s2.take(f"mT_lo{b}", [P, DC, P], F32R) for b in range(2)]
        h_t = s2.take("h_t", [P, D], F32)
        hT = s2.take("hT", [P, DC, P], F32)
        ffg = s2.take("ffg", [P, D], F32)
        junk2 = s2.take("junk2", [P, D], BF16)
        w_r = s2.take("w_r", [P, DC, NGRP + NE], F32)
        b_rt = s2.take("b_rt", [P, NGRP + NE], F32)
        logits = s2.take("logits", [P, T, NGRP + NE], F32)
        s3 = Region(nc, base, s2.at, 212800)
        idx_src = s3.take("idx_src", [P, NE], I32)
        idx_dst = s3.take("idx_dst", [P, NE], I32)
        rk = s3.take("rk", [P, 2, T], F32)
        rhs_t = s3.take("rhs_t", [P, 2, T, 3 * NE], BF16)
        s3b = Region(nc, base, a1 + 4 * D, a1 + 4 * D + 8 * D + 16 * D)
        one_e = s3b.take("one_e", [P, 2, T, NE], F32)
        m_bf = s3b.take("m_bf", [P, T, NE], BF16)
        rank_s = s3b.take("rank_s", [P, T, NE], F32)
        tmp_e = s3b.take("tmp_e", [P, T, NE], F32)
        g8 = [s3b.take(f"g8_{n}", [P, T, EPG], F32) for n in range(6)]
        c9 = [s3b.take(f"c9_{n}", [P, T], F32) for n in range(12)]
        oh_r = s3b.take("oh_r", [P, 2, T, P], BF16)
        tr_bf = s3b.take("tr_bf", [P, P], BF16)
        on_bf = s3b.take("on_bf", [P, P], BF16)
        tab = s3b.take("tab", [P, 3 * NE], F32)
        tab2 = s3b.take("tab2", [P, 3, NE], F32)
        cnt_i = s3b.take("cnt_i", [P, 1], I32)
        wg = []
        wd = []
        for n, at in enumerate([65536, 90112, 0, 24576]):
            e = Region(nc, base, at, at + 24576)
            wg.append(e.take(f"wg{n}", [P, 2, DC, FE], F32))
            wd.append(e.take(f"wd{n}", [P, 2, D], F32))
        s4 = Region(nc, base, s3b.at, a1 + 28 * D + 14 * D)
        xg = [s4.take(f"xg{b}", [P, D], F32) for b in range(2)]
        xg += [Region(nc, base, at, at + 4 * D).take(f"xg{2 + n}", [P, D], F32) for n, at in enumerate([49152, 53248])]
        xgT = s4.take("xgT", [P, DC, P], F32)
        y_t = [s4.take(f"y_t{b}", [P, D], F32) for b in range(2)]
        sg = s4.take("sg", [P, FE], F32)
        hid = s4.take("hid", [P, FE], F32)
        hidT = s4.take("hidT", [P, 2, P], F32)
        ic_src = s4.take("ic_src", [P, 4], I32)
        ic_dst = s4.take("ic_dst", [P, 4], I32)
        s6 = Region(nc, base, 0, 65536)
        yy = [s6.take(f"yy{b}", [P, 2, D], F32) for b in range(2)]
        out_t = [s6.take(f"out_t{b}", [P, D], F32) for b in range(2)]
        fing = s6.take("fing", [P, D], F32)
        junk3 = s6.take("junk3", [P, D], BF16)
        fst = s6.take("fst", [P, 2, 4], F32)

        ident = cst[:, C_ID:C_ID + P]

        def x1(t):
            if isinstance(t, int) and t == T_P:
                return x1b[:]
            return x1a[:, t, :] if isinstance(t, int) else x1a[:, bass.ds(t, 1), :].squeeze(1)

        def rows(ap, t, n=P):
            return ap[t * P:t * P + n, :] if isinstance(t, int) else ap[bass.ds(t * P, n), :]

        s_settled = sem("s_settled")
        s_cst = sem("s_cst")
        s_small = sem("s_small")
        s_gmix = sem("s_gmix")
        s_ws = sem("s_ws")
        s_kc = sem("s_kc")
        s_vc = sem("s_vc")
        s_wraw = [sem(f"s_wraw{n}") for n in range(3)]
        s_x = sem("s_x")
        s_whi = sem("s_whi")
        s_wlo = sem("s_wlo")
        s_zero = sem("s_zero")
        s_wmask = sem("s_wmask")
        s_tset = sem("s_tset")
        s_eset_a = sem("s_eset_a")
        s_eset_v = sem("s_eset_v")
        s_sq = sem("s_sq")
        s_rstd = sem("s_rstd")
        s_xTp = sem("s_xTp")
        s_xh = sem("s_xh")
        s_xl = sem("s_xl")
        s_z = sem("s_z")
        s_csr = sem("s_csr")
        s_qr = sem("s_qr")
        s_kr = sem("s_kr")
        s_qkTp = sem("s_qkTp")
        s_qT = sem("s_qT")
        s_kT = sem("s_kT")
        s_v = sem("s_v")
        s_vs = sem("s_vs")
        s_u = sem("s_u")
        s_vg = sem("s_vg")
        s_var = sem("s_var")
        s_lnr = sem("s_lnr")
        s_vn = sem("s_vn")
        s_sc = sem("s_sc")
        s_sm = sem("s_sm")
        s_nb = sem("s_nb")
        s_p = sem("s_p")
        s_pTp = sem("s_pTp")
        s_pTa = sem("s_pTa")
        s_pTv = sem("s_pTv")
        s_pv = sem("s_pv")
        s_gm = sem("s_gm")
        s_gmo = sem("s_gmo")
        s_att = sem("s_att")
        s_mix = sem("s_mix")
        s_kvout = sem("s_kvout")
        dve_step = sem("dve_step")
        act_step = sem("act_step")
        pool_step = sem("pool_step")
        s_sp = sem("s_sp")
        s_sv = sem("s_sv")
        s_sa = sem("s_sa")
        s_ml = [sem(f"s_ml{b}") for b in range(2)]
        s_xr = [sem(f"s_xr{b}") for b in range(2)]
        s_p2 = sem("s_p2")
        s_mTp = sem("s_mTp")
        s_mh = sem("s_mh")
        s_mlo = sem("s_mlo")
        s_op = sem("s_op")
        s_x1 = sem("s_x1")
        s_sq2 = sem("s_sq2")
        s_r2 = sem("s_r2")
        s_h = sem("s_h")
        s_hst = sem("s_hst")
        s_hTp = sem("s_hTp")
        s_hTa = sem("s_hTa")
        s_hTv = sem("s_hTv")
        s_lg = sem("s_lg")
        s_lgo = sem("s_lgo")
        s_rv = sem("s_rv")
        s_ra = sem("s_ra")
        s_rp = sem("s_rp")
        s_idx = sem("s_idx")
        s_w = [sem(f"s_w{n}") for n in range(4)]
        s_isrc = sem("s_isrc")
        s_idst = sem("s_idst")
        s_ga = [sem(f"s_ga{k}") for k in range(4)]
        s_gTp = sem("s_gTp")
        s_gTa = sem("s_gTa")
        s_gTv = sem("s_gTv")
        s_gu = sem("s_gu")
        s_sg = sem("s_sg")
        s_hid = sem("s_hid")
        s_dTp = sem("s_dTp")
        s_dT = sem("s_dT")
        s_dn = sem("s_dn")
        s_ya = sem("s_ya")
        s_yv = sem("s_yv")
        s_sc4 = [sem(f"s_sc4_{b}") for b in range(2)]
        s_zx = sem("s_zx")
        o_idx = sem("o_idx")
        o_step = sem("o_step")
        o_free = sem("o_free")
        o_oh = sem("o_oh")
        o_tab = sem("o_tab")
        o_ic = sem("o_ic")
        o_w = sem("o_w")
        o_ga = sem("o_ga")
        o_gTp = sem("o_gTp")
        o_gTa = sem("o_gTa")
        o_gTv = sem("o_gTv")
        o_gu = sem("o_gu")
        o_sg = sem("o_sg")
        o_hid = sem("o_hid")
        o_dTp = sem("o_dTp")
        o_dT = sem("o_dT")
        o_dn = sem("o_dn")
        o_y = sem("o_y")
        o_ya = sem("o_ya")
        o_sc = sem("o_sc")
        o_done = sem("o_done")
        s_yy = [sem(f"s_yy{b}") for b in range(2)]
        s_fg = sem("s_fg")
        s_ysum = sem("s_ysum")
        s_fsq = sem("s_fsq")
        s_fr = sem("s_fr")
        s_fo = sem("s_fo")
        s_out = [sem(f"s_out{b}") for b in range(2)]

        block = ctx.enter_context(nc.Block())

        def settle(eng):
            eng.sem_inc(s_settled, 1)

        wo_r = w_out.rearrange("(c p) n -> p c n", p=P)
        N_WO = 4
        WO_SLOT = [2, 1, 0, 2]
        WO_TURN = [3, 3, 4, 4]

        @block.sync
        def _(sp):
            sp.dma_start(cst[:], consts).then_inc(s_cst, 16)
            sp.dma_start(gmix[:], mix_g).then_inc(s_gmix, 16)
            wi_r = w_in.rearrange("(c p) n -> p c n", p=P)

            def load_wi(n):
                if n >= 3:
                    sp.wait_ge(s_whi, n - 2)
                    sp.wait_ge(s_wlo, n - 2)
                sp.dma_start(w_stage[n % 3][:].rearrange("p (c n) -> p c n", c=DC),
                             wi_r[:, :, n * KC:(n + 1) * KC]).then_inc(s_wraw[n % 3], 16)

            load_wi(0)
            sp.dma_start(x_t[:], rows(x_rows, 0)).then_inc(s_x, 16)
            load_wi(1)
            load_wi(2)
            sp.dma_start(ws_raw[:], w_s.rearrange("g t s -> t g s")).then_inc(s_ws, 16)
            sp.dma_start(kc_t[:], cache_k.rearrange("b s n -> s b n")).then_inc(s_kc, 16)
            sp.dma_start(sink_t[:], sinks_b.to_broadcast([P, NQ])).then_inc(s_small, 16)
            sp.dma_start(lng[:], ln_g.to_broadcast([P, GW])).then_inc(s_small, 16)
            sp.dma_start(lnb[:], ln_b.to_broadcast([P, GW])).then_inc(s_small, 16)
            sp.dma_start(bsT[:], b_sT).then_inc(s_small, 16)
            sp.dma_start(sinkr[0:64, :], sink_rows).then_inc(s_small, 16)
            with nc.allow_non_contiguous_dma(reason="eight elements"):
                sp.dma_start(w00[0:N_SAMPLE, :], w_s[:, 0:1, 0:1].rearrange("g a b -> (a b) g")
                             .to_broadcast([N_SAMPLE, NG])).then_inc(s_small, 16)
                sp.dma_start(b00[0:N_SAMPLE, :], b_s[:, 0:1].rearrange("g a -> a g")
                             .to_broadcast([N_SAMPLE, NG])).then_inc(s_small, 16)
            for n in range(3, N_WI):
                load_wi(n)

            def stage1(t):
                if not (isinstance(t, int) and t == T_P):
                    sp.wait_ge(s_xTp, 2 * t + 2)
                    settle(sp)
                    sp.wait_ge(s_sq, t + 1)
                    sp.dma_start(x_t[:], rows(x_rows, t + 1)).then_inc(s_x, 16)
                if isinstance(t, int) and t == T_P - 1:
                    sp.wait_ge(s_kr, t + 1)
                    sp.dma_start(k_prompt, k_ro[:]).then_inc(s_kvout, 16)
                    sp.wait_ge(s_v, t + 1)
                    sp.dma_start(v_prompt, v_new[:]).then_inc(s_kvout, 16)
                if not (isinstance(t, int) and t == 0):
                    sp.wait_ge(s_att, 2 * t)
                    sp.wait_ge(s_gmo, t)
                    sp.dma_start(rows(mix_d, t - 1), mix_t[:]).then_inc(s_mix, 16)

            stage1(0)
            stage1(1)
            sp.wait_ge(s_whi, N_WI)
            sp.wait_ge(s_wlo, N_WI)
            sp.dma_start(vc_t[:], cache_v.rearrange("b s n -> s b n")).then_inc(s_vc, 16)
            with sp.Fori(2, T_P - 1) as t:
                stage1(t)
            stage1(T_P - 1)
            sp.dma_start(w_stage[2][:].rearrange("p (c n) -> p c n", c=2), wo_r[:, 0:2, :]).then_inc(s_wraw[2], 16)
            stage1(T_P)
            sp.wait_ge(s_kr, T)
            sp.dma_start(k_sample, k_ro[0:N_SAMPLE, :]).then_inc(s_kvout, 16)
            sp.wait_ge(s_v, T)
            sp.dma_start(v_sample, v_new[0:N_SAMPLE, :]).then_inc(s_kvout, 16)
            sp.wait_ge(s_vn, T)
            sp.dma_start(g_sample, vn_t[0:N_SAMPLE, :]).then_inc(s_kvout, 16)
            sp.dma_start(w_stage[1][:].rearrange("p (c n) -> p c n", c=2), wo_r[:, 2:4, :]).then_inc(s_wraw[1], 16)
            sp.wait_ge(s_sv, 10)
            sp.dma_start(rows(mix_d, T_P), mix_t[:]).then_inc(s_mix, 16)
            for n in range(2, N_WO):
                k = WO_SLOT[n]
                if n == 3:
                    sp.wait_ge(s_whi, N_WI + 1)
                    sp.wait_ge(s_wlo, N_WI + 1)
                sp.dma_start(w_stage[k][:].rearrange("p (c n) -> p c n", c=2),
                             wo_r[:, 2 * n:2 * n + 2, :]).then_inc(s_wraw[k], 16)
            sp.wait_ge(s_kvout, 5 * 16)
            sp.wait_ge(s_mix, T * 16)
            sp.dma_start(m_t[0][:], rows(mix_d, 0)).then_inc(s_ml[0], 16)
            sp.dma_start(ffg[:], ffn_g.to_broadcast([P, D])).then_inc(s_p2, 16)
            sp.dma_start(w_r[:, :, 0:NGRP], w_rg.rearrange("(p c) n -> p c n", c=DC)).then_inc(s_p2, 16)
            sp.dma_start(w_r[:, :, NGRP:], w_re.rearrange("(p c) n -> p c n", c=DC)).then_inc(s_p2, 16)
            sp.dma_start(b_rt[:], b_r.to_broadcast([P, NGRP + NE])).then_inc(s_p2, 16)
            sp.wait_ge(s_whi, N_WI + N_WO)
            sp.wait_ge(s_wlo, N_WI + N_WO)
            sp.dma_start(x1(0), rows(x_rows, 0)).then_inc(s_xr[0], 16)

            def load_expert(e, k, s, weights):
                for j, w in enumerate((w_gate, w_up)):
                    src = w[e] if isinstance(e, int) else w[bass.ds(e, 1)].squeeze(0)
                    weights.dma_start(wg[k][:, j], src.rearrange("(p c) f -> p c f", c=DC)).then_inc(s, 16)
                src = w_down[e] if isinstance(e, int) else w_down[bass.ds(e, 1)].squeeze(0)
                weights.dma_start(wd[k][:], src.rearrange("(p c) n -> p c n", c=2)).then_inc(s, 16)

            def stage2(t, b):
                if not (isinstance(t, int) and t == T_P):
                    if not (isinstance(t, int) and t == 0):
                        sp.wait_ge(s_mTp, 2 * t)
                    sp.dma_start(m_t[1 - b][:], rows(mix_d, t + 1)).then_inc(s_ml[1 - b], 16)
                    sp.dma_start(x1(t + 1), rows(x_rows, t + 1)).then_inc(s_xr[1 - b], 16)
                if not (isinstance(t, int) and t == 0):
                    store_h(t - 1)

            def store_h(t):
                sp.wait_ge(s_h, t + 1)
                sp.dma_start(rows(h_d, t), h_t[:]).then_inc(s_hst, 16)

            sp.wait_ge(s_z, 4 * T)
            load_expert(0, 0, s_w[0], sp)
            load_expert(1, 1, s_w[1], sp)
            stage2(0, 0)
            with sp.Fori(1, T_P - 2, 2) as t:
                stage2(t, 1)
                stage2(t + 1, 0)
            stage2(T_P - 1, 1)
            stage2(T_P, 0)
            sp.wait_ge(s_op, 2 * T)
            load_expert(2, 2, s_w[2], sp)
            store_h(T_P)
            load_expert(3, 3, s_w[3], sp)

            def stage4(e, k):
                sp.wait_ge(s_dn, e - 3)
                load_expert(e, k, s_w[k], sp)

            with sp.Fori(4, NE - 3, 4) as e:
                for k in range(4):
                    stage4(e + k, k)
            sp.wait_ge(s_dn, NE)

            sp.wait_ge(s_idx, 1)
            most = sp.value_load(cnt_i[0:1, 0:1], min_val=0, max_val=N_TOK)
            with sp.If(most > SLOTS):
                with sp.Fori(0, N_CHUNK - 1) as m:
                    with sp.Fori(0, NE) as e:
                        sp.wait_ge(o_ic, m * NE + e + 1)
                        load_expert(e, 0, o_w, sp)
            sp.wait_ge(o_done, 1)
            sp.dma_start(fing[:], fin_g.to_broadcast([P, D])).then_inc(s_fg, 16)

            def load_y(t, b, n=P):
                src = y_d.rearrange("(r k) n -> r (k n)", k=2)
                sp.dma_start(yy[b][0:n].rearrange("p k n -> p (k n)"), rows(src, t, n)).then_inc(s_yy[b], 16)

            def store_y(t, b, n=P):
                sp.wait_ge(s_fo, t + 1)
                sp.dma_start(rows(y_rows, t, n), out_t[b][0:n]).then_inc(s_out[b], 16)

            load_y(0, 0)
            load_y(1, 1)
            with sp.Fori(0, T_P - 3, 2) as t:
                for b in range(2):
                    sp.wait_ge(s_ysum, t + b + 1)
                    load_y(t + b + 2, b)
                    store_y(t + b, b)
            sp.wait_ge(s_ysum, T_P - 1)
            load_y(T_P, 0, N_SAMPLE)
            store_y(T_P - 2, 0)
            store_y(T_P - 1, 1)
            store_y(T_P, 0, N_SAMPLE)
            sp.wait_ge(s_out[0], 16 * (T_P // 2 + 1))
            sp.wait_ge(s_out[1], 16 * (T_P // 2))

        @block.tensor
        def _(pe):
            def transposes(src, n, bank_):
                for j in range(n):
                    last = nc.tensor.transpose(bank_[:, j * P:(j + 1) * P], src(j), ident)
                return last

            pe.wait_ge(s_cst, 16)
            pe.wait_ge(s_wmask, 1)
            for b in range(2):
                transposes(lambda j: ws_raw[:, 4 * b + j, :], 4, psT[b]).then_inc(s_tset, 1)
            pe.wait_ge(s_kc, 16)
            for b in range(2):
                pe.wait_ge(s_eset_a if b == 0 else s_eset_v, 1)
                transposes(lambda j: kc_t[:, 4 * b + j, :], 4, psT[b]).then_inc(s_tset, 1)

            def t_x(t):
                pe.wait_ge(s_x, 16 * (t + 1))
                for b in range(2):
                    if isinstance(t, int) and t == 0:
                        pe.wait_ge(s_eset_a if b == 0 else s_eset_v, 2)
                    else:
                        pe.wait_ge(s_qT if b == 0 else s_kT, t)
                    transposes(lambda j: x_t[:, (4 * b + j) * P:(4 * b + j + 1) * P], 4, psT[b]).then_inc(s_xTp, 1)

            def z_group(t, g):
                c0, n, splits = Z_GROUPS[g]
                if isinstance(t, int) and t == 0:
                    pe.wait_ge(s_whi, splits)
                    pe.wait_ge(s_wlo, splits)
                if g == 0:
                    pe.wait_ge(s_xh, 2 * t + 2)
                    pe.wait_ge(s_xl, 2 * t + 2)
                if g == 2:
                    pe.wait_ge(s_qr, t + 1)
                elif g == 3:
                    pe.wait_ge(s_kr, t + 1)
                    pe.wait_ge(s_v, t + 1)
                elif not (isinstance(t, int) and t == 0):
                    pe.wait_ge(s_u if g == 0 else s_vg, t)
                k = 0
                for c in range(DC):
                    for a, w in ((xT_hi, wi_hi), (xT_lo, wi_hi), (xT_hi, wi_lo)):
                        last = nc.tensor.matmul(psZ[g % 2][:, 0:n], a[:, c, :], w[:, c, c0:c0 + n],
                                                start=(k == 0), stop=(k == 3 * DC - 1))
                        k += 1
                last.then_inc(s_z, 1)

            def t_qk(t):
                pe.wait_ge(s_qr, t + 1)
                if not (isinstance(t, int) and t == 0):
                    pe.wait_ge(s_pTa, 2 * t)
                transposes(lambda j: q_ro[:, j * P:(j + 1) * P], 4, psT[0]).then_inc(s_qkTp, 1)
                pe.wait_ge(s_kr, t + 1)
                if not (isinstance(t, int) and t == 0):
                    pe.wait_ge(s_pTv, 2 * t)
                transposes(lambda j: k_ro[:], 1, psT[1]).then_inc(s_qkTp, 1)

            def scores(t, g):
                if g == 0:
                    pe.wait_ge(s_qT, t + 1)
                    pe.wait_ge(s_kT, t + 1)
                    if not (isinstance(t, int) and t == 0):
                        pe.wait_ge(s_sm, 2 * t)
                else:
                    pe.wait_ge(s_sm, 2 * t + 1)
                rows_ = slice(g * HD, (g + 1) * HD)
                for c in range(QPK):
                    last = nc.tensor.matmul(psS[:, c * 256:(c + 1) * 256], qT[rows_, c, :], kT[rows_, :],
                                            start=True, stop=True, skip_group_check=True)
                last.then_inc(s_sc, 1)

            def t_p(t, g):
                pe.wait_ge(s_p, 2 * t + g + 1)
                for b in range(2):
                    if g == 1:
                        pe.wait_ge(s_pTa if b == 0 else s_pTv, 2 * t + 1)
                    transposes(lambda j: s_t[g][:, 2 * b + j // 2, (j % 2) * P:(j % 2 + 1) * P], 4, psT[b])\
                        .then_inc(s_pTp, 1)

            def pv(t, g):
                pe.wait_ge(s_pTa, 2 * t + g + 1)
                pe.wait_ge(s_pTv, 2 * t + g + 1)
                if g == 0:
                    pe.wait_ge(s_vs, t + 1)
                    if not (isinstance(t, int) and t == 0):
                        pe.wait_ge(s_att, 2 * t)
                else:
                    pe.wait_ge(s_att, 2 * t + 1)
                for c in range(QPK):
                    for k in range(2):
                        last = nc.tensor.matmul(psO[:, (g * QPK + c) * HD:(g * QPK + c + 1) * HD],
                                                pT[:, 2 * c + k, :], v_t[:, k, g * HD:(g + 1) * HD],
                                                start=(k == 0), stop=(k == 1), skip_group_check=True)
                last.then_inc(s_pv, 1)

            def gm(t):
                pe.wait_ge(s_vn, t + 1)
                if not (isinstance(t, int) and t == 0):
                    pe.wait_ge(s_gmo, t)
                for g in range(NG):
                    last = nc.tensor.matmul(psG[:, g * HD:(g + 1) * HD], wsT[:, g, :], vn_t[:, g * HD:(g + 1) * HD],
                                            start=True, stop=True, skip_group_check=True)
                last.then_inc(s_gm, 1)

            def stage1(t):
                before = not (isinstance(t, int) and t == 0)
                sample = isinstance(t, int) and t == T_P
                z_group(t, 0)
                if before:
                    gm(t - 1)
                    t_p(t - 1, 0)
                    scores(t - 1, 1)
                    pv(t - 1, 0)
                z_group(t, 1)
                z_group(t, 2)
                if before:
                    t_p(t - 1, 1)
                    pv(t - 1, 1)
                z_group(t, 3)
                t_qk(t)
                if not sample:
                    t_x(t + 1)
                    scores(t, 0)

            t_x(0)
            stage1(0)
            stage1(1)
            with pe.Fori(2, T_P - 1) as t:
                stage1(t)
            stage1(T_P - 1)
            stage1(T_P)

            pe.wait_ge(s_qT, T)
            pe.wait_ge(s_kT, T)
            pe.wait_ge(s_sm, 2 * T_P)
            for g in range(NKV):
                r = slice(g * HD, (g + 1) * HD)
                for b in range(N_SAMPLE):
                    last = nc.tensor.matmul(psS[:, 512 * g + 4 * b:512 * g + 4 * b + 4], kcT[r, b, :], qT[r, :, b],
                                            start=True, stop=True, skip_group_check=True)
            last.then_inc(s_sp, 1)
            pe.wait_ge(s_sv, 1)
            nc.tensor.matmul(psG[0:64, 128:129], prod[:], small[:, 0:1], start=True, stop=True).then_inc(s_sp, 1)
            pe.wait_ge(s_sv, 2)
            nc.tensor.transpose(psO[0:64, 0:P], sT_s[:].rearrange("p g r -> p (g r)"), ident).then_inc(s_sp, 1)
            pe.wait_ge(s_sv, 6)
            nc.tensor.transpose(psT[0][:, 0:64], s_s[:, 0:P], ident[0:64, 0:64]).then_inc(s_sp, 1)
            nc.tensor.matmul(psG[0:N_SAMPLE, 0:64], selp[:], ident[0:64, 0:64], start=True, stop=True).then_inc(s_sp, 1)
            pe.wait_ge(s_sv, 8)
            pe.wait_ge(s_vc, 16)
            pe.wait_ge(s_v, T)
            nc.tensor.matmul(psO[:, 0:64], v_new[0:N_SAMPLE, :], d_s[:], start=True, stop=False, skip_group_check=True)
            for b in range(N_SAMPLE):
                o = psO[:, 0:64].rearrange("p (g r) -> p g r", g=NKV)[:, :, 4 * b:4 * b + 4]
                q = pT_s[:].rearrange("p (g r) -> p g r", g=NKV)[:, :, 4 * b:4 * b + 4]
                last = nc.tensor.matmul(o, vc_t[:, b, :], q, start=False, stop=(b == N_SAMPLE - 1), skip_group_check=True)
            last.then_inc(s_sp, 1)
            pe.wait_ge(s_sv, 9)
            for c in range(QPK):
                last = nc.tensor.transpose(psT[1][0:N_SAMPLE, c * P:(c + 1) * P], oT_s[:, :, c], ident)
            last.then_inc(s_sp, 1)

            def t_m(t, b):
                pe.wait_ge(s_ml[b], (t - b + 2) * 8)
                for k in range(2):
                    if isinstance(t, int) and t == 0:
                        pe.wait_ge(s_sv, 10)
                    else:
                        pe.wait_ge(s_mh, 2 * t - 1 + k)
                        pe.wait_ge(s_mlo, 2 * t - 1 + k)
                    transposes(lambda j: m_t[b][:, (4 * k + j) * P:(4 * k + j + 1) * P], 4, psT[k]).then_inc(s_mTp, 1)

            def out_half(t, b, h):
                if h == 0:
                    pe.wait_ge(s_mh, 2 * t + 2)
                    pe.wait_ge(s_mlo, 2 * t + 2)
                if isinstance(t, int) and t == 0:
                    pe.wait_ge(s_whi, N_WI + N_WO)
                    pe.wait_ge(s_wlo, N_WI + N_WO)
                else:
                    pe.wait_ge(s_x1, 2 * t - 1 + h)
                k = 0
                for c in range(DC):
                    for a, w in ((mT_hi, wo_hi), (mT_lo, wo_hi), (mT_hi, wo_lo)):
                        last = nc.tensor.matmul(psZ[h][:], a[b][:, c, :], w[:, c, h * 512:(h + 1) * 512],
                                                start=(k == 0), stop=(k == 3 * DC - 1))
                        k += 1
                last.then_inc(s_op, 1)

            def t_h(t):
                pe.wait_ge(s_h, t + 1)
                if not (isinstance(t, int) and t == 0):
                    pe.wait_ge(s_hTa, t)
                    pe.wait_ge(s_hTv, t)
                for j in range(DC):
                    last = nc.tensor.transpose(psS[:, j * P:(j + 1) * P], h_t[:, j * P:(j + 1) * P], ident)
                last.then_inc(s_hTp, 1)

            def route(t):
                pe.wait_ge(s_hTa, t + 1)
                pe.wait_ge(s_hTv, t + 1)
                if isinstance(t, int) and t == 0:
                    pe.wait_ge(s_p2, 64)
                else:
                    pe.wait_ge(s_lgo, t)
                for c in range(DC):
                    last = nc.tensor.matmul(psG[:, 0:NGRP + NE], hT[:, c, :], w_r[:, c, :],
                                            start=(c == 0), stop=(c == DC - 1))
                last.then_inc(s_lg, 1)

            def stage2(t, b):
                out_half(t, b, 0)
                if not (isinstance(t, int) and t == T_P):
                    t_m(t + 1, 1 - b)
                if not (isinstance(t, int) and t == 0):
                    t_h(t - 1)
                out_half(t, b, 1)
                if not (isinstance(t, int) and t == 0):
                    route(t - 1)

            t_m(0, 0)
            stage2(0, 0)
            with pe.Fori(1, T_P - 2, 2) as t:
                stage2(t, 1)
                stage2(t + 1, 0)
            stage2(T_P - 1, 1)
            stage2(T_P, 0)
            t_h(T_P)
            route(T_P)

            pe.wait_ge(s_rv, 1)
            mm = lambda out, a, b, **k: nc.tensor.matmul(out, a, b, skip_group_check=True, **k)
            mm(psZ[0][:, 0:T * NE], tr_bf[:], m_bf[:].rearrange("p t e -> p (t e)"), start=True, stop=False)
            for j in range(T - 1):
                last = mm(psZ[0][:, (j + 1) * NE:T * NE].rearrange("p (t e) -> p t e", e=NE), on_bf[:],
                          m_bf[:, j:j + 1, :].to_broadcast([P, T - 1 - j, NE]), start=False, stop=(j == T - 2))
            for j in range(T):
                last = mm(psZ[1][:, 0:NE], on_bf[:], m_bf[:, j, :], start=(j == 0), stop=(j == T - 1))
            last.then_inc(s_rp, 1)

            def table(done):
                for t in range(T):
                    for k in range(2):
                        last = mm(psG[:, 0:3 * NE], oh_r[:, k, t, :], rhs_t[:, k, t, :],
                                  start=(t == 0 and k == 0), stop=(t == T - 1 and k == 1))
                last.then_inc(done, 1)

            pe.wait_ge(s_rv, 2)
            table(s_rp)

            def t_g(slot, done):
                for k in range(2):
                    transposes(lambda j: xg[slot][:, (4 * k + j) * P:(4 * k + j + 1) * P], 4, psT[k]).then_inc(done, 1)

            def gate_up(z, w, done):
                for c in range(DC):
                    last = nc.tensor.matmul(psZ[z][:], xgT[:, c, :], w[:, :, c, :], start=(c == 0), stop=(c == DC - 1))
                last.then_inc(done, 1)

            def t_hid(done):
                transposes(lambda j: hid[:, j * P:(j + 1) * P], 2, psO).then_inc(done, 1)

            def down(w, done):
                for h in range(2):
                    for c in range(2):
                        last = nc.tensor.matmul(psS[:, h * 512:(h + 1) * 512], hidT[:, c, :],
                                                w[:, c, h * 512:(h + 1) * 512], start=(c == 0), stop=(c == 1))
                last.then_inc(done, 1)

            def first_g(e, k):
                pe.wait_ge(s_ga[k], (e - k + 4) * 4)
                if not (isinstance(e, int) and e == 0):
                    pe.wait_ge(s_gTa, e)
                    pe.wait_ge(s_gTv, e)
                t_g(k, s_gTp)

            def last_d(e, k):
                pe.wait_ge(s_dT, e + 1)
                if not (isinstance(e, int) and e == 0):
                    pe.wait_ge(s_ya, e)
                    pe.wait_ge(s_yv, e)
                down(wd[k], s_dn)

            def stage4(e, k):
                b = k % 2
                pe.wait_ge(s_gTa, e + 1)
                pe.wait_ge(s_gTv, e + 1)
                pe.wait_ge(s_w[k], (e - k + 4) * 12)
                if not (isinstance(e, int) and e < 2):
                    pe.wait_ge(s_hid, e - 1)
                gate_up(b, wg[k][:], s_gu)
                if not (isinstance(e, int) and e == NE - 1):
                    first_g(e + 1, (k + 1) % 4)
                if not (isinstance(e, int) and e == 0):
                    last_d(e - 1, (k + 3) % 4)
                pe.wait_ge(s_hid, e + 1)
                t_hid(s_dTp)

            first_g(0, 0)
            for k in range(4):
                stage4(k, k)
            with pe.Fori(4, NE - 7, 4) as e:
                for k in range(4):
                    stage4(e + k, k)
            for k in range(4):
                stage4(NE - 4 + k, k)
            last_d(NE - 1, 3)

            pe.wait_ge(s_idx, 1)
            most = pe.value_load(cnt_i[0:1, 0:1], min_val=0, max_val=N_TOK)
            with pe.If(most > SLOTS):
                with pe.Fori(0, N_CHUNK - 1) as m:
                    pe.wait_ge(o_oh, m + 1)
                    table(o_tab)
                    with pe.Fori(0, NE) as e:
                        n = m * NE + e
                        pe.wait_ge(o_ga, 16 * n + 16)
                        t_g(0, o_gTp)
                        pe.wait_ge(o_gTa, n + 1)
                        pe.wait_ge(o_gTv, n + 1)
                        pe.wait_ge(o_w, 48 * n + 48)
                        gate_up(0, wg[0][:], o_gu)
                        pe.wait_ge(o_hid, n + 1)
                        t_hid(o_dTp)
                        pe.wait_ge(o_dT, n + 1)
                        down(wd[0], o_dn)

        @block.scalar
        def _(act):
            act.wait_ge(s_gmix, 16)

            def split(n):
                act.wait_ge(s_wraw[n % 3], 16 * (n // 3 + 1))
                for c in range(DC):
                    last = nc.scalar.activation(wi_hi[:, c, n * KC:(n + 1) * KC], w_stage[n % 3][:, c * KC:(c + 1) * KC],
                                                ACT.Copy, scale=gmix[:, c:c + 1])
                last.then_inc(s_whi, 1)

            def copy(out, in_):
                return nc.scalar.activation(out, in_, ACT.Copy)

            split(0)
            act.wait_ge(s_tset, 1)
            copy(wsT[:, 0:4, :].rearrange("p g t -> p (g t)"), psT[0][:]).then_inc(s_eset_a, 1)
            act.wait_ge(s_tset, 3)
            copy(kcT[:, 0:4, :].rearrange("p g t -> p (g t)"), psT[0][:]).then_inc(s_eset_a, 1)

            def square(t):
                act.wait_ge(s_x, 16 * (t + 1))
                if not (isinstance(t, int) and t == 0):
                    act.wait_ge(s_rstd, t)
                    act.wait_ge(s_sq, t)
                nc.scalar.activation(junk[:], x_t[:], ACT.Square, accum_out=st[:, 0:1]).then_inc(s_sq, 1)

            def x_hi(t):
                for b in range(2):
                    act.wait_ge(s_xTp, 2 * t + b + 1)
                    if not (isinstance(t, int) and t == 0):
                        act.wait_ge(s_z, 4 * t)
                    copy(xT_hi[:, 4 * b:4 * b + 4, :].rearrange("p c t -> p (c t)"), psT[b][:]).then_inc(s_xh, 1)

            def exps(t, g):
                act.wait_ge(s_nb, 2 * t + g + 1)
                for c in range(QPK):
                    h = g * QPK + c
                    nc.scalar.activation(s_t[g][:, c, :], s_t[g][:, c, :], ACT.Exp, bias=st[:, 8 + h:9 + h],
                                         accum_out=st[:, 16 + h:17 + h])
                nc.scalar.activation(st[:, 32 + 4 * g:36 + 4 * g], st[:, 24 + 4 * g:28 + 4 * g], ACT.Exp).then_inc(s_p, 1)

            def p_out(t, g):
                act.wait_ge(s_pTp, 4 * t + 2 * g + 1)
                if g == 1:
                    act.wait_ge(s_pv, 2 * t + 1)
                elif not (isinstance(t, int) and t == 0):
                    act.wait_ge(s_pv, 2 * t)
                copy(pT[:, 0:4, :].rearrange("p j t -> p (j t)"), psT[0][:]).then_inc(s_pTa, 1)

            def values(t):
                act.wait_ge(s_rstd, t + 1)
                act.wait_ge(s_kr, t + 1)
                if isinstance(t, int) and t == T_P:
                    act.wait_ge(s_kvout, 32)
                if not (isinstance(t, int) and t == 0):
                    act.wait_ge(s_vs, t)
                nc.scalar.activation(v_new[:], psZ[1][:, P:2 * P], ACT.Copy, scale=st[:, 2:3]).then_inc(s_v, 1)

            def shift(t):
                if isinstance(t, int) and t == 0:
                    act.wait_ge(s_zero, 1)
                else:
                    act.wait_ge(s_pv, 2 * t)
                    copy(v_t[:, 0, :], v_t[:, 1, :]).then_inc(act_step, 1)
                    act.wait_ge(act_step, t)
                act.wait_ge(s_v, t + 1)
                copy(v_t[:, 1, :], v_new[:]).then_inc(s_vs, 1)

            def gelu_u(t):
                act.wait_ge(s_z, 4 * t + 3)
                if not (isinstance(t, int) and t == 0):
                    act.wait_ge(s_gmo, t)
                nc.scalar.activation(u_t[:], psZ[0][:], ACT.Gelu, scale=st[:, 2:3]).then_inc(s_u, 1)

            def gelu_v(t):
                act.wait_ge(s_z, 4 * t + 4)
                if not (isinstance(t, int) and t == 0):
                    act.wait_ge(s_vn, t)
                nc.scalar.activation(vg_t[:], psZ[1][:], ACT.Gelu, scale=st[:, 2:3]).then_inc(s_vg, 1)

            def q_out(t):
                act.wait_ge(s_qkTp, 2 * t + 1)
                if not (isinstance(t, int) and t == 0):
                    act.wait_ge(s_sc, 2 * t)
                copy(qT[:].rearrange("p c t -> p (c t)"), psT[0][:]).then_inc(s_qT, 1)

            def stage1(t):
                before = not (isinstance(t, int) and t == 0)
                sample = isinstance(t, int) and t == T_P
                if before:
                    exps(t - 1, 0)
                    p_out(t - 1, 0)
                else:
                    for n in range(2, N_WI):
                        split(n)
                values(t)
                if before:
                    exps(t - 1, 1)
                    p_out(t - 1, 1)
                if not sample:
                    shift(t)
                gelu_u(t)
                q_out(t)
                gelu_v(t)
                if not sample:
                    square(t + 1)
                    x_hi(t + 1)

            square(0)
            x_hi(0)
            split(1)
            stage1(0)
            stage1(1)
            with act.Fori(2, T_P - 1) as t:
                stage1(t)
            stage1(T_P - 1)
            stage1(T_P)

            act.wait_ge(s_sv, 4)
            nc.scalar.activation(s_s[:, 0:129], s_s[:, 0:129], ACT.Exp, bias=st[0:64, 40:41], scale=SCALE,
                                 accum_out=st[0:64, 42:43])
            nc.scalar.activation(st[0:64, 43:44], st[0:64, 41:42], ACT.Exp).then_inc(s_sa, 1)

            def split_out(n):
                k = WO_SLOT[n]
                act.wait_ge(s_z, 4 * T)
                act.wait_ge(s_wraw[k], 16 * WO_TURN[n])
                copy(wo_hi[:, 2 * n:2 * n + 2, :].rearrange("p c n -> p (c n)"), w_stage[k][:]).then_inc(s_whi, 1)

            for n in range(N_WO):
                split_out(n)

            def m_hi(t, b):
                for k in range(2):
                    act.wait_ge(s_mTp, 2 * t + k + 1)
                    if not (isinstance(t, int) and t < 2):
                        act.wait_ge(s_op, 2 * t - 2)
                    copy(mT_hi[b][:, 4 * k:4 * k + 4, :].rearrange("p c t -> p (c t)"), psT[k][:]).then_inc(s_mh, 1)

            def square2(t):
                act.wait_ge(s_x1, 2 * t + 2)
                if not (isinstance(t, int) and t == 0):
                    act.wait_ge(s_r2, t)
                    act.wait_ge(s_sq2, t)
                nc.scalar.activation(junk2[:], x1(t), ACT.Square, accum_out=small[:, 8:9]).then_inc(s_sq2, 1)

            def h_out(t):
                act.wait_ge(s_hTp, t + 1)
                if not (isinstance(t, int) and t == 0):
                    act.wait_ge(s_lg, t)
                copy(hT[:, 0:4, :].rearrange("p c t -> p (c t)"), psS[:, 0:512]).then_inc(s_hTa, 1)

            def stage2(t, b):
                if not (isinstance(t, int) and t == T_P):
                    m_hi(t + 1, 1 - b)
                if not (isinstance(t, int) and t == 0):
                    h_out(t - 1)
                square2(t)

            m_hi(0, 0)
            stage2(0, 0)
            with act.Fori(1, T_P - 2, 2) as t:
                stage2(t, 1)
                stage2(t + 1, 0)
            stage2(T_P - 1, 1)
            stage2(T_P, 0)
            h_out(T_P)

            act.wait_ge(s_ra, 1)
            nc.scalar.activation(g8[0][:, :, 0:4], g8[0][:, :, 0:4], ACT.Exp).then_inc(s_sa, 1)
            act.wait_ge(s_ra, 2)
            nc.scalar.activation(c9[6][:], c9[6][:], ACT.Exp).then_inc(s_sa, 1)

            def g_out(e):
                act.wait_ge(s_gTp, 2 * e + 1)
                if not (isinstance(e, int) and e == 0):
                    act.wait_ge(s_gu, e)
                copy(xgT[:, 0:4, :].rearrange("p c t -> p (c t)"), psT[0][:]).then_inc(s_gTa, 1)

            def silu(e, b):
                act.wait_ge(s_gu, e + 1)
                if not (isinstance(e, int) and e == 0):
                    act.wait_ge(s_hid, e)
                nc.scalar.activation(sg[:], psZ[b][:, 0:FE], ACT.Silu).then_inc(s_sg, 1)

            def hid_out(e):
                act.wait_ge(s_dTp, e + 1)
                if not (isinstance(e, int) and e == 0):
                    act.wait_ge(s_dn, e)
                copy(hidT[:].rearrange("p c t -> p (c t)"), psO[:, 0:256]).then_inc(s_dT, 1)

            def y_out(e, b):
                act.wait_ge(s_dn, e + 1)
                if not (isinstance(e, int) and e < 2):
                    act.wait_ge(s_sc4[b], (e - b) * 8)
                copy(y_t[b][:, 0:512], psS[:, 0:512]).then_inc(s_ya, 1)

            def stage4(e, k):
                b = k % 2
                silu(e, b)
                if not (isinstance(e, int) and e == NE - 1):
                    g_out(e + 1)
                if not (isinstance(e, int) and e == 0):
                    y_out(e - 1, 1 - b)
                hid_out(e)

            g_out(0)
            for k in range(4):
                stage4(k, k)
            with act.Fori(4, NE - 7, 4) as e:
                for k in range(4):
                    stage4(e + k, k)
            for k in range(4):
                stage4(NE - 4 + k, k)
            y_out(NE - 1, 1)

            act.wait_ge(s_idx, 1)
            most = act.value_load(cnt_i[0:1, 0:1], min_val=0, max_val=N_TOK)
            with act.If(most > SLOTS):
                with act.Fori(0, (N_CHUNK - 1) * NE) as n:
                    act.wait_ge(o_gTp, 2 * n + 1)
                    copy(xgT[:, 0:4, :].rearrange("p c t -> p (c t)"), psT[0][:]).then_inc(o_gTa, 1)
                    act.wait_ge(o_gu, n + 1)
                    nc.scalar.activation(sg[:], psZ[0][:, 0:FE], ACT.Silu).then_inc(o_sg, 1)
                    act.wait_ge(o_dTp, n + 1)
                    copy(hidT[:].rearrange("p c t -> p (c t)"), psO[:, 0:256]).then_inc(o_dT, 1)
                    act.wait_ge(o_dn, n + 1)
                    copy(y_t[0][:, 0:512], psS[:, 0:512]).then_inc(o_ya, 1)
            act.wait_ge(o_done, 1)

            def sq_final(t, b, n=P):
                act.wait_ge(s_ysum, t + 1)
                if not (isinstance(t, int) and t == 0):
                    act.wait_ge(s_fsq, t)
                if not (isinstance(t, int) and t < 2):
                    act.wait_ge(s_fr, t - 1)
                nc.scalar.activation(junk3[0:n], out_t[b][0:n], ACT.Square, accum_out=fst[0:n, b, 0:1]).then_inc(s_fsq, 1)

            sq_final(0, 0)
            with act.Fori(1, T_P - 2, 2) as t:
                sq_final(t, 1)
                sq_final(t + 1, 0)
            sq_final(T_P - 1, 1)
            sq_final(T_P, 0, N_SAMPLE)

        @block.vector
        def _(dve):
            step = Chain(dve, dve_step)
            tt = nc.vector.tensor_tensor
            ts = nc.vector.tensor_scalar
            stt = nc.vector.scalar_tensor_tensor
            cp = nc.vector.tensor_copy
            nc.vector.memset(kT[:], 0.0)
            nc.vector.memset(v_t[:], 0.0)
            nc.vector.memset(small[:, 0:1], 1.0).then_inc(s_zero, 1)
            dve.wait_ge(s_zero, 1)
            dve.wait_ge(s_cst, 16)
            dve.wait_ge(s_gmix, 16)

            def split(n):
                dve.wait_ge(s_wraw[n % 3], 16 * (n // 3 + 1))
                dve.wait_ge(s_whi, n + 1)
                for c in range(DC):
                    last = stt(out=wi_lo[:, c, n * KC:(n + 1) * KC], in0=w_stage[n % 3][:, c * KC:(c + 1) * KC],
                               scalar=gmix[:, c:c + 1], in1=wi_hi[:, c, n * KC:(n + 1) * KC].bitcast(F32),
                               op0=ALU.mult, op1=ALU.subtract)
                last.then_inc(s_wlo, 1)

            def x_lo(t):
                for b in range(2):
                    dve.wait_ge(s_xh, 2 * t + b + 1)
                    dst = slice(4 * b, 4 * b + 4)
                    tt(xT_lo[:, dst, :].rearrange("p c t -> p (c t)"), psT[b][:],
                       xT_hi[:, dst, :].rearrange("p c t -> p (c t)").bitcast(F32), ALU.subtract).then_inc(s_xl, 1)

            dve.wait_ge(s_tset, 2)
            cp(wsT[:, 4:8, :].rearrange("p g t -> p (g t)"), psT[1][:]).then_inc(s_eset_v, 1)
            dve.wait_ge(s_tset, 4)
            cp(kcT[:, 4:8, :].rearrange("p g t -> p (g t)"), psT[1][:]).then_inc(s_eset_v, 1)

            def rope(src, n, dst):
                cos = csr[:, 0:32].unsqueeze(1).unsqueeze(1).to_broadcast([P, n, 2, 32])
                sin = csr[:, 32:64].unsqueeze(1).unsqueeze(1).to_broadcast([P, n, 2, 32])
                a = rope_a[:, 0:n * HD].rearrange("p (h two d) -> p h two d", two=2, d=32)
                b = rope_b[:, 0:n * HD].rearrange("p (h two d) -> p h two d", two=2, d=32)
                src4 = src.rearrange("p (h two d) -> p h two d", two=2, d=32)
                tt(a, src4, cos, ALU.mult)
                step(tt(b, src4, sin, ALU.mult))
                tt(dst[0], a[:, :, 0, :], b[:, :, 1, :], ALU.subtract)
                return tt(dst[1], a[:, :, 1, :], b[:, :, 0, :], ALU.add)

            def rope_q(t):
                dve.wait_ge(s_rstd, t + 1)
                cs = cst[:, C_CS + t * HD:C_CS + t * HD + HD] if isinstance(t, int) else cst[:, bass.ds(t * HD + C_CS, HD)]
                step(ts(csr[:], cs, st[:, 2:3], None, ALU.mult))
                dve.wait_ge(s_z, 4 * t + 1)
                if not (isinstance(t, int) and t == 0):
                    dve.wait_ge(s_qkTp, 2 * t)
                q = q_ro[:].rearrange("p (c k two d) -> p k c two d", k=2, two=2, d=32)
                for k in range(2):
                    last = rope(psZ[0][:, k * 256:(k + 1) * 256], QPK, (q[:, k, :, 0, :], q[:, k, :, 1, :]))
                    if k == 0:
                        step(last)
                last.then_inc(s_qr, 1)

            def rope_k(t):
                dve.wait_ge(s_z, 4 * t + 2)
                dve.wait_ge(s_qr, t + 1)
                if isinstance(t, int) and t == T_P:
                    dve.wait_ge(s_kvout, 32)
                k = k_ro[:].rearrange("p (k two d) -> p k two d", two=2, d=32)
                rope(psZ[1][:, 0:P], NKV, (k[:, :, 0, :], k[:, :, 1, :])).then_inc(s_kr, 1)

            def softmax(t, g):
                dve.wait_ge(s_sc, 2 * t + g + 1)
                if not (isinstance(t, int) and t == 0):
                    dve.wait_ge(s_pTp, 4 * t - 2 + 2 * g)
                    dve.wait_ge(s_att, 2 * t - 1 + g)
                first = isinstance(t, int) and t == 0
                c = C_MF if first else C_MR
                mask = cst[:, c:c + 2 * P].unsqueeze(1).to_broadcast([P, QPK, 2 * P])
                stt(out=s_t[g][:], in0=psS[:].rearrange("p (c s) -> p c s", c=QPK), scalar=SCALE, in1=mask,
                    op0=ALU.mult, op1=ALU.add).then_inc(s_sm, 1)
                dve.wait_ge(s_sm, 2 * t + g + 1)
                mx = st[:, 44 + 4 * g:48 + 4 * g]
                sink = sink_t[:, 4 * g:4 * g + 4]
                step(nc.vector.tensor_reduce(mx, s_t[g][:], AX, ALU.max))
                step(tt(mx, mx, sink, ALU.max))
                ts(st[:, 8 + 4 * g:12 + 4 * g], mx, -1.0, None, ALU.mult)
                tt(st[:, 24 + 4 * g:28 + 4 * g], sink, mx, ALU.subtract).then_inc(s_nb, 1)

            def p_out(t, g):
                dve.wait_ge(s_pTp, 4 * t + 2 * g + 2)
                if g == 1:
                    dve.wait_ge(s_pv, 2 * t + 1)
                elif not (isinstance(t, int) and t == 0):
                    dve.wait_ge(s_pv, 2 * t)
                cp(pT[:, 4:8, :].rearrange("p j t -> p (j t)"), psT[1][:]).then_inc(s_pTv, 1)

            def att_out(t, g):
                dve.wait_ge(s_p, 2 * t + g + 1)
                r = st[:, 52 + 4 * g:56 + 4 * g]
                step(tt(r, st[:, 16 + 4 * g:20 + 4 * g], st[:, 32 + 4 * g:36 + 4 * g], ALU.add))
                step(nc.vector.reciprocal(r, r))
                dve.wait_ge(s_pv, 2 * t + g + 1)
                w = QPK * HD
                tt(mix_t[:, g * w:(g + 1) * w].rearrange("p (c d) -> p c d", c=QPK),
                   psO[:, g * w:(g + 1) * w].rearrange("p (c d) -> p c d", c=QPK),
                   r.unsqueeze(2).to_broadcast([P, QPK, HD]), ALU.mult).then_inc(s_att, 1)

            def gm_out(t):
                dve.wait_ge(s_gm, t + 1)
                dve.wait_ge(s_u, t + 1)
                if not (isinstance(t, int) and t == 0):
                    dve.wait_ge(s_mix, 16 * t)
                half = mix_t[:, ATT:D]
                step(tt(half.rearrange("p (g d) -> p g d", g=NG), psG[:].rearrange("p (g d) -> p g d", g=NG),
                        bsT[:].unsqueeze(2).to_broadcast([P, NG, HD]), ALU.add))
                tt(half, half, u_t[:], ALU.mult).then_inc(s_gmo, 1)

            def norm_v(t):
                dve.wait_ge(s_vg, t + 1)
                step(nc.vector.bn_stats(rope_a[:, 0:6], vg_t[:]))
                settle(dve)
                nc.vector.bn_aggr(st[:, 3:5], rope_a[:, 0:6]).then_inc(s_var, 1)
                dve.wait_ge(s_var, t + 1)
                if not (isinstance(t, int) and t == 0):
                    dve.wait_ge(s_gm, t)
                step(stt(out=vn_t[:], in0=vg_t[:], scalar=st[:, 3:4], in1=lng[:], op0=ALU.subtract, op1=ALU.mult))
                dve.wait_ge(s_lnr, t + 1)
                stt(out=vn_t[:], in0=vn_t[:], scalar=st[:, 6:7], in1=lnb[:], op0=ALU.mult, op1=ALU.add).then_inc(s_vn, 1)

            def k_out(t):
                dve.wait_ge(s_qkTp, 2 * t + 2)
                if not (isinstance(t, int) and t == 0):
                    dve.wait_ge(s_sc, 2 * t)
                    dve.wait_ge(s_kT, t)
                    step(cp(kT[:, 0:P], kT[:, P:2 * P]))
                cp(kT[:, P:2 * P], psT[1][:, 0:P]).then_inc(s_kT, 1)

            def stage1(t):
                before = not (isinstance(t, int) and t == 0)
                sample = isinstance(t, int) and t == T_P
                if before:
                    softmax(t - 1, 0)
                rope_q(t)
                if before:
                    gm_out(t - 1)
                    p_out(t - 1, 0)
                    softmax(t - 1, 1)
                    att_out(t - 1, 0)
                rope_k(t)
                if before:
                    p_out(t - 1, 1)
                    att_out(t - 1, 1)
                else:
                    for n in range(3, N_WI):
                        split(n)
                k_out(t)
                if not sample:
                    x_lo(t + 1)
                norm_v(t)

            split(0)
            x_lo(0)
            dve.wait_ge(s_small, 16 * 7)
            split(1)
            split(2)
            stage1(0)
            n1 = step.n
            stage1(1)
            per = step.n - n1
            n2 = step.n
            with dve.Fori(2, T_P - 1) as t:
                step.n = (t - 2) * per + n2
                stage1(t)
            step.n = n2 + (T_P - 3) * per
            stage1(T_P - 1)
            stage1(T_P)

            dve.wait_ge(s_qT, T)
            dve.wait_ge(s_kT, T)
            step(nc.vector.memset(prod[:], 0.0))
            for g in range(NKV):
                r = slice(g * HD, (g + 1) * HD)
                last = tt(prod[r, 32 * g:32 * g + 32].rearrange("p (b c) -> p b c", c=QPK),
                          qT[r, :, 0:N_SAMPLE].rearrange("p c b -> p b c"),
                          kT[r, P:P + N_SAMPLE].unsqueeze(2).to_broadcast([HD, N_SAMPLE, QPK]), ALU.mult)
            last.then_inc(s_sv, 1)
            dve.wait_ge(s_sp, 1)
            cp(sT_s[:], psS[:].rearrange("p (g r) -> p g r", g=NKV)[:, :, 0:32]).then_inc(s_sv, 1)
            dve.wait_ge(s_mix, 16 * T_P)
            step(nc.vector.memset(mix_t[:], 0.0))
            dve.wait_ge(s_vn, T)
            dve.wait_ge(s_u, T)
            v3 = vn_t[0:N_SAMPLE, :].rearrange("p (g d) -> p g d", g=NG)
            m3 = mix_t[0:N_SAMPLE, ATT:D].rearrange("p (g d) -> p g d", g=NG)
            step(tt(m3, v3, w00[0:N_SAMPLE, :].unsqueeze(2).to_broadcast([N_SAMPLE, NG, HD]), ALU.mult))
            step(tt(m3, m3, b00[0:N_SAMPLE, :].unsqueeze(2).to_broadcast([N_SAMPLE, NG, HD]), ALU.add))
            step(tt(mix_t[0:N_SAMPLE, ATT:D], mix_t[0:N_SAMPLE, ATT:D], u_t[0:N_SAMPLE, :], ALU.mult))
            dve.wait_ge(s_sp, 3)
            cp(s_s[:, 0:P], psO[0:64, 0:P])
            cp(s_s[:, P:P + 1], psG[0:64, 128:129]).then_inc(s_sv, 1)
            dve.wait_ge(s_sv, 3)
            step(nc.vector.tensor_reduce(st[0:64, 44:45], s_s[:, 0:P + 1], AX, ALU.max))
            step(ts(st[0:64, 44:45], st[0:64, 44:45], SCALE, sinkr[0:64, :], ALU.mult, ALU.max))
            ts(st[0:64, 40:41], st[0:64, 44:45], -1.0, None, ALU.mult)
            tt(st[0:64, 41:42], sinkr[0:64, :], st[0:64, 44:45], ALU.subtract).then_inc(s_sv, 1)
            dve.wait_ge(s_sa, 1)
            step(tt(st[0:64, 45:46], st[0:64, 42:43], st[0:64, 43:44], ALU.add))
            step(nc.vector.reciprocal(st[0:64, 45:46], st[0:64, 45:46]))
            ts(s_s[:, 0:P + 1], s_s[:, 0:P + 1], st[0:64, 45:46], None, ALU.mult).then_inc(s_sv, 1)
            dve.wait_ge(s_sv, 5)
            ts(selp[:], cst[0:64, C_SEL:C_SEL + N_SAMPLE], s_s[:, P:P + 1], None, ALU.mult).then_inc(s_sv, 1)
            dve.wait_ge(s_sp, 4)
            cp(pT_s[:], psT[0][:, 0:64]).then_inc(s_sv, 1)
            dve.wait_ge(s_sp, 5)
            cp(d_s[:], psG[0:N_SAMPLE, 0:64]).then_inc(s_sv, 1)
            dve.wait_ge(s_sp, 6)
            for g in range(NKV):
                r = slice(g * HD, (g + 1) * HD)
                last = cp(oT_s[r, :, :].rearrange("p b c -> p (b c)"), psO[r, 32 * g:32 * g + 32])
            last.then_inc(s_sv, 1)
            dve.wait_ge(s_sp, 7)
            cp(mix_t[0:N_SAMPLE, 0:ATT].rearrange("p (k c d) -> p c k d", k=NKV, c=QPK),
               psT[1][0:N_SAMPLE, :].rearrange("p (c k d) -> p c k d", k=NKV, c=QPK)).then_inc(s_sv, 1)

            for n in range(N_WO):
                k = WO_SLOT[n]
                dve.wait_ge(s_whi, N_WI + n + 1)
                dve.wait_ge(s_wraw[k], 16 * WO_TURN[n])
                tt(wo_lo[:, 2 * n:2 * n + 2, :].rearrange("p c n -> p (c n)"), w_stage[k][:],
                   wo_hi[:, 2 * n:2 * n + 2, :].rearrange("p c n -> p (c n)").bitcast(F32), ALU.subtract)\
                    .then_inc(s_wlo, 1)

            def m_lo(t, b):
                for k in range(2):
                    dve.wait_ge(s_mh, 2 * t + k + 1)
                    dst = slice(4 * k, 4 * k + 4)
                    tt(mT_lo[b][:, dst, :].rearrange("p c t -> p (c t)"), psT[k][:],
                       mT_hi[b][:, dst, :].rearrange("p c t -> p (c t)").bitcast(F32), ALU.subtract).then_inc(s_mlo, 1)

            def residual(t, b, h):
                if h == 0:
                    dve.wait_ge(s_xr[b], (t - b + 2) * 8)
                dve.wait_ge(s_op, 2 * t + h + 1)
                part = x1(t)[:, h * 512:(h + 1) * 512]
                tt(part, part, psZ[h][:], ALU.add).then_inc(s_x1, 1)

            def h_rows(t):
                dve.wait_ge(s_r2, t + 1)
                dve.wait_ge(s_x1, 2 * t + 2)
                if not (isinstance(t, int) and t == 0):
                    dve.wait_ge(s_hst, 16 * t)
                    dve.wait_ge(s_hTp, t)
                stt(out=h_t[:].rearrange("p (c q) -> p q c", c=DC), in0=x1(t).rearrange("p (q c) -> p q c", c=DC),
                    scalar=small[:, 10:11], in1=ffg[:].rearrange("p (q c) -> p q c", c=DC), op0=ALU.mult, op1=ALU.mult)\
                    .then_inc(s_h, 1)

            def h_out(t):
                dve.wait_ge(s_hTp, t + 1)
                if not (isinstance(t, int) and t == 0):
                    dve.wait_ge(s_lg, t)
                cp(hT[:, 4:8, :].rearrange("p c t -> p (c t)"), psS[:, 512:1024]).then_inc(s_hTv, 1)

            def logits_out(t):
                dve.wait_ge(s_lg, t + 1)
                dst = logits[:, t, :] if isinstance(t, int) else logits[:, bass.ds(t, 1), :].squeeze(1)
                tt(dst, psG[:, 0:NGRP + NE], b_rt[:], ALU.add).then_inc(s_lgo, 1)

            def stage2(t, b):
                if not (isinstance(t, int) and t == T_P):
                    m_lo(t + 1, 1 - b)
                if not (isinstance(t, int) and t == 0):
                    h_out(t - 1)
                residual(t, b, 0)
                residual(t, b, 1)
                if not (isinstance(t, int) and t == 0):
                    logits_out(t - 1)
                h_rows(t)

            m_lo(0, 0)
            dve.wait_ge(s_p2, 64)
            stage2(0, 0)
            with dve.Fori(1, T_P - 2, 2) as t:
                stage2(t, 1)
                stage2(t + 1, 0)
            stage2(T_P - 1, 1)
            stage2(T_P, 0)
            h_out(T_P)
            logits_out(T_P)

            dve.wait_ge(s_lgo, T)
            dve.wait_ge(s_op, 2 * T)
            red = nc.vector.tensor_reduce
            lg = logits[:, :, 0:NGRP]
            gmax, gsum, gidx = c9[0], c9[1], c9[2]
            b9 = lambda a, n: a[:].unsqueeze(2).to_broadcast([P, T, n])
            io = lambda n: cst[:, C_IO:C_IO + n].unsqueeze(1).to_broadcast([P, T, n])
            step(red(gmax[:], lg, AX, ALU.max))
            tt(g8[0][:, :, 0:4], lg, b9(gmax, 4), ALU.subtract).then_inc(s_ra, 1)
            step(tt(g8[1][:, :, 0:4], lg, b9(gmax, 4), ALU.is_equal))

            def first_of(eq, n, tmp, idx, onehot):
                step(stt(out=tmp, in0=eq, scalar=-64.0, in1=io(n), op0=ALU.mult, op1=ALU.add))
                step(red(idx[:], tmp, AX, ALU.min))
                step(ts(idx[:], idx[:], 64.0, None, ALU.add))
                step(tt(onehot, io(n), b9(idx, n), ALU.is_equal))

            first_of(g8[1][:, :, 0:4], 4, g8[1][:, :, 0:4], gidx, g8[1][:, :, 0:4])
            le = logits[:, :, NGRP:].rearrange("p t (g e) -> p t g e", g=NGRP)
            for g in range(NGRP):
                o = g8[1][:, :, g:g + 1].to_broadcast([P, T, EPG])
                dst = tmp_e[:, :, g * EPG:(g + 1) * EPG]
                last = tt(dst, le[:, :, g, :], o, ALU.mult)
            step(last)
            esel, e2 = g8[2], g8[3]
            step(red(esel[:], tmp_e[:].rearrange("p t (g e) -> p t e g", g=NGRP), AX, ALU.add))
            m1, m2, i1, i2 = c9[3], c9[4], c9[5], c9[7]
            step(red(m1[:], esel[:], AX, ALU.max))
            step(tt(g8[4][:], esel[:], b9(m1, 8), ALU.is_equal))
            first_of(g8[4][:], 8, g8[4][:], i1, g8[5][:])
            step(stt(out=e2[:], in0=g8[5][:], scalar=NEG, in1=esel[:], op0=ALU.mult, op1=ALU.add))
            step(red(m2[:], e2[:], AX, ALU.max))
            step(tt(g8[4][:], e2[:], b9(m2, 8), ALU.is_equal))
            first_of(g8[4][:], 8, g8[4][:], i2, g8[5][:])
            tt(c9[6][:], m2[:], m1[:], ALU.subtract).then_inc(s_ra, 1)
            step(stt(out=gidx[:], in0=gidx[:], scalar=float(EPG), in1=cst[:, C_INV:C_INV + T], op0=ALU.mult, op1=ALU.add))
            tt(i1[:], gidx[:], i1[:], ALU.add)
            step(tt(i2[:], gidx[:], i2[:], ALU.add))
            tt(one_e[:, 0], io(NE), b9(i1, NE), ALU.is_equal)
            step(tt(one_e[:, 1], io(NE), b9(i2, NE), ALU.is_equal))
            cp(tr_bf[:], cst[:, C_TR:C_TR + P])
            nc.vector.memset(on_bf[:], 1.0)
            tt(m_bf[:], one_e[:, 0], one_e[:, 1], ALU.add).then_inc(s_rv, 1)
            for k in range(2):
                ts(rhs_t[:, k, :, 0:NE], one_e[:, k], cst[:, C_PR:C_PR + 1], None, ALU.mult)
                tt(rhs_t[:, k, :, NE:2 * NE], one_e[:, k],
                   cst[:, C_TILE:C_TILE + T].unsqueeze(2).to_broadcast([P, T, NE]), ALU.mult)
                ts(rhs_t[:, k, :, 2 * NE:3 * NE], one_e[:, k], float(k + 1), None, ALU.mult)
            dve.wait_ge(s_sa, 2)
            step(red(gsum[:], g8[0][:, :, 0:4], AX, ALU.add))
            dve.wait_ge(s_sa, 3)
            step(ts(c9[8][:], c9[6][:], 1.0, None, ALU.add))
            step(tt(c9[8][:], c9[8][:], gsum[:], ALU.mult))
            step(nc.vector.reciprocal(w_of[:, 0, :], c9[8][:]))
            step(tt(w_of[:, 1, :], w_of[:, 0, :], c9[6][:], ALU.mult))
            dve.wait_ge(s_rp, 1)
            cp(rank_s[:].rearrange("p t e -> p (t e)"), psZ[0][:, 0:T * NE])
            step(red(c9[9][:, 0:1], psZ[1][:, 0:NE], AX, ALU.max))
            cp(cnt_i[:], c9[9][:, 0:1])
            for k in range(2):
                step(tt(tmp_e[:], one_e[:, k], rank_s[:], ALU.mult))
                step(red(rk[:, k, :], tmp_e[:], AX, ALU.add))

            def one_hots(done):
                for t in range(T):
                    for k in range(2):
                        last = ts(oh_r[:, k, t, :], cst[:, C_IO:C_IO + P], rk[:, k, t:t + 1], None, ALU.is_equal)
                last.then_inc(done, 1)

            def table_out(link, done):
                link(cp(tab[:], psG[:, 0:3 * NE]))
                a, b, c = tab[:, 0:NE], tab[:, NE:2 * NE], tab[:, 2 * NE:3 * NE]
                ts(tab2[:, 0, :], c, 0.0, OOB, ALU.is_equal, ALU.mult)
                link(stt(out=tab2[:, 1, :], in0=b, scalar=float(P), in1=a, op0=ALU.mult, op1=ALU.add))
                link(stt(out=tab2[:, 2, :], in0=tab2[:, 1, :], scalar=2.0, in1=c, op0=ALU.mult, op1=ALU.add))
                tt(idx_src[:], tab2[:, 1, :], tab2[:, 0, :], ALU.add)
                link(stt(out=tab2[:, 2, :], in0=tab2[:, 2, :], scalar=-1.0, in1=tab2[:, 0, :], op0=ALU.add, op1=ALU.add))
                cp(idx_dst[:], tab2[:, 2, :]).then_inc(done, 1)

            one_hots(s_rv)
            dve.wait_ge(s_rp, 2)
            table_out(step, s_idx)
            dve.wait_ge(s_idx, 1)

            for k in range(3):
                nc.vector.memset(xg[k][:], 0.0)
            nc.vector.memset(xg[3][:], 0.0).then_inc(s_zx, 1)

            def col(ap, e):
                return ap[:, e:e + 1] if isinstance(e, int) else ap[:, bass.ds(e, 1)]

            def src_rows(e, k):
                if not (isinstance(e, int) and e < 4):
                    dve.wait_ge(s_ga[k], (e - k) * 4)
                cp(ic_src[:, k:k + 1], col(idx_src, e)).then_inc(s_isrc, 1)

            def dst_rows(e, k):
                if not (isinstance(e, int) and e < 4):
                    dve.wait_ge(s_sc4[k % 2], (e - k % 2 - 2) * 8)
                cp(ic_dst[:, k:k + 1], col(idx_dst, e)).then_inc(s_idst, 1)

            def into_hid(u):
                halves = lambda a: a.rearrange("p (q c) -> p q c", c=2)
                return tt(hid[:].rearrange("p (c q) -> p q c", c=2), halves(sg[:]), halves(u), ALU.mult)

            def g_out(e):
                dve.wait_ge(s_gTp, 2 * e + 2)
                if not (isinstance(e, int) and e == 0):
                    dve.wait_ge(s_gu, e)
                cp(xgT[:, 4:8, :].rearrange("p c t -> p (c t)"), psT[1][:]).then_inc(s_gTv, 1)

            def y_out(e, b):
                dve.wait_ge(s_dn, e + 1)
                if not (isinstance(e, int) and e < 2):
                    dve.wait_ge(s_sc4[b], (e - b) * 8)
                cp(y_t[b][:, 512:D], psS[:, 512:D]).then_inc(s_yv, 1)

            def stage4(e, k):
                b = k % 2
                dve.wait_ge(s_sg, e + 1)
                if not (isinstance(e, int) and e == 0):
                    dve.wait_ge(s_dTp, e)
                into_hid(psZ[b][:, FE:2 * FE]).then_inc(s_hid, 1)
                if not (isinstance(e, int) and e == NE - 1):
                    g_out(e + 1)
                if not (isinstance(e, int) and e == 0):
                    y_out(e - 1, 1 - b)
                if not (isinstance(e, int) and e >= NE - 4):
                    src_rows(e + 4, k)
                if not (isinstance(e, int) and e == NE - 1):
                    dst_rows(e + 1, (k + 1) % 4)

            for k in range(4):
                src_rows(k, k)
            dst_rows(0, 0)
            g_out(0)
            for k in range(4):
                stage4(k, k)
            with dve.Fori(4, NE - 7, 4) as e:
                for k in range(4):
                    stage4(e + k, k)
            for k in range(4):
                stage4(NE - 4 + k, k)
            y_out(NE - 1, 1)

            most = dve.value_load(cnt_i[0:1, 0:1], min_val=0, max_val=N_TOK)
            with dve.If(most > SLOTS):
                link = Chain(dve, o_step)
                with dve.Fori(0, N_CHUNK - 1) as m:
                    link.n = m * OV_LINKS
                    flat = rk[:].rearrange("p k t -> p (k t)")
                    link(ts(flat, flat, -float(SLOTS), None, ALU.add))
                    one_hots(o_oh)
                    dve.wait_ge(o_tab, m + 1)
                    table_out(link, o_idx)
                    dve.wait_ge(o_idx, m + 1)
                    settle(dve)
                    with dve.Fori(0, NE) as e:
                        n = m * NE + e
                        dve.wait_ge(o_free, n + 1)
                        cp(ic_src[:, 0:1], idx_src[:, bass.ds(e, 1)])
                        cp(ic_dst[:, 0:1], idx_dst[:, bass.ds(e, 1)]).then_inc(o_ic, 1)
                        dve.wait_ge(o_gTp, 2 * n + 2)
                        cp(xgT[:, 4:8, :].rearrange("p c t -> p (c t)"), psT[1][:]).then_inc(o_gTv, 1)
                        dve.wait_ge(o_sg, n + 1)
                        into_hid(psZ[0][:, FE:2 * FE]).then_inc(o_hid, 1)
                        dve.wait_ge(o_dn, n + 1)
                        cp(y_t[0][:, 512:D], psS[:, 512:D]).then_inc(o_y, 1)
            dve.wait_ge(o_done, 1)

            dve.wait_ge(s_fg, 16)

            def sum_rows(t, b, n=P):
                dve.wait_ge(s_yy[b], (t - b + 2) * 8)
                if not (isinstance(t, int) and t < 2):
                    dve.wait_ge(s_out[b], (t - b) * 8)
                w = [w_of[0:n, k, t:t + 1] if isinstance(t, int) else w_of[0:n, k, bass.ds(t, 1)] for k in range(2)]
                step(stt(out=out_t[b][0:n], in0=yy[b][0:n, 0, :], scalar=w[0], in1=x1(t)[0:n], op0=ALU.mult, op1=ALU.add))
                stt(out=out_t[b][0:n], in0=yy[b][0:n, 1, :], scalar=w[1], in1=out_t[b][0:n], op0=ALU.mult, op1=ALU.add)\
                    .then_inc(s_ysum, 1)

            def scale_rows(t, b, n=P):
                dve.wait_ge(s_fr, t + 1)
                dve.wait_ge(s_ysum, t + 1)
                stt(out=out_t[b][0:n], in0=out_t[b][0:n], scalar=fst[0:n, b, 2:3], in1=fing[0:n], op0=ALU.mult,
                    op1=ALU.mult).then_inc(s_fo, 1)

            sum_rows(0, 0)
            n6 = step.n
            with dve.Fori(0, T_P - 3, 2) as t:
                step.n = t + n6
                sum_rows(t + 1, 1)
                scale_rows(t, 0)
                sum_rows(t + 2, 0)
                scale_rows(t + 1, 1)
            step.n = n6 + T_P - 2
            sum_rows(T_P - 1, 1)
            scale_rows(T_P - 2, 0)
            sum_rows(T_P, 0, N_SAMPLE)
            scale_rows(T_P - 1, 1)
            scale_rows(T_P, 0, N_SAMPLE)

        @block.gpsimd
        def _(pool):
            link = Chain(pool, pool_step)
            ptt = nc.gpsimd.tensor_tensor
            nc.gpsimd.memset(small[:, 1:2], -0.5)
            nc.gpsimd.memset(small[:, 2:3], 1.0 / D)
            link(nc.gpsimd.memset(small[:, 3:4], EPS))
            pool.wait_ge(s_ws, 16)
            nc.gpsimd.affine_select(out=ws_raw[:], in_=ws_raw[:], compare_op=ALU.is_ge, fill=0.0, base=0,
                                    pattern=[[0, NG], [-1, P]], channel_multiplier=1).then_inc(s_wmask, 1)

            def rsqrt(out, src, tmp, done, n=P, mean=True):
                if mean:
                    link(ptt(tmp, src, small[0:n, 2:3], ALU.mult))
                link(ptt(tmp, tmp if mean else src, small[0:n, 3:4], ALU.add))
                ptt(out, tmp, small[0:n, 1:2], ALU.pow).then_inc(done, 1)

            def row_scale(t):
                pool.wait_ge(s_sq, t + 1)
                rsqrt(st[:, 2:3], st[:, 0:1], st[:, 1:2], s_rstd)

            def ln_scale(t):
                pool.wait_ge(s_var, t + 1)
                rsqrt(st[:, 6:7], st[:, 4:5], st[:, 5:6], s_lnr, mean=False)

            row_scale(0)
            n1 = link.n
            with pool.Fori(0, T_P) as t:
                link.n = 3 * t + n1
                row_scale(t + 1)
                ln_scale(t)
            link.n = n1 + 3 * T_P
            ln_scale(T_P)

            def h_scale(t):
                pool.wait_ge(s_sq2, t + 1)
                if not (isinstance(t, int) and t == 0):
                    pool.wait_ge(s_h, t)
                rsqrt(small[:, 10:11], small[:, 8:9], small[:, 9:10], s_r2)

            h_scale(0)
            n2 = link.n
            with pool.Fori(1, T) as t:
                link.n = 2 * t - 2 + n2
                h_scale(t)
            link.n = n2 + 2 * T_P

            def gather(k, done):
                nc.gpsimd.indirect_dma_start(xg[k][:], None, h_d, bass.IndirectOffsetOnAxis(ic_src[:, k:k + 1].bitcast(U32), 0),
                                             bounds_check=T * P - 1, oob_is_err=False).then_inc(done, 16)

            def scatter(k, b, done):
                nc.gpsimd.indirect_dma_start(y_d, bass.IndirectOffsetOnAxis(ic_dst[:, k:k + 1].bitcast(U32), 0), y_t[b][:], None,
                                             bounds_check=2 * T * P - 1, oob_is_err=False).then_inc(done, 16)

            def gather4(e, k):
                pool.wait_ge(s_isrc, e + 1)
                if not (isinstance(e, int) and e < 4):
                    pool.wait_ge(s_gTp, 2 * e - 6)
                settle(pool)
                gather(k, s_ga[k])

            def stage4(e, k):
                if not (isinstance(e, int) and e >= NE - 4):
                    gather4(e + 4, k)
                pool.wait_ge(s_idst, e + 1)
                pool.wait_ge(s_ya, e + 1)
                pool.wait_ge(s_yv, e + 1)
                settle(pool)
                scatter(k, k % 2, s_sc4[k % 2])

            pool.wait_ge(s_hst, 16 * T)
            pool.wait_ge(s_zx, 1)
            for k in range(4):
                gather4(k, k)
            for k in range(4):
                stage4(k, k)
            with pool.Fori(4, NE - 7, 4) as e:
                for k in range(4):
                    stage4(e + k, k)
            for k in range(4):
                stage4(NE - 4 + k, k)
            for b in range(2):
                pool.wait_ge(s_sc4[b], NE // 2 * 16)

            most = pool.value_load(cnt_i[0:1, 0:1], min_val=0, max_val=N_TOK)
            with pool.If(most > SLOTS):
                with pool.Fori(0, (N_CHUNK - 1) * NE) as n:
                    pool.sem_inc(o_free, 1)
                    pool.wait_ge(o_ic, n + 1)
                    settle(pool)
                    gather(0, o_ga)
                    pool.wait_ge(o_ya, n + 1)
                    pool.wait_ge(o_y, n + 1)
                    settle(pool)
                    scatter(0, 0, o_sc)
                    pool.wait_ge(o_sc, 16 * n + 16)
            pool.sem_inc(o_done, 1)

            def final_scale(t, b, n=P):
                pool.wait_ge(s_fsq, t + 1)
                if not (isinstance(t, int) and t < 2):
                    pool.wait_ge(s_fo, t - 1)
                rsqrt(fst[0:n, b, 2:3], fst[0:n, b, 0:1], fst[0:n, b, 1:2], s_fr, n)

            final_scale(0, 0)
            final_scale(1, 1)
            n6 = link.n
            with pool.Fori(2, T_P - 1, 2) as t:
                link.n = 2 * t - 4 + n6
                final_scale(t, 0)
                final_scale(t + 1, 1)
            link.n = n6 + 2 * T_P - 4
            final_scale(T_P, 0, N_SAMPLE)


def shape_constants():
    import numpy as np
    c = np.zeros((P, C_END), np.float32)
    r = np.arange(P)
    c[:, C_ID:C_ID + P] = np.eye(P)
    causal = np.where(r[None, :] <= r[:, None], 0.0, NEG)
    c[:, C_MF:C_MF + P] = NEG
    c[:, C_MF + P:C_MF + 2 * P] = causal
    c[:, C_MR:C_MR + P] = np.where(r[None, :] >= r[:, None], 0.0, NEG)
    c[:, C_MR + P:C_MR + 2 * P] = causal
    c[:, C_IO:C_IO + P] = r[None, :]
    c[:, C_TR:C_TR + P] = r[:, None] < r[None, :]
    c[:, C_PR] = r
    q = np.arange(64)
    c[q, C_SEL + (q % 32) // QPK] = 1.0
    c[N_SAMPLE:, C_INV + T_P] = 1000.0
    c[:, C_TILE:C_TILE + T] = np.arange(T)[None, :]
    inv_freq = (10000.0 ** (-np.arange(HD // 2) * 2.0 / HD)).astype(np.float32)
    for t in range(T):
        pos = (t * P + r if t < T_P else np.full(P, PAST)).astype(np.float32)
        angle = (pos[:, None] * inv_freq[None, :]).astype(np.float64)
        c[:, C_CS + t * HD:C_CS + t * HD + 32] = np.cos(angle)
        c[:, C_CS + t * HD + 32:C_CS + (t + 1) * HD] = np.sin(angle)
    return c


def kernel(**inputs):
    import numpy as np
    import concourse.bacc as bacc
    from concourse.bass_utils import run_bass_kernel_spmd

    a = {k: np.asarray(v) for k, v in inputs.items()}
    x_rows = np.zeros((T * P, D), a["x_prompt"].dtype)
    x_rows[:N_PROMPT] = a["x_prompt"].reshape(N_PROMPT, D)
    x_rows[N_PROMPT:N_TOK] = a["x_sample"].reshape(N_SAMPLE, D)
    sinks = a["attn_sinks"].reshape(NKV, 1, QPK)
    arrays = dict(
        x_rows=x_rows,
        cache_k=a["cache_swa_k"].reshape(N_SAMPLE, WIN, P),
        cache_v=a["cache_swa_v"].reshape(N_SAMPLE, WIN, P),
        mix_g=np.ascontiguousarray(a["norm_mix_g"].reshape(DC, P).T),
        w_in=a["w_in"].reshape(D, Z_COLS),
        sinks_b=a["attn_sinks"].reshape(1, NQ),
        sink_rows=np.ascontiguousarray(np.broadcast_to(sinks, (NKV, N_SAMPLE, QPK)).reshape(64, 1)),
        ln_g=a["gmlp_ln_g"].reshape(1, GW),
        ln_b=a["gmlp_ln_b"].reshape(1, GW),
        w_s=a["gmlp_w_s"].reshape(NG, P, P),
        b_sT=np.ascontiguousarray(a["gmlp_b_s"].reshape(NG, P).T),
        b_s=a["gmlp_b_s"].reshape(NG, P),
        w_out=a["w_out"].reshape(D, D),
        ffn_g=a["norm_ffn_g"].reshape(1, D),
        w_rg=a["router_group_w"].reshape(D, NGRP),
        b_r=np.concatenate([a["router_group_b"].reshape(1, NGRP), a["router_expert_b"].reshape(1, NE)], axis=1),
        w_re=a["router_expert_w"].reshape(D, NE),
        w_gate=a["expert_w_gate"].reshape(NE, D, FE),
        w_up=a["expert_w_up"].reshape(NE, D, FE),
        w_down=a["expert_w_down"].reshape(NE, FE, D),
        fin_g=a["final_norm_g"].reshape(1, D),
        consts=shape_constants(),
    )
    outs = dict(y_rows=(N_TOK, D), k_prompt=(P, P), v_prompt=(P, P), k_sample=(N_SAMPLE, P), v_sample=(N_SAMPLE, P),
                g_sample=(N_SAMPLE, GW))
    nc = bacc.Bacc("TRN2", target_bir_lowering=False, num_devices=1)
    aps = {n: nc.dram_tensor(n, v.shape, mybir.dt.from_np(v.dtype), kind="ExternalInput").ap() for n, v in arrays.items()}
    aps |= {n: nc.dram_tensor(n, s, F32, kind="ExternalOutput").ap() for n, s in outs.items()}
    build(nc, **aps)
    r = run_bass_kernel_spmd(nc, [arrays], core_ids=[0]).results[0]
    y = r["y_rows"]
    return (y[:N_PROMPT].reshape(1, N_PROMPT, D), y[N_PROMPT:].reshape(N_SAMPLE, 1, D),
            r["k_prompt"].reshape(1, 1, WIN, NKV, HD), r["v_prompt"].reshape(1, 1, WIN, NKV, HD),
            r["k_sample"].reshape(1, N_SAMPLE, 1, NKV, HD), r["v_sample"].reshape(1, N_SAMPLE, 1, NKV, HD),
            r["g_sample"].reshape(1, N_SAMPLE, 1, GW))
```

```python
from contextlib import ExitStack

import concourse.bass as bass
from concourse import mybir

F32 = mybir.dt.float32
F32R = mybir.dt.float32r
BF16 = mybir.dt.bfloat16
I32 = mybir.dt.int32
U32 = mybir.dt.uint32
ALU = mybir.AluOpType
ACT = mybir.ActivationFunctionType
AX = mybir.AxisListType.X

P = 128
D = 1024
DC = D // P
N_PROMPT = 1024
N_SAMPLE = 8
N_TOK = N_PROMPT + N_SAMPLE
T_P = N_PROMPT // P
T = T_P + 1
HD = 64
NQ = 8
NKV = 2
QPK = NQ // NKV
ATT = NQ * HD
GW = 512
NG = 8
Z_COLS = 1792
WIN = 128
NGRP = 4
EPG = 8
NE = 32
FE = 256
EPS = 1e-6
SCALE = HD ** -0.5
NEG = -1e30
SLOTS = 128
PAST = 8192
OV_LINKS = 5
N_CHUNK = -(-N_TOK // SLOTS)
OOB = 100000.0
Z_GROUPS = [(0, 512), (512, 256), (768, 512), (1280, 512)]
WI_COLS = [(0, 768), (768, 1792)]
N_WI = 2 * DC // 2
N_WO = 4
WO_STAGED = 2

C_ID = 0
C_MF = C_ID + P
C_MR = C_MF + 2 * P
C_IO = C_MR + 2 * P
C_TR = C_IO + P
C_PR = C_TR + P
C_SEL = C_PR + 1
C_INV = C_SEL + N_SAMPLE
C_TILE = C_INV + T
C_CS = C_TILE + T
C_END = C_CS + T * HD


class Region:

    def __init__(self, nc, base, start, end):
        self.nc, self.base, self.at, self.end = nc, base, start, end

    def take(self, name, shape, dt):
        n = 1
        for s in shape[1:]:
            n *= s
        size = -(-n * (2 if dt == BF16 else 4) // 32) * 32
        got = self.nc.alloc_sbuf_tensor_at(name, shape, dt, offset=self.base + self.at)
        self.at += size
        assert self.at <= self.end, (name, self.at, self.end)
        return got


class Chain:

    def __init__(self, eng, sem):
        self.eng, self.sem, self.n = eng, sem, 0

    def __call__(self, ins):
        ins.then_inc(self.sem, 1)
        self.n = self.n + 1
        self.eng.wait_ge(self.sem, self.n)


def build(nc, x_rows, cache_k, cache_v, mix_g, w_in, sinks_b, sink_rows, ln_g, ln_b, w_s, b_sT, b_s, w_out, ffn_g,
          w_rg, b_r, w_re, w_gate, w_up, w_down, fin_g, consts,
          y_rows, k_prompt, v_prompt, k_sample, v_sample, g_sample):
    mix_d = nc.dram_tensor("mix_d", [T * P, D], F32).ap()
    h_d = nc.dram_tensor("h_d", [T * P, D], F32).ap()
    y_d = nc.dram_tensor("y_d", [2 * T * P, D], F32).ap()

    ctx = ExitStack()
    with ctx:
        def bank(name, n=1):
            return ctx.enter_context(nc.psum_tensor(name, [P, n * 512], F32))

        def sem(name):
            return ctx.enter_context(nc.semaphore(name))

        psT = [bank("psT0"), bank("psT1")]
        psZ = [bank("psZ0"), bank("psZ1")]
        psS = bank("psS", 2)
        psO = bank("psO")
        psG = bank("psG")

        base = 16512
        r1 = Region(nc, base, 0, 114688)
        r2 = Region(nc, base, 114688, 147456)
        r3 = Region(nc, base, 147456, 212800)
        cst = r3.take("cst", [P, C_END], F32)
        w_of = r3.take("w_of", [P, 2, T], F32)
        small = r3.take("small", [P, 64], F32)
        wi_hi = r1.take("wi_hi", [P, DC, Z_COLS], F32R)
        wi_lo = r1.take("wi_lo", [P, DC, Z_COLS], F32R)
        wi_raw = Region(nc, base, r1.at - 4 * DC * Z_COLS, r1.at).take("wi_raw", [P, DC, Z_COLS], F32)
        wo_stage = [r2.take(f"wo_stage{n}", [P, 2 * D], F32) for n in range(WO_STAGED)]
        x_t = r2.take("x_t", [P, D], F32)
        q_ro = r2.take("q_ro", [P, ATT], F32)
        qT = r2.take("qT", [P, QPK, P], F32)
        a1 = r3.at
        mix_t = r3.take("mix_t", [P, D], F32)
        xT_hi = r3.take("xT_hi", [P, DC, P], F32R)
        xT_lo = r3.take("xT_lo", [P, DC, P], F32R)
        k_ro = r3.take("k_ro", [P, P], F32)
        kT = r3.take("kT", [P, 2 * P], F32)
        v_t = r3.take("v_t", [P, 2, P], F32)
        v_new = r3.take("v_new", [P, P], F32)
        u_t = r3.take("u_t", [P, GW], F32)
        vg_t = r3.take("vg_t", [P, GW], F32)
        vn_t = r3.take("vn_t", [P, GW], F32)
        s_at = r3.at
        s_t = [r3.take(f"s_t{g}", [P, QPK, 2 * P], F32) for g in range(2)]
        s_end = r3.at
        r_tmp = Region(nc, base, s_at, s_end)
        ws_raw = r_tmp.take("ws_raw", [P, NG, P], F32)
        kc_t = r_tmp.take("kc_t", [P, N_SAMPLE, P], F32)
        pT = r3.take("pT", [P, 2 * QPK, P], F32)
        lng = r3.take("lng", [P, GW], F32)
        lnb = r3.take("lnb", [P, GW], F32)
        wsT = r3.take("wsT", [P, NG, P], F32)
        rope_a = r3.take("rope_a", [P, ATT], F32)
        rope_b = r3.take("rope_b", [P, ATT], F32)
        junk = r3.take("junk", [P, D], BF16)
        kcT = r3.take("kcT", [P, N_SAMPLE, P], F32)
        csr = r3.take("csr", [P, HD], F32)
        sink_t = r3.take("sink_t", [P, NQ], F32)
        bsT = r3.take("bsT", [P, NG], F32)
        gmix = r3.take("gmix", [P, DC], F32)
        st = r3.take("st", [P, 64], F32)
        sinkr = r3.take("sinkr", [P, 1], F32)
        w00 = r3.take("w00", [P, NG], F32)
        b00 = r3.take("b00", [P, NG], F32)
        r_s = Region(nc, base, r2.at, 147456)
        vc_t = r_s.take("vc_t", [P, N_SAMPLE, P], F32)
        sT_s = r_s.take("sT_s", [P, NKV, 32], F32)
        prod = r_s.take("prod", [P, 64], F32)
        s_s = r_s.take("s_s", [64, 132], F32)
        pT_s = r_s.take("pT_s", [P, 64], F32)
        selp = r_s.take("selp", [64, N_SAMPLE], F32)
        d_s = r_s.take("d_s", [N_SAMPLE, 64], F32)
        oT_s = r_s.take("oT_s", [P, N_SAMPLE, QPK], F32)
        q1 = Region(nc, base, 0, 114688)
        wo_hi = q1.take("wo_hi", [P, DC, D], F32R)
        wo_lo = q1.take("wo_lo", [P, DC, D], F32R)
        wo_in = Region(nc, base, q1.at - 4 * DC * D, q1.at).take("wo_in", [P, DC, D], F32)
        x1a = Region(nc, base, 114688, 147456).take("x1a", [P, T_P, D], F32)
        s2 = Region(nc, base, a1, 212800)
        x1b = s2.take("x1b", [P, D], F32)
        at4 = s2.at
        m_t = [s2.take(f"m_t{b}", [P, D], F32) for b in range(2)]
        h_t = s2.take("h_t", [P, D], F32)
        hT = s2.take("hT", [P, DC, P], F32)
        at4_end = s2.at = s_at
        mT_hi = [s2.take(f"mT_hi{b}", [P, DC, P], F32R) for b in range(2)]
        mT_lo = [s2.take(f"mT_lo{b}", [P, DC, P], F32R) for b in range(2)]
        at3, at3_end = s_at, s2.at
        ffg = s2.take("ffg", [P, D], F32)
        junk2 = s2.take("junk2", [P, D], BF16)
        w_r = s2.take("w_r", [P, DC, NGRP + NE], F32)
        b_rt = s2.take("b_rt", [P, NGRP + NE], F32)
        logits = s2.take("logits", [P, T, NGRP + NE], F32)
        s3 = Region(nc, base, s2.at, 212800)
        idx_src = s3.take("idx_src", [P, NE], I32)
        idx_dst = s3.take("idx_dst", [P, NE], I32)
        rk = s3.take("rk", [P, 2, T], F32)
        rhs_t = s3.take("rhs_t", [P, 2, T, 3 * NE], BF16)
        s3b = Region(nc, base, at3, at3_end)
        one_e = s3b.take("one_e", [P, 2, T, NE], F32)
        m_bf = s3b.take("m_bf", [P, T, NE], BF16)
        rank_s = s3b.take("rank_s", [P, T, NE], F32)
        tmp_e = s3b.take("tmp_e", [P, T, NE], F32)
        g8 = [s3b.take(f"g8_{n}", [P, T, EPG], F32) for n in range(6)]
        c9 = [s3b.take(f"c9_{n}", [P, T], F32) for n in range(12)]
        oh_r = s3b.take("oh_r", [P, 2, T, P], BF16)
        tr_bf = s3b.take("tr_bf", [P, P], BF16)
        on_bf = s3b.take("on_bf", [P, P], BF16)
        tab = s3b.take("tab", [P, 3 * NE], F32)
        tab2 = s3b.take("tab2", [P, 3, NE], F32)
        cnt_i = s3b.take("cnt_i", [P, 1], I32)
        wg = []
        wd = []
        for n, at in enumerate([65536, 90112, 0, 24576]):
            e = Region(nc, base, at, at + 24576)
            wg.append(e.take(f"wg{n}", [P, 2, DC, FE], F32))
            wd.append(e.take(f"wd{n}", [P, 2, D], F32))
        s4 = Region(nc, base, at4, at4_end)
        xg = [s4.take(f"xg{b}", [P, D], F32) for b in range(2)]
        xg += [Region(nc, base, at, at + 4 * D).take(f"xg{2 + n}", [P, D], F32) for n, at in enumerate([49152, 53248])]
        y_t = [s4.take(f"y_t{b}", [P, D], F32) for b in range(2)]
        sg = s4.take("sg", [P, FE], F32)
        s4b = Region(nc, base, s3b.at, at3_end)
        hid = s4b.take("hid", [P, FE], F32)
        hidT = s4b.take("hidT", [P, 2, P], F32)
        ic_src = s4b.take("ic_src", [P, 4], I32)
        ic_dst = s4b.take("ic_dst", [P, 4], I32)
        s4c = Region(nc, base, at3_end, at3_end + 4 * D)
        xgT = s4c.take("xgT", [P, DC, P], F32)
        s6 = Region(nc, base, 57344, 65536)
        fing = s6.take("fing", [P, D], F32)
        junk3 = s6.take("junk3", [P, D], BF16)
        fst = s6.take("fst", [P, 2, 4], F32)
        s6y = Region(nc, base, 0, 57344)
        yy = [s6y.take(f"yy{b}", [P, 2, D], F32) for b in range(4)]

        ident = cst[:, C_ID:C_ID + P]

        def x1(t):
            if isinstance(t, int) and t == T_P:
                return x1b[:]
            return x1a[:, t, :] if isinstance(t, int) else x1a[:, bass.ds(t, 1), :].squeeze(1)

        def rows(ap, t, n=P):
            return ap[t * P:t * P + n, :] if isinstance(t, int) else ap[bass.ds(t * P, n), :]

        s_settled = sem("s_settled")
        s_cst = sem("s_cst")
        s_small = sem("s_small")
        s_gmix = sem("s_gmix")
        s_ws = sem("s_ws")
        s_kc = sem("s_kc")
        s_vc = sem("s_vc")
        s_wi = [sem(f"s_wi{n}") for n in range(N_WI)]
        s_wo = [sem(f"s_wo{n}") for n in range(N_WO)]
        s_x = sem("s_x")
        s_whi = sem("s_whi")
        s_wlo = sem("s_wlo")
        s_zero = sem("s_zero")
        s_wmask = sem("s_wmask")
        s_tset = sem("s_tset")
        s_eset_a = sem("s_eset_a")
        s_eset_v = sem("s_eset_v")
        s_sq = sem("s_sq")
        s_rstd = sem("s_rstd")
        s_xTp = sem("s_xTp")
        s_xh = sem("s_xh")
        s_xl = sem("s_xl")
        s_z = sem("s_z")
        s_csr = sem("s_csr")
        s_qr = sem("s_qr")
        s_kr = sem("s_kr")
        s_qkTp = sem("s_qkTp")
        s_qT = sem("s_qT")
        s_kT = sem("s_kT")
        s_v = sem("s_v")
        s_vs = sem("s_vs")
        s_u = sem("s_u")
        s_vg = sem("s_vg")
        s_var = sem("s_var")
        s_lnr = sem("s_lnr")
        s_vn = sem("s_vn")
        s_sc = sem("s_sc")
        s_sm = sem("s_sm")
        s_nb = sem("s_nb")
        s_p = sem("s_p")
        s_pTp = sem("s_pTp")
        s_pTa = sem("s_pTa")
        s_pTv = sem("s_pTv")
        s_pv = sem("s_pv")
        s_gm = sem("s_gm")
        s_gmo = sem("s_gmo")
        s_att = sem("s_att")
        s_mix = sem("s_mix")
        s_kvout = sem("s_kvout")
        dve_step = sem("dve_step")
        act_step = sem("act_step")
        pool_step = sem("pool_step")
        s_sp = sem("s_sp")
        s_sv = sem("s_sv")
        s_sa = sem("s_sa")
        s_ml = [sem(f"s_ml{b}") for b in range(2)]
        s_xr = [sem(f"s_xr{b}") for b in range(2)]
        s_p2 = sem("s_p2")
        s_mTp = sem("s_mTp")
        s_mh = sem("s_mh")
        s_mlo = sem("s_mlo")
        s_op = sem("s_op")
        s_x1 = sem("s_x1")
        s_sq2 = sem("s_sq2")
        s_r2 = sem("s_r2")
        s_h = sem("s_h")
        s_hst = sem("s_hst")
        s_hTp = sem("s_hTp")
        s_hTa = sem("s_hTa")
        s_hTv = sem("s_hTv")
        s_lg = sem("s_lg")
        s_lgo = sem("s_lgo")
        s_rv = sem("s_rv")
        s_ra = sem("s_ra")
        s_rp = sem("s_rp")
        s_idx = sem("s_idx")
        s_wg = [sem(f"s_wg{n}") for n in range(4)]
        s_wd = [sem(f"s_wd{n}") for n in range(4)]
        s_isrc = sem("s_isrc")
        s_idst = sem("s_idst")
        s_ga = [sem(f"s_ga{k}") for k in range(4)]
        s_gTp = sem("s_gTp")
        s_gTa = sem("s_gTa")
        s_gTv = sem("s_gTv")
        s_gu = sem("s_gu")
        s_sg = sem("s_sg")
        s_hid = sem("s_hid")
        s_dTp = sem("s_dTp")
        s_dT = sem("s_dT")
        s_dn = sem("s_dn")
        s_ya = sem("s_ya")
        s_yv = sem("s_yv")
        s_sc4 = [sem(f"s_sc4_{b}") for b in range(2)]
        s_zx = sem("s_zx")
        o_idx = sem("o_idx")
        o_step = sem("o_step")
        o_free = sem("o_free")
        o_oh = sem("o_oh")
        o_tab = sem("o_tab")
        o_ic = sem("o_ic")
        o_w = sem("o_w")
        o_ga = sem("o_ga")
        o_gTp = sem("o_gTp")
        o_gTa = sem("o_gTa")
        o_gTv = sem("o_gTv")
        o_gu = sem("o_gu")
        o_sg = sem("o_sg")
        o_hid = sem("o_hid")
        o_dTp = sem("o_dTp")
        o_dT = sem("o_dT")
        o_dn = sem("o_dn")
        o_y = sem("o_y")
        o_ya = sem("o_ya")
        o_sc = sem("o_sc")
        o_done = sem("o_done")
        s_yy = [sem(f"s_yy{b}") for b in range(4)]
        s_fg = sem("s_fg")
        s_ysum = sem("s_ysum")
        s_fsq = sem("s_fsq")
        s_fr = sem("s_fr")
        s_fo = sem("s_fo")
        s_out = sem("s_out")

        block = ctx.enter_context(nc.Block())

        def settle(eng):
            eng.sem_inc(s_settled, 1)

        wo_r = w_out.rearrange("(c p) n -> p c n", p=P)

        def wi_piece(t, n):
            c0, c1 = WI_COLS[n // 4]
            return t[:, 2 * (n % 4):2 * (n % 4) + 2, c0:c1]

        def wo_raw(n):
            if n < WO_STAGED:
                return wo_stage[n][:].rearrange("p (c n) -> p c n", c=2)
            return wo_in[:, 2 * n:2 * n + 2, :]

        @block.sync
        def _(sp):
            wi_r = w_in.rearrange("(c p) n -> p c n", p=P)

            def load_wi(n):
                sp.dma_start(wi_piece(wi_raw, n), wi_piece(wi_r, n)).then_inc(s_wi[n], 16)

            def load_wo(n):
                sp.dma_start(wo_raw(n), wo_r[:, 2 * n:2 * n + 2, :]).then_inc(s_wo[n], 16)

            sp.dma_start(gmix[:], mix_g).then_inc(s_gmix, 16)
            load_wi(0)
            sp.dma_start(x_t[:], rows(x_rows, 0)).then_inc(s_x, 16)
            sp.dma_start(cst[:], consts).then_inc(s_cst, 16)
            for n in range(1, N_WI):
                load_wi(n)
            sp.dma_start(ws_raw[:], w_s.rearrange("g t s -> t g s")).then_inc(s_ws, 16)
            sp.dma_start(kc_t[:], cache_k.rearrange("b s n -> s b n")).then_inc(s_kc, 16)
            sp.dma_start(sink_t[:], sinks_b.to_broadcast([P, NQ])).then_inc(s_small, 16)
            sp.dma_start(lng[:], ln_g.to_broadcast([P, GW])).then_inc(s_small, 16)
            sp.dma_start(lnb[:], ln_b.to_broadcast([P, GW])).then_inc(s_small, 16)
            sp.dma_start(bsT[:], b_sT).then_inc(s_small, 16)
            sp.dma_start(sinkr[0:64, :], sink_rows).then_inc(s_small, 16)
            with nc.allow_non_contiguous_dma(reason="eight elements"):
                sp.dma_start(w00[0:N_SAMPLE, :], w_s[:, 0:1, 0:1].rearrange("g a b -> (a b) g")
                             .to_broadcast([N_SAMPLE, NG])).then_inc(s_small, 16)
                sp.dma_start(b00[0:N_SAMPLE, :], b_s[:, 0:1].rearrange("g a -> a g")
                             .to_broadcast([N_SAMPLE, NG])).then_inc(s_small, 16)

            def stage1(t):
                if not (isinstance(t, int) and t == T_P):
                    sp.wait_ge(s_xTp, 2 * t + 2)
                    settle(sp)
                    sp.wait_ge(s_sq, t + 1)
                    sp.dma_start(x_t[:], rows(x_rows, t + 1)).then_inc(s_x, 16)
                if isinstance(t, int) and t == T_P - 1:
                    sp.wait_ge(s_kr, t + 1)
                    sp.dma_start(k_prompt, k_ro[:]).then_inc(s_kvout, 16)
                    sp.wait_ge(s_v, t + 1)
                    sp.dma_start(v_prompt, v_new[:]).then_inc(s_kvout, 16)
                if not (isinstance(t, int) and t == 0):
                    sp.wait_ge(s_att, 2 * t)
                    sp.wait_ge(s_gmo, t)
                    sp.dma_start(rows(mix_d, t - 1), mix_t[:]).then_inc(s_mix, 16)

            stage1(0)
            stage1(1)
            sp.dma_start(vc_t[:], cache_v.rearrange("b s n -> s b n")).then_inc(s_vc, 16)
            for n in range(WO_STAGED):
                load_wo(n)
            with sp.Fori(2, T_P - 1) as t:
                stage1(t)
            stage1(T_P - 1)
            stage1(T_P)
            sp.wait_ge(s_z, 4 * T)
            sp.wait_ge(s_mix, 16)
            sp.dma_start(m_t[0][:], rows(mix_d, 0)).then_inc(s_ml[0], 16)
            for n in range(WO_STAGED, N_WO):
                load_wo(n)
            sp.wait_ge(s_kr, T)
            sp.dma_start(k_sample, k_ro[0:N_SAMPLE, :]).then_inc(s_kvout, 16)
            sp.wait_ge(s_v, T)
            sp.dma_start(v_sample, v_new[0:N_SAMPLE, :]).then_inc(s_kvout, 16)
            sp.wait_ge(s_gm, T_P)
            sp.dma_start(ffg[:], ffn_g.to_broadcast([P, D])).then_inc(s_p2, 16)
            sp.dma_start(w_r[:, :, 0:NGRP], w_rg.rearrange("(p c) n -> p c n", c=DC)).then_inc(s_p2, 16)
            sp.dma_start(w_r[:, :, NGRP:], w_re.rearrange("(p c) n -> p c n", c=DC)).then_inc(s_p2, 16)
            sp.dma_start(b_rt[:], b_r.to_broadcast([P, NGRP + NE])).then_inc(s_p2, 16)
            sp.wait_ge(s_vn, T)
            sp.dma_start(g_sample, vn_t[0:N_SAMPLE, :]).then_inc(s_kvout, 16)
            sp.wait_ge(s_wlo, N_WI + 1)
            sp.dma_start(x1(0), rows(x_rows, 0)).then_inc(s_xr[0], 16)

            def load_gate_up(e, k, done):
                for j, w in enumerate((w_gate, w_up)):
                    src = w[e] if isinstance(e, int) else w[bass.ds(e, 1)].squeeze(0)
                    sp.dma_start(wg[k][:, j], src.rearrange("(p c) f -> p c f", c=DC)).then_inc(done, 16)

            def load_down(e, k, done):
                src = w_down[e] if isinstance(e, int) else w_down[bass.ds(e, 1)].squeeze(0)
                sp.dma_start(wd[k][:], src.rearrange("(p c) n -> p c n", c=2)).then_inc(done, 16)

            def load_expert(e):
                load_gate_up(e, e, s_wg[e])
                load_down(e, e, s_wd[e])

            def stage2(t, b):
                if not (isinstance(t, int) and t == T_P):
                    if not (isinstance(t, int) and t == 0):
                        sp.wait_ge(s_mTp, 2 * t)
                    sp.dma_start(m_t[1 - b][:], rows(mix_d, t + 1)).then_inc(s_ml[1 - b], 16)
                    sp.dma_start(x1(t + 1), rows(x_rows, t + 1)).then_inc(s_xr[1 - b], 16)
                if not (isinstance(t, int) and t == 0):
                    store_h(t - 1)

            def store_h(t):
                sp.wait_ge(s_h, t + 1)
                sp.dma_start(rows(h_d, t), h_t[:]).then_inc(s_hst, 16)

            stage2(0, 0)
            load_expert(0)
            sp.wait_ge(s_sv, 10)
            sp.dma_start(rows(mix_d, T_P), mix_t[:]).then_inc(s_mix, 16)
            sp.wait_ge(s_mix, T * 16)
            sp.wait_ge(s_wlo, N_WI + N_WO)
            with sp.Fori(1, T_P - 2, 2) as t:
                stage2(t, 1)
                stage2(t + 1, 0)
            stage2(T_P - 1, 1)
            load_expert(1)
            stage2(T_P, 0)
            sp.wait_ge(s_op, 2 * T)
            load_gate_up(2, 2, s_wg[2])
            store_h(T_P)
            load_down(2, 2, s_wd[2])
            load_expert(3)

            def stage4(e, k):
                sp.wait_ge(s_gu, e - 3)
                load_gate_up(e, k, s_wg[k])
                sp.wait_ge(s_dn, e - 3)
                load_down(e, k, s_wd[k])

            with sp.Fori(4, NE - 3, 4) as e:
                for k in range(4):
                    stage4(e + k, k)
            sp.wait_ge(s_dn, NE)

            sp.wait_ge(s_idx, 1)
            most = sp.value_load(cnt_i[0:1, 0:1], min_val=0, max_val=N_TOK)
            with sp.If(most > SLOTS):
                with sp.Fori(0, N_CHUNK - 1) as m:
                    with sp.Fori(0, NE) as e:
                        sp.wait_ge(o_ic, m * NE + e + 1)
                        load_gate_up(e, 0, o_w)
                        load_down(e, 0, o_w)
            sp.dma_start(fing[:], fin_g.to_broadcast([P, D])).then_inc(s_fg, 16)
            sp.wait_ge(o_done, 1)

            def n_rows(t):
                return N_SAMPLE if t == T_P else P

            def load_y(t):
                src = y_d.rearrange("(r k) n -> r (k n)", k=2)
                sp.dma_start(yy[t % 4][0:n_rows(t)].rearrange("p k n -> p (k n)"), rows(src, t, n_rows(t)))\
                    .then_inc(s_yy[t % 4], 16)

            for t in range(4):
                load_y(t)
            for t in range(T):
                if t + 4 < T:
                    sp.wait_ge(s_ysum, t + 1)
                    load_y(t + 4)
                sp.wait_ge(s_fo, t + 1)
                sp.dma_start(rows(y_rows, t, n_rows(t)), x1(t)[0:n_rows(t)]).then_inc(s_out, 16)
            sp.wait_ge(s_out, 16 * T)

        @block.tensor
        def _(pe):
            def transposes(src, n, bank_):
                for j in range(n):
                    last = nc.tensor.transpose(bank_[:, j * P:(j + 1) * P], src(j), ident)
                return last

            def set_up():
                pe.wait_ge(s_wmask, 1)
                for b in range(2):
                    if b == 0:
                        pe.wait_ge(s_xh, 2)
                        pe.wait_ge(s_xl, 2)
                    transposes(lambda j: ws_raw[:, 4 * b + j, :], 4, psT[b]).then_inc(s_tset, 1)
                pe.wait_ge(s_kc, 16)
                for b in range(2):
                    pe.wait_ge(s_eset_a if b == 0 else s_eset_v, 1)
                    transposes(lambda j: kc_t[:, 4 * b + j, :], 4, psT[b]).then_inc(s_tset, 1)

            def t_x(t):
                pe.wait_ge(s_x, 16 * (t + 1))
                for b in range(2):
                    if isinstance(t, int) and t == 1 and b == 0:
                        pe.wait_ge(s_eset_a, 2)
                    elif not (isinstance(t, int) and t == 0):
                        pe.wait_ge(s_pTa if b == 0 else s_kT, 2 * t - 2 if b == 0 else t)
                    transposes(lambda j: x_t[:, (4 * b + j) * P:(4 * b + j + 1) * P], 4, psT[b]).then_inc(s_xTp, 1)

            def z_group(t, g):
                c0, n = Z_GROUPS[g]
                if g == 0:
                    pe.wait_ge(s_xh, 2 * t + 2)
                    pe.wait_ge(s_xl, 2 * t + 2)
                if g == 2:
                    pe.wait_ge(s_qr, t + 1)
                elif g == 3:
                    pe.wait_ge(s_kr, t + 1)
                    pe.wait_ge(s_v, t + 1)
                elif not (isinstance(t, int) and t == 0):
                    pe.wait_ge(s_u if g == 0 else s_vg, t)
                k = 0
                for c in range(DC):
                    if isinstance(t, int) and t == 0 and g % 2 == 0 and c % 2 == 0:
                        pe.wait_ge(s_whi, 2 * g + c // 2 + 1)
                        pe.wait_ge(s_wlo, 2 * g + c // 2 + 1)
                    for a, w in ((xT_hi, wi_hi), (xT_lo, wi_hi), (xT_hi, wi_lo)):
                        last = nc.tensor.matmul(psZ[g % 2][:, 0:n], a[:, c, :], w[:, c, c0:c0 + n],
                                                start=(k == 0), stop=(k == 3 * DC - 1))
                        k += 1
                last.then_inc(s_z, 1)

            def t_qk(t):
                pe.wait_ge(s_qr, t + 1)
                if not (isinstance(t, int) and t == 0):
                    pe.wait_ge(s_gmo, t)
                transposes(lambda j: q_ro[:, j * P:(j + 1) * P], 4, psG).then_inc(s_qkTp, 1)
                pe.wait_ge(s_kr, t + 1)
                if not (isinstance(t, int) and t == 0):
                    pe.wait_ge(s_pTv, 2 * t)
                else:
                    pe.wait_ge(s_eset_v, 2)
                transposes(lambda j: k_ro[:], 1, psT[1]).then_inc(s_qkTp, 1)

            def scores(t, g):
                if g == 0:
                    pe.wait_ge(s_qT, t + 1)
                    pe.wait_ge(s_kT, t + 1)
                    if not (isinstance(t, int) and t == 0):
                        pe.wait_ge(s_sm, 2 * t)
                else:
                    pe.wait_ge(s_sm, 2 * t + 1)
                rows_ = slice(g * HD, (g + 1) * HD)
                for c in range(QPK):
                    last = nc.tensor.matmul(psS[:, c * 256:(c + 1) * 256], qT[rows_, c, :], kT[rows_, :],
                                            start=True, stop=True, skip_group_check=True)
                last.then_inc(s_sc, 1)

            def t_p(t, g):
                pe.wait_ge(s_p, 2 * t + g + 1)
                for b in range(2):
                    if g == 1:
                        pe.wait_ge(s_pTa if b == 0 else s_pTv, 2 * t + 1)
                    transposes(lambda j: s_t[g][:, 2 * b + j // 2, (j % 2) * P:(j % 2 + 1) * P], 4, psT[b])\
                        .then_inc(s_pTp, 1)

            def pv(t, g):
                pe.wait_ge(s_pTa, 2 * t + g + 1)
                pe.wait_ge(s_pTv, 2 * t + g + 1)
                if g == 0:
                    pe.wait_ge(s_vs, t + 1)
                    if not (isinstance(t, int) and t == 0):
                        pe.wait_ge(s_att, 2 * t)
                else:
                    pe.wait_ge(s_att, 2 * t + 1)
                for c in range(QPK):
                    for k in range(2):
                        last = nc.tensor.matmul(psO[:, (g * QPK + c) * HD:(g * QPK + c + 1) * HD],
                                                pT[:, 2 * c + k, :], v_t[:, k, g * HD:(g + 1) * HD],
                                                start=(k == 0), stop=(k == 1), skip_group_check=True)
                last.then_inc(s_pv, 1)

            def gm(t):
                pe.wait_ge(s_vn, t + 1)
                pe.wait_ge(s_qT, t + 1)
                for g in range(NG):
                    last = nc.tensor.matmul(psG[:, g * HD:(g + 1) * HD], wsT[:, g, :], vn_t[:, g * HD:(g + 1) * HD],
                                            start=True, stop=True, skip_group_check=True)
                last.then_inc(s_gm, 1)

            def stage1(t):
                before = not (isinstance(t, int) and t == 0)
                sample = isinstance(t, int) and t == T_P
                z_group(t, 0)
                if before:
                    gm(t - 1)
                z_group(t, 1)
                if before:
                    t_p(t - 1, 0)
                    scores(t - 1, 1)
                    pv(t - 1, 0)
                z_group(t, 2)
                if before:
                    t_p(t - 1, 1)
                else:
                    set_up()
                z_group(t, 3)
                t_qk(t)
                if before:
                    pv(t - 1, 1)
                if not sample:
                    t_x(t + 1)
                    scores(t, 0)

            pe.wait_ge(s_cst, 16)
            t_x(0)
            stage1(0)
            stage1(1)
            with pe.Fori(2, T_P - 1) as t:
                stage1(t)
            stage1(T_P - 1)
            stage1(T_P)

            def sample_scores():
                pe.wait_ge(s_qT, T)
                pe.wait_ge(s_kT, T)
                pe.wait_ge(s_sm, 2 * T_P)
                for g in range(NKV):
                    r = slice(g * HD, (g + 1) * HD)
                    for b in range(N_SAMPLE):
                        last = nc.tensor.matmul(psS[:, 512 * g + 4 * b:512 * g + 4 * b + 4], kcT[r, b, :], qT[r, :, b],
                                                start=True, stop=True, skip_group_check=True)
                last.then_inc(s_sp, 1)
                pe.wait_ge(s_sv, 1)
                nc.tensor.matmul(psG[0:64, 128:129], prod[:], small[:, 0:1], start=True, stop=True).then_inc(s_sp, 1)

            def sample_rows():
                pe.wait_ge(s_sv, 2)
                nc.tensor.transpose(psO[0:64, 0:P], sT_s[:].rearrange("p g r -> p (g r)"), ident).then_inc(s_sp, 1)

            def sample_weights():
                pe.wait_ge(s_sv, 6)
                nc.tensor.transpose(psS[:, 0:64], s_s[:, 0:P], ident[0:64, 0:64]).then_inc(s_sp, 1)
                nc.tensor.matmul(psG[0:N_SAMPLE, 0:64], selp[:], ident[0:64, 0:64], start=True, stop=True)\
                    .then_inc(s_sp, 1)

            def sample_values():
                pe.wait_ge(s_sv, 8)
                pe.wait_ge(s_vc, 16)
                pe.wait_ge(s_v, T)
                nc.tensor.matmul(psO[:, 0:64], v_new[0:N_SAMPLE, :], d_s[:], start=True, stop=False, skip_group_check=True)
                for b in range(N_SAMPLE):
                    o = psO[:, 0:64].rearrange("p (g r) -> p g r", g=NKV)[:, :, 4 * b:4 * b + 4]
                    q = pT_s[:].rearrange("p (g r) -> p g r", g=NKV)[:, :, 4 * b:4 * b + 4]
                    last = nc.tensor.matmul(o, vc_t[:, b, :], q, start=False, stop=(b == N_SAMPLE - 1),
                                            skip_group_check=True)
                last.then_inc(s_sp, 1)

            def sample_out():
                pe.wait_ge(s_sv, 9)
                for c in range(QPK):
                    last = nc.tensor.transpose(psS[0:N_SAMPLE, 512 + c * P:512 + (c + 1) * P], oT_s[:, :, c], ident)
                last.then_inc(s_sp, 1)

            def t_m(t, b):
                pe.wait_ge(s_ml[b], (t - b + 2) * 8)
                for k in range(2):
                    if isinstance(t, int) and t == 0:
                        pe.wait_ge(s_pTa if k == 0 else s_kT, 2 * T_P if k == 0 else T)
                    else:
                        pe.wait_ge(s_mh, 2 * t - 1 + k)
                        pe.wait_ge(s_mlo, 2 * t - 1 + k)
                    transposes(lambda j: m_t[b][:, (4 * k + j) * P:(4 * k + j + 1) * P], 4, psT[k]).then_inc(s_mTp, 1)

            def out_half(t, b, h):
                if h == 0:
                    pe.wait_ge(s_mh, 2 * t + 2)
                    pe.wait_ge(s_mlo, 2 * t + 2)
                if isinstance(t, int) and t == 0:
                    pe.wait_ge(s_u if h == 0 else s_vg, T)
                else:
                    pe.wait_ge(s_x1, 2 * t - 1 + h)
                k = 0
                for c in range(DC):
                    if isinstance(t, int) and t == 0 and h == 0 and c % 2 == 0:
                        pe.wait_ge(s_whi, N_WI + c // 2 + 1)
                        pe.wait_ge(s_wlo, N_WI + c // 2 + 1)
                    for a, w in ((mT_hi, wo_hi), (mT_lo, wo_hi), (mT_hi, wo_lo)):
                        last = nc.tensor.matmul(psZ[h][:], a[b][:, c, :], w[:, c, h * 512:(h + 1) * 512],
                                                start=(k == 0), stop=(k == 3 * DC - 1))
                        k += 1
                last.then_inc(s_op, 1)

            def t_h(t):
                pe.wait_ge(s_h, t + 1)
                if isinstance(t, int) and t == 0:
                    pe.wait_ge(s_sv, 10)
                if not (isinstance(t, int) and t == 0):
                    pe.wait_ge(s_hTa, t)
                    pe.wait_ge(s_hTv, t)
                for j in range(DC):
                    last = nc.tensor.transpose(psS[:, j * P:(j + 1) * P], h_t[:, j * P:(j + 1) * P], ident)
                last.then_inc(s_hTp, 1)

            def route(t):
                pe.wait_ge(s_hTa, t + 1)
                pe.wait_ge(s_hTv, t + 1)
                if isinstance(t, int) and t == 0:
                    pe.wait_ge(s_p2, 64)
                else:
                    pe.wait_ge(s_lgo, t)
                for c in range(DC):
                    last = nc.tensor.matmul(psG[:, 0:NGRP + NE], hT[:, c, :], w_r[:, c, :],
                                            start=(c == 0), stop=(c == DC - 1))
                last.then_inc(s_lg, 1)

            def stage2(t, b):
                first = isinstance(t, int) and t == 0
                out_half(t, b, 0)
                if not (isinstance(t, int) and t == T_P):
                    t_m(t + 1, 1 - b)
                if first:
                    sample_weights()
                else:
                    t_h(t - 1)
                out_half(t, b, 1)
                if first:
                    sample_values()
                    sample_out()
                else:
                    route(t - 1)

            sample_scores()
            sample_rows()
            t_m(0, 0)
            stage2(0, 0)
            with pe.Fori(1, T_P - 2, 2) as t:
                stage2(t, 1)
                stage2(t + 1, 0)
            stage2(T_P - 1, 1)
            stage2(T_P, 0)
            t_h(T_P)
            route(T_P)

            pe.wait_ge(s_rv, 1)
            mm = lambda out, a, b, **k: nc.tensor.matmul(out, a, b, skip_group_check=True, **k)
            mm(psZ[0][:, 0:T * NE], tr_bf[:], m_bf[:].rearrange("p t e -> p (t e)"), start=True, stop=False)
            for j in range(T - 1):
                last = mm(psZ[0][:, (j + 1) * NE:T * NE].rearrange("p (t e) -> p t e", e=NE), on_bf[:],
                          m_bf[:, j:j + 1, :].to_broadcast([P, T - 1 - j, NE]), start=False, stop=(j == T - 2))
            for j in range(T):
                last = mm(psZ[1][:, 0:NE], on_bf[:], m_bf[:, j, :], start=(j == 0), stop=(j == T - 1))
            last.then_inc(s_rp, 1)

            def table(done):
                for t in range(T):
                    for k in range(2):
                        last = mm(psG[:, 0:3 * NE], oh_r[:, k, t, :], rhs_t[:, k, t, :],
                                  start=(t == 0 and k == 0), stop=(t == T - 1 and k == 1))
                last.then_inc(done, 1)

            pe.wait_ge(s_rv, 2)
            table(s_rp)

            def t_g(slot, done):
                for k in range(2):
                    transposes(lambda j: xg[slot][:, (4 * k + j) * P:(4 * k + j + 1) * P], 4, psT[k]).then_inc(done, 1)

            def gate_up(z, w, done):
                for c in range(DC):
                    last = nc.tensor.matmul(psZ[z][:], xgT[:, c, :], w[:, :, c, :], start=(c == 0), stop=(c == DC - 1))
                last.then_inc(done, 1)

            def t_hid(done):
                transposes(lambda j: hid[:, j * P:(j + 1) * P], 2, psO).then_inc(done, 1)

            def down(w, done):
                for h in range(2):
                    for c in range(2):
                        last = nc.tensor.matmul(psS[:, h * 512:(h + 1) * 512], hidT[:, c, :],
                                                w[:, c, h * 512:(h + 1) * 512], start=(c == 0), stop=(c == 1))
                last.then_inc(done, 1)

            def first_g(e, k):
                pe.wait_ge(s_ga[k], (e - k + 4) * 4)
                if not (isinstance(e, int) and e == 0):
                    pe.wait_ge(s_gTa, e)
                    pe.wait_ge(s_gTv, e)
                t_g(k, s_gTp)

            def last_d(e, k):
                pe.wait_ge(s_dT, e + 1)
                if not (isinstance(e, int) and e == 0):
                    pe.wait_ge(s_ya, e)
                    pe.wait_ge(s_yv, e)
                pe.wait_ge(s_wd[k], (e - k + 4) * 4)
                down(wd[k], s_dn)

            def stage4(e, k):
                b = k % 2
                pe.wait_ge(s_gTa, e + 1)
                pe.wait_ge(s_gTv, e + 1)
                pe.wait_ge(s_wg[k], (e - k + 4) * 8)
                if not (isinstance(e, int) and e < 2):
                    pe.wait_ge(s_hid, e - 1)
                gate_up(b, wg[k][:], s_gu)
                if not (isinstance(e, int) and e == NE - 1):
                    first_g(e + 1, (k + 1) % 4)
                if not (isinstance(e, int) and e == 0):
                    last_d(e - 1, (k + 3) % 4)
                pe.wait_ge(s_hid, e + 1)
                t_hid(s_dTp)

            first_g(0, 0)
            for k in range(4):
                stage4(k, k)
            with pe.Fori(4, NE - 7, 4) as e:
                for k in range(4):
                    stage4(e + k, k)
            for k in range(4):
                stage4(NE - 4 + k, k)
            last_d(NE - 1, 3)

            pe.wait_ge(s_idx, 1)
            most = pe.value_load(cnt_i[0:1, 0:1], min_val=0, max_val=N_TOK)
            with pe.If(most > SLOTS):
                with pe.Fori(0, N_CHUNK - 1) as m:
                    pe.wait_ge(o_oh, m + 1)
                    table(o_tab)
                    with pe.Fori(0, NE) as e:
                        n = m * NE + e
                        pe.wait_ge(o_ga, 16 * n + 16)
                        t_g(0, o_gTp)
                        pe.wait_ge(o_gTa, n + 1)
                        pe.wait_ge(o_gTv, n + 1)
                        pe.wait_ge(o_w, 48 * n + 48)
                        gate_up(0, wg[0][:], o_gu)
                        pe.wait_ge(o_hid, n + 1)
                        t_hid(o_dTp)
                        pe.wait_ge(o_dT, n + 1)
                        down(wd[0], o_dn)

        @block.scalar
        def _(act):
            act.wait_ge(s_gmix, 16)

            def split(n):
                act.wait_ge(s_wi[n], 16)
                for c in range(2):
                    g = 2 * (n % 4) + c
                    last = nc.scalar.activation(wi_piece(wi_hi, n)[:, c, :], wi_piece(wi_raw, n)[:, c, :],
                                                ACT.Copy, scale=gmix[:, g:g + 1])
                last.then_inc(s_whi, 1)

            def copy(out, in_):
                return nc.scalar.activation(out, in_, ACT.Copy)

            def set_up():
                act.wait_ge(s_tset, 1)
                copy(wsT[:, 0:4, :].rearrange("p g t -> p (g t)"), psT[0][:]).then_inc(s_eset_a, 1)
                act.wait_ge(s_tset, 3)
                copy(kcT[:, 0:4, :].rearrange("p g t -> p (g t)"), psT[0][:]).then_inc(s_eset_a, 1)

            def square(t):
                act.wait_ge(s_x, 16 * (t + 1))
                if not (isinstance(t, int) and t == 0):
                    act.wait_ge(s_rstd, t)
                    act.wait_ge(s_sq, t)
                nc.scalar.activation(junk[:], x_t[:], ACT.Square, accum_out=st[:, 0:1]).then_inc(s_sq, 1)

            def x_hi(t):
                for b in range(2):
                    act.wait_ge(s_xTp, 2 * t + b + 1)
                    if not (isinstance(t, int) and t == 0):
                        act.wait_ge(s_z, 4 * t)
                    copy(xT_hi[:, 4 * b:4 * b + 4, :].rearrange("p c t -> p (c t)"), psT[b][:]).then_inc(s_xh, 1)

            def exps(t, g):
                act.wait_ge(s_nb, 2 * t + g + 1)
                for c in range(QPK):
                    h = g * QPK + c
                    nc.scalar.activation(s_t[g][:, c, :], s_t[g][:, c, :], ACT.Exp, bias=st[:, 8 + h:9 + h],
                                         accum_out=st[:, 16 + h:17 + h])
                nc.scalar.activation(st[:, 32 + 4 * g:36 + 4 * g], st[:, 24 + 4 * g:28 + 4 * g], ACT.Exp).then_inc(s_p, 1)

            def p_out(t, g):
                act.wait_ge(s_pTp, 4 * t + 2 * g + 1)
                if g == 1:
                    act.wait_ge(s_pv, 2 * t + 1)
                elif not (isinstance(t, int) and t == 0):
                    act.wait_ge(s_pv, 2 * t)
                copy(pT[:, 0:4, :].rearrange("p j t -> p (j t)"), psT[0][:]).then_inc(s_pTa, 1)

            def values(t):
                act.wait_ge(s_rstd, t + 1)
                act.wait_ge(s_kr, t + 1)
                if isinstance(t, int) and t == T_P:
                    act.wait_ge(s_kvout, 32)
                if not (isinstance(t, int) and t == 0):
                    act.wait_ge(s_vs, t)
                nc.scalar.activation(v_new[:], psZ[1][:, P:2 * P], ACT.Copy, scale=st[:, 2:3]).then_inc(s_v, 1)

            def shift(t):
                if isinstance(t, int) and t == 0:
                    act.wait_ge(s_zero, 1)
                else:
                    act.wait_ge(s_pv, 2 * t)
                    copy(v_t[:, 0, :], v_t[:, 1, :]).then_inc(act_step, 1)
                    act.wait_ge(act_step, t)
                act.wait_ge(s_v, t + 1)
                copy(v_t[:, 1, :], v_new[:]).then_inc(s_vs, 1)

            def gelu_u(t):
                act.wait_ge(s_z, 4 * t + 3)
                if not (isinstance(t, int) and t == 0):
                    act.wait_ge(s_gmo, t)
                nc.scalar.activation(u_t[:], psZ[0][:], ACT.Gelu, scale=st[:, 2:3]).then_inc(s_u, 1)

            def gelu_v(t):
                act.wait_ge(s_z, 4 * t + 4)
                if not (isinstance(t, int) and t == 0):
                    act.wait_ge(s_vn, t)
                nc.scalar.activation(vg_t[:], psZ[1][:], ACT.Gelu, scale=st[:, 2:3]).then_inc(s_vg, 1)

            def q_out(t):
                act.wait_ge(s_qkTp, 2 * t + 1)
                if not (isinstance(t, int) and t == 0):
                    act.wait_ge(s_sc, 2 * t)
                copy(qT[:].rearrange("p c t -> p (c t)"), psG[:]).then_inc(s_qT, 1)

            def stage1(t):
                before = not (isinstance(t, int) and t == 0)
                sample = isinstance(t, int) and t == T_P
                if before:
                    exps(t - 1, 0)
                    p_out(t - 1, 0)
                else:
                    for n in range(4, N_WI):
                        split(n)
                values(t)
                if before:
                    exps(t - 1, 1)
                    p_out(t - 1, 1)
                else:
                    set_up()
                gelu_u(t)
                q_out(t)
                gelu_v(t)
                if not sample:
                    x_hi(t + 1)
                    shift(t)
                    square(t + 1)

            split(0)
            split(1)
            square(0)
            x_hi(0)
            split(2)
            split(3)
            stage1(0)
            stage1(1)
            with act.Fori(2, T_P - 1) as t:
                stage1(t)
            stage1(T_P - 1)
            stage1(T_P)

            def sample_exps():
                act.wait_ge(s_sv, 4)
                nc.scalar.activation(s_s[:, 0:129], s_s[:, 0:129], ACT.Exp, bias=st[0:64, 40:41], scale=SCALE,
                                     accum_out=st[0:64, 42:43])
                nc.scalar.activation(st[0:64, 43:44], st[0:64, 41:42], ACT.Exp).then_inc(s_sa, 1)

            def split_out(n):
                act.wait_ge(s_z, 4 * T)
                act.wait_ge(s_wo[n], 16)
                copy(wo_hi[:, 2 * n:2 * n + 2, :], wo_raw(n)).then_inc(s_whi, 1)

            def m_hi(t, b):
                for k in range(2):
                    act.wait_ge(s_mTp, 2 * t + k + 1)
                    if not (isinstance(t, int) and t < 2):
                        act.wait_ge(s_op, 2 * t - 2)
                    copy(mT_hi[b][:, 4 * k:4 * k + 4, :].rearrange("p c t -> p (c t)"), psT[k][:]).then_inc(s_mh, 1)

            def square2(t):
                act.wait_ge(s_x1, 2 * t + 2)
                if not (isinstance(t, int) and t == 0):
                    act.wait_ge(s_r2, t)
                    act.wait_ge(s_sq2, t)
                nc.scalar.activation(junk2[:], x1(t), ACT.Square, accum_out=small[:, 8:9]).then_inc(s_sq2, 1)

            def h_out(t):
                act.wait_ge(s_hTp, t + 1)
                if not (isinstance(t, int) and t == 0):
                    act.wait_ge(s_lg, t)
                copy(hT[:, 0:4, :].rearrange("p c t -> p (c t)"), psS[:, 0:512]).then_inc(s_hTa, 1)

            def stage2(t, b):
                if not (isinstance(t, int) and t == T_P):
                    m_hi(t + 1, 1 - b)
                if not (isinstance(t, int) and t == 0):
                    h_out(t - 1)
                square2(t)

            split_out(0)
            split_out(1)
            m_hi(0, 0)
            split_out(2)
            split_out(3)
            sample_exps()
            stage2(0, 0)
            with act.Fori(1, T_P - 2, 2) as t:
                stage2(t, 1)
                stage2(t + 1, 0)
            stage2(T_P - 1, 1)
            stage2(T_P, 0)
            h_out(T_P)

            act.wait_ge(s_ra, 1)
            nc.scalar.activation(g8[0][:, :, 0:4], g8[0][:, :, 0:4], ACT.Exp).then_inc(s_sa, 1)
            act.wait_ge(s_ra, 2)
            nc.scalar.activation(c9[6][:], c9[6][:], ACT.Exp).then_inc(s_sa, 1)

            def g_out(e):
                act.wait_ge(s_gTp, 2 * e + 1)
                if not (isinstance(e, int) and e == 0):
                    act.wait_ge(s_gu, e)
                copy(xgT[:, 0:4, :].rearrange("p c t -> p (c t)"), psT[0][:]).then_inc(s_gTa, 1)

            def silu(e, b):
                act.wait_ge(s_gu, e + 1)
                if not (isinstance(e, int) and e == 0):
                    act.wait_ge(s_hid, e)
                nc.scalar.activation(sg[:], psZ[b][:, 0:FE], ACT.Silu).then_inc(s_sg, 1)

            def hid_out(e):
                act.wait_ge(s_dTp, e + 1)
                if not (isinstance(e, int) and e == 0):
                    act.wait_ge(s_dn, e)
                copy(hidT[:].rearrange("p c t -> p (c t)"), psO[:, 0:256]).then_inc(s_dT, 1)

            def y_out(e, b):
                act.wait_ge(s_dn, e + 1)
                if not (isinstance(e, int) and e < 2):
                    act.wait_ge(s_sc4[b], (e - b) * 8)
                copy(y_t[b][:, 0:512], psS[:, 0:512]).then_inc(s_ya, 1)

            def stage4(e, k):
                b = k % 2
                silu(e, b)
                if not (isinstance(e, int) and e == NE - 1):
                    g_out(e + 1)
                if not (isinstance(e, int) and e == 0):
                    y_out(e - 1, 1 - b)
                hid_out(e)

            g_out(0)
            for k in range(4):
                stage4(k, k)
            with act.Fori(4, NE - 7, 4) as e:
                for k in range(4):
                    stage4(e + k, k)
            for k in range(4):
                stage4(NE - 4 + k, k)
            y_out(NE - 1, 1)

            act.wait_ge(s_idx, 1)
            most = act.value_load(cnt_i[0:1, 0:1], min_val=0, max_val=N_TOK)
            with act.If(most > SLOTS):
                with act.Fori(0, (N_CHUNK - 1) * NE) as n:
                    act.wait_ge(o_gTp, 2 * n + 1)
                    copy(xgT[:, 0:4, :].rearrange("p c t -> p (c t)"), psT[0][:]).then_inc(o_gTa, 1)
                    act.wait_ge(o_gu, n + 1)
                    nc.scalar.activation(sg[:], psZ[0][:, 0:FE], ACT.Silu).then_inc(o_sg, 1)
                    act.wait_ge(o_dTp, n + 1)
                    copy(hidT[:].rearrange("p c t -> p (c t)"), psO[:, 0:256]).then_inc(o_dT, 1)
                    act.wait_ge(o_dn, n + 1)
                    copy(y_t[0][:, 0:512], psS[:, 0:512]).then_inc(o_ya, 1)
            act.wait_ge(o_done, 1)

            def sq_final(t, b, n=P):
                act.wait_ge(s_ysum, t + 1)
                if not (isinstance(t, int) and t == 0):
                    act.wait_ge(s_fsq, t)
                if not (isinstance(t, int) and t < 2):
                    act.wait_ge(s_fr, t - 1)
                nc.scalar.activation(junk3[0:n], x1(t)[0:n], ACT.Square, accum_out=fst[0:n, b, 0:1]).then_inc(s_fsq, 1)

            sq_final(0, 0)
            with act.Fori(1, T_P - 2, 2) as t:
                sq_final(t, 1)
                sq_final(t + 1, 0)
            sq_final(T_P - 1, 1)
            sq_final(T_P, 0, N_SAMPLE)

        @block.vector
        def _(dve):
            step = Chain(dve, dve_step)
            tt = nc.vector.tensor_tensor
            ts = nc.vector.tensor_scalar
            stt = nc.vector.scalar_tensor_tensor
            cp = nc.vector.tensor_copy
            nc.vector.memset(kT[:], 0.0)
            nc.vector.memset(v_t[:], 0.0)
            nc.vector.memset(small[:, 0:1], 1.0).then_inc(s_zero, 1)
            dve.wait_ge(s_zero, 1)
            dve.wait_ge(s_cst, 16)
            dve.wait_ge(s_gmix, 16)

            def split(n):
                dve.wait_ge(s_wi[n], 16)
                dve.wait_ge(s_whi, n + 1)
                for c in range(2):
                    g = 2 * (n % 4) + c
                    last = stt(out=wi_piece(wi_lo, n)[:, c, :], in0=wi_piece(wi_raw, n)[:, c, :], scalar=gmix[:, g:g + 1],
                               in1=wi_piece(wi_hi, n)[:, c, :].bitcast(F32), op0=ALU.mult, op1=ALU.subtract)
                last.then_inc(s_wlo, 1)

            def x_lo(t):
                for b in range(2):
                    dve.wait_ge(s_xh, 2 * t + b + 1)
                    dst = slice(4 * b, 4 * b + 4)
                    tt(xT_lo[:, dst, :].rearrange("p c t -> p (c t)"), psT[b][:],
                       xT_hi[:, dst, :].rearrange("p c t -> p (c t)").bitcast(F32), ALU.subtract).then_inc(s_xl, 1)

            def set_up():
                dve.wait_ge(s_tset, 2)
                cp(wsT[:, 4:8, :].rearrange("p g t -> p (g t)"), psT[1][:]).then_inc(s_eset_v, 1)
                dve.wait_ge(s_tset, 4)
                cp(kcT[:, 4:8, :].rearrange("p g t -> p (g t)"), psT[1][:]).then_inc(s_eset_v, 1)

            def rope(src, n, dst):
                cos = csr[:, 0:32].unsqueeze(1).unsqueeze(1).to_broadcast([P, n, 2, 32])
                sin = csr[:, 32:64].unsqueeze(1).unsqueeze(1).to_broadcast([P, n, 2, 32])
                a = rope_a[:, 0:n * HD].rearrange("p (h two d) -> p h two d", two=2, d=32)
                b = rope_b[:, 0:n * HD].rearrange("p (h two d) -> p h two d", two=2, d=32)
                src4 = src.rearrange("p (h two d) -> p h two d", two=2, d=32)
                tt(a, src4, cos, ALU.mult)
                step(tt(b, src4, sin, ALU.mult))
                tt(dst[0], a[:, :, 0, :], b[:, :, 1, :], ALU.subtract)
                return tt(dst[1], a[:, :, 1, :], b[:, :, 0, :], ALU.add)

            def rope_q(t):
                dve.wait_ge(s_rstd, t + 1)
                cs = cst[:, C_CS + t * HD:C_CS + t * HD + HD] if isinstance(t, int) else cst[:, bass.ds(t * HD + C_CS, HD)]
                step(ts(csr[:], cs, st[:, 2:3], None, ALU.mult))
                dve.wait_ge(s_z, 4 * t + 1)
                if not (isinstance(t, int) and t == 0):
                    dve.wait_ge(s_qkTp, 2 * t)
                q = q_ro[:].rearrange("p (c k two d) -> p k c two d", k=2, two=2, d=32)
                for k in range(2):
                    last = rope(psZ[0][:, k * 256:(k + 1) * 256], QPK, (q[:, k, :, 0, :], q[:, k, :, 1, :]))
                    if k == 0:
                        step(last)
                last.then_inc(s_qr, 1)

            def rope_k(t):
                dve.wait_ge(s_z, 4 * t + 2)
                dve.wait_ge(s_qr, t + 1)
                if isinstance(t, int) and t == T_P:
                    dve.wait_ge(s_kvout, 32)
                k = k_ro[:].rearrange("p (k two d) -> p k two d", two=2, d=32)
                rope(psZ[1][:, 0:P], NKV, (k[:, :, 0, :], k[:, :, 1, :])).then_inc(s_kr, 1)

            def softmax(t, g):
                dve.wait_ge(s_sc, 2 * t + g + 1)
                if not (isinstance(t, int) and t == 0):
                    dve.wait_ge(s_pTp, 4 * t - 2 + 2 * g)
                    dve.wait_ge(s_att, 2 * t - 1 + g)
                first = isinstance(t, int) and t == 0
                c = C_MF if first else C_MR
                mask = cst[:, c:c + 2 * P].unsqueeze(1).to_broadcast([P, QPK, 2 * P])
                stt(out=s_t[g][:], in0=psS[:].rearrange("p (c s) -> p c s", c=QPK), scalar=SCALE, in1=mask,
                    op0=ALU.mult, op1=ALU.add).then_inc(s_sm, 1)
                dve.wait_ge(s_sm, 2 * t + g + 1)
                mx = st[:, 44 + 4 * g:48 + 4 * g]
                sink = sink_t[:, 4 * g:4 * g + 4]
                step(nc.vector.tensor_reduce(mx, s_t[g][:], AX, ALU.max))
                step(tt(mx, mx, sink, ALU.max))
                ts(st[:, 8 + 4 * g:12 + 4 * g], mx, -1.0, None, ALU.mult)
                tt(st[:, 24 + 4 * g:28 + 4 * g], sink, mx, ALU.subtract).then_inc(s_nb, 1)

            def p_out(t, g):
                dve.wait_ge(s_pTp, 4 * t + 2 * g + 2)
                if g == 1:
                    dve.wait_ge(s_pv, 2 * t + 1)
                elif not (isinstance(t, int) and t == 0):
                    dve.wait_ge(s_pv, 2 * t)
                cp(pT[:, 4:8, :].rearrange("p j t -> p (j t)"), psT[1][:]).then_inc(s_pTv, 1)

            def att_out(t, g):
                dve.wait_ge(s_p, 2 * t + g + 1)
                r = st[:, 52 + 4 * g:56 + 4 * g]
                step(tt(r, st[:, 16 + 4 * g:20 + 4 * g], st[:, 32 + 4 * g:36 + 4 * g], ALU.add))
                step(nc.vector.reciprocal(r, r))
                dve.wait_ge(s_pv, 2 * t + g + 1)
                w = QPK * HD
                tt(mix_t[:, g * w:(g + 1) * w].rearrange("p (c d) -> p c d", c=QPK),
                   psO[:, g * w:(g + 1) * w].rearrange("p (c d) -> p c d", c=QPK),
                   r.unsqueeze(2).to_broadcast([P, QPK, HD]), ALU.mult).then_inc(s_att, 1)

            def gm_out(t):
                dve.wait_ge(s_gm, t + 1)
                dve.wait_ge(s_u, t + 1)
                if not (isinstance(t, int) and t == 0):
                    dve.wait_ge(s_mix, 16 * t)
                half = mix_t[:, ATT:D]
                step(tt(half.rearrange("p (g d) -> p g d", g=NG), psG[:].rearrange("p (g d) -> p g d", g=NG),
                        bsT[:].unsqueeze(2).to_broadcast([P, NG, HD]), ALU.add))
                tt(half, half, u_t[:], ALU.mult).then_inc(s_gmo, 1)

            def norm_v(t):
                dve.wait_ge(s_vg, t + 1)
                step(nc.vector.bn_stats(rope_a[:, 0:6], vg_t[:]))
                settle(dve)
                nc.vector.bn_aggr(st[:, 3:5], rope_a[:, 0:6]).then_inc(s_var, 1)
                dve.wait_ge(s_var, t + 1)
                if not (isinstance(t, int) and t == 0):
                    dve.wait_ge(s_gm, t)
                step(stt(out=vn_t[:], in0=vg_t[:], scalar=st[:, 3:4], in1=lng[:], op0=ALU.subtract, op1=ALU.mult))
                dve.wait_ge(s_lnr, t + 1)
                stt(out=vn_t[:], in0=vn_t[:], scalar=st[:, 6:7], in1=lnb[:], op0=ALU.mult, op1=ALU.add).then_inc(s_vn, 1)

            def k_out(t):
                dve.wait_ge(s_qkTp, 2 * t + 2)
                if not (isinstance(t, int) and t == 0):
                    dve.wait_ge(s_sc, 2 * t)
                    dve.wait_ge(s_kT, t)
                    step(cp(kT[:, 0:P], kT[:, P:2 * P]))
                cp(kT[:, P:2 * P], psT[1][:, 0:P]).then_inc(s_kT, 1)

            def stage1(t):
                before = not (isinstance(t, int) and t == 0)
                sample = isinstance(t, int) and t == T_P
                if before:
                    softmax(t - 1, 0)
                else:
                    split(4)
                    split(5)
                rope_q(t)
                if before:
                    gm_out(t - 1)
                    p_out(t - 1, 0)
                    softmax(t - 1, 1)
                    att_out(t - 1, 0)
                rope_k(t)
                if before:
                    p_out(t - 1, 1)
                else:
                    split(6)
                    split(7)
                    set_up()
                    dve.wait_ge(s_small, 16 * 7)
                k_out(t)
                if before:
                    att_out(t - 1, 1)
                if not sample:
                    x_lo(t + 1)
                norm_v(t)

            split(0)
            split(1)
            x_lo(0)
            split(2)
            split(3)
            stage1(0)
            n1 = step.n
            stage1(1)
            per = step.n - n1
            n2 = step.n
            with dve.Fori(2, T_P - 1) as t:
                step.n = (t - 2) * per + n2
                stage1(t)
            step.n = n2 + (T_P - 3) * per
            stage1(T_P - 1)
            stage1(T_P)

            def sample_products():
                dve.wait_ge(s_qT, T)
                dve.wait_ge(s_kT, T)
                step(nc.vector.memset(prod[:], 0.0))
                for g in range(NKV):
                    r = slice(g * HD, (g + 1) * HD)
                    last = tt(prod[r, 32 * g:32 * g + 32].rearrange("p (b c) -> p b c", c=QPK),
                              qT[r, :, 0:N_SAMPLE].rearrange("p c b -> p b c"),
                              kT[r, P:P + N_SAMPLE].unsqueeze(2).to_broadcast([HD, N_SAMPLE, QPK]), ALU.mult)
                last.then_inc(s_sv, 1)

            def sample_cache_scores():
                dve.wait_ge(s_sp, 1)
                cp(sT_s[:], psS[:].rearrange("p (g r) -> p g r", g=NKV)[:, :, 0:32]).then_inc(s_sv, 1)

            def sample_gmlp():
                dve.wait_ge(s_mix, 16 * T_P)
                step(nc.vector.memset(mix_t[:], 0.0))
                dve.wait_ge(s_vn, T)
                dve.wait_ge(s_u, T)
                v3 = vn_t[0:N_SAMPLE, :].rearrange("p (g d) -> p g d", g=NG)
                m3 = mix_t[0:N_SAMPLE, ATT:D].rearrange("p (g d) -> p g d", g=NG)
                step(tt(m3, v3, w00[0:N_SAMPLE, :].unsqueeze(2).to_broadcast([N_SAMPLE, NG, HD]), ALU.mult))
                step(tt(m3, m3, b00[0:N_SAMPLE, :].unsqueeze(2).to_broadcast([N_SAMPLE, NG, HD]), ALU.add))
                step(tt(mix_t[0:N_SAMPLE, ATT:D], mix_t[0:N_SAMPLE, ATT:D], u_t[0:N_SAMPLE, :], ALU.mult))

            def sample_maxima():
                dve.wait_ge(s_sp, 3)
                cp(s_s[:, 0:P], psO[0:64, 0:P])
                cp(s_s[:, P:P + 1], psG[0:64, 128:129]).then_inc(s_sv, 1)
                dve.wait_ge(s_sv, 3)
                step(nc.vector.tensor_reduce(st[0:64, 44:45], s_s[:, 0:P + 1], AX, ALU.max))
                step(ts(st[0:64, 44:45], st[0:64, 44:45], SCALE, sinkr[0:64, :], ALU.mult, ALU.max))
                ts(st[0:64, 40:41], st[0:64, 44:45], -1.0, None, ALU.mult)
                tt(st[0:64, 41:42], sinkr[0:64, :], st[0:64, 44:45], ALU.subtract).then_inc(s_sv, 1)

            def sample_weights():
                dve.wait_ge(s_sa, 1)
                step(tt(st[0:64, 45:46], st[0:64, 42:43], st[0:64, 43:44], ALU.add))
                step(nc.vector.reciprocal(st[0:64, 45:46], st[0:64, 45:46]))
                ts(s_s[:, 0:P + 1], s_s[:, 0:P + 1], st[0:64, 45:46], None, ALU.mult).then_inc(s_sv, 1)
                dve.wait_ge(s_sv, 5)
                ts(selp[:], cst[0:64, C_SEL:C_SEL + N_SAMPLE], s_s[:, P:P + 1], None, ALU.mult).then_inc(s_sv, 1)

            def sample_weights_out():
                dve.wait_ge(s_sp, 4)
                cp(pT_s[:], psS[:, 0:64]).then_inc(s_sv, 1)
                dve.wait_ge(s_sp, 5)
                cp(d_s[:], psG[0:N_SAMPLE, 0:64]).then_inc(s_sv, 1)

            def sample_values_out():
                dve.wait_ge(s_sp, 6)
                for g in range(NKV):
                    r = slice(g * HD, (g + 1) * HD)
                    last = cp(oT_s[r, :, :].rearrange("p b c -> p (b c)"), psO[r, 32 * g:32 * g + 32])
                last.then_inc(s_sv, 1)

            def sample_rows_out():
                dve.wait_ge(s_sp, 7)
                cp(mix_t[0:N_SAMPLE, 0:ATT].rearrange("p (k c d) -> p c k d", k=NKV, c=QPK),
                   psS[0:N_SAMPLE, 512:1024].rearrange("p (c k d) -> p c k d", k=NKV, c=QPK)).then_inc(s_sv, 1)

            def split_out(n):
                dve.wait_ge(s_whi, N_WI + n + 1)
                dve.wait_ge(s_wo[n], 16)
                tt(wo_lo[:, 2 * n:2 * n + 2, :], wo_raw(n), wo_hi[:, 2 * n:2 * n + 2, :].bitcast(F32), ALU.subtract)\
                    .then_inc(s_wlo, 1)

            def m_lo(t, b):
                for k in range(2):
                    dve.wait_ge(s_mh, 2 * t + k + 1)
                    dst = slice(4 * k, 4 * k + 4)
                    tt(mT_lo[b][:, dst, :].rearrange("p c t -> p (c t)"), psT[k][:],
                       mT_hi[b][:, dst, :].rearrange("p c t -> p (c t)").bitcast(F32), ALU.subtract).then_inc(s_mlo, 1)

            def residual(t, b, h):
                if h == 0:
                    dve.wait_ge(s_xr[b], (t - b + 2) * 8)
                dve.wait_ge(s_op, 2 * t + h + 1)
                part = x1(t)[:, h * 512:(h + 1) * 512]
                tt(part, part, psZ[h][:], ALU.add).then_inc(s_x1, 1)

            def h_rows(t):
                dve.wait_ge(s_r2, t + 1)
                dve.wait_ge(s_x1, 2 * t + 2)
                if not (isinstance(t, int) and t == 0):
                    dve.wait_ge(s_hst, 16 * t)
                    dve.wait_ge(s_hTp, t)
                stt(out=h_t[:].rearrange("p (c q) -> p q c", c=DC), in0=x1(t).rearrange("p (q c) -> p q c", c=DC),
                    scalar=small[:, 10:11], in1=ffg[:].rearrange("p (q c) -> p q c", c=DC), op0=ALU.mult, op1=ALU.mult)\
                    .then_inc(s_h, 1)

            def h_out(t):
                dve.wait_ge(s_hTp, t + 1)
                if not (isinstance(t, int) and t == 0):
                    dve.wait_ge(s_lg, t)
                cp(hT[:, 4:8, :].rearrange("p c t -> p (c t)"), psS[:, 512:1024]).then_inc(s_hTv, 1)

            def logits_out(t):
                dve.wait_ge(s_lg, t + 1)
                dst = logits[:, t, :] if isinstance(t, int) else logits[:, bass.ds(t, 1), :].squeeze(1)
                tt(dst, psG[:, 0:NGRP + NE], b_rt[:], ALU.add).then_inc(s_lgo, 1)

            def stage2(t, b):
                first = isinstance(t, int) and t == 0
                if not (isinstance(t, int) and t == T_P):
                    m_lo(t + 1, 1 - b)
                if not first:
                    h_out(t - 1)
                residual(t, b, 0)
                if first:
                    sample_weights_out()
                    sample_gmlp()
                residual(t, b, 1)
                if first:
                    sample_values_out()
                    sample_rows_out()
                    dve.wait_ge(s_p2, 64)
                    dve.wait_ge(s_kvout, 5 * 16)
                else:
                    logits_out(t - 1)
                h_rows(t)

            sample_products()
            split_out(0)
            sample_cache_scores()
            m_lo(0, 0)
            split_out(1)
            sample_maxima()
            split_out(2)
            split_out(3)
            sample_weights()
            stage2(0, 0)
            with dve.Fori(1, T_P - 2, 2) as t:
                stage2(t, 1)
                stage2(t + 1, 0)
            stage2(T_P - 1, 1)
            stage2(T_P, 0)
            h_out(T_P)
            logits_out(T_P)

            dve.wait_ge(s_lgo, T)
            dve.wait_ge(s_op, 2 * T)
            red = nc.vector.tensor_reduce
            lg = logits[:, :, 0:NGRP]
            gmax, gsum, gidx = c9[0], c9[1], c9[2]
            b9 = lambda a, n: a[:, 0:T].unsqueeze(2).to_broadcast([P, T, n])
            io = lambda n: cst[:, C_IO:C_IO + n].unsqueeze(1).to_broadcast([P, T, n])
            step(red(gmax[:], lg, AX, ALU.max))
            tt(g8[0][:, :, 0:4], lg, b9(gmax, 4), ALU.subtract).then_inc(s_ra, 1)
            step(tt(g8[1][:, :, 0:4], lg, b9(gmax, 4), ALU.is_equal))

            def first_of(eq, n, tmp, idx, onehot):
                step(stt(out=tmp, in0=eq, scalar=-64.0, in1=io(n), op0=ALU.mult, op1=ALU.add))
                step(red(idx[:], tmp, AX, ALU.min))
                step(ts(idx[:], idx[:], 64.0, None, ALU.add))
                step(tt(onehot, io(n), b9(idx, n), ALU.is_equal))

            first_of(g8[1][:, :, 0:4], 4, g8[1][:, :, 0:4], gidx, g8[1][:, :, 0:4])
            le = logits[:, :, NGRP:].rearrange("p t (g e) -> p t g e", g=NGRP)
            for g in range(NGRP):
                o = g8[1][:, :, g:g + 1].to_broadcast([P, T, EPG])
                dst = tmp_e[:, :, g * EPG:(g + 1) * EPG]
                last = tt(dst, le[:, :, g, :], o, ALU.mult)
            step(last)
            esel, e2 = g8[2], g8[3]
            step(red(esel[:], tmp_e[:].rearrange("p t (g e) -> p t e g", g=NGRP), AX, ALU.add))
            m1, m2, i1, i2 = c9[3], c9[4], c9[5], c9[7]
            step(red(m1[:], esel[:], AX, ALU.max))
            step(tt(g8[4][:], esel[:], b9(m1, 8), ALU.is_equal))
            first_of(g8[4][:], 8, g8[4][:], i1, g8[5][:])
            step(stt(out=e2[:], in0=g8[5][:], scalar=NEG, in1=esel[:], op0=ALU.mult, op1=ALU.add))
            step(red(m2[:], e2[:], AX, ALU.max))
            step(tt(g8[4][:], e2[:], b9(m2, 8), ALU.is_equal))
            first_of(g8[4][:], 8, g8[4][:], i2, g8[5][:])
            tt(c9[6][:], m2[:], m1[:], ALU.subtract).then_inc(s_ra, 1)
            step(stt(out=gidx[:], in0=gidx[:], scalar=float(EPG), in1=cst[:, C_INV:C_INV + T], op0=ALU.mult, op1=ALU.add))
            tt(i1[:], gidx[:], i1[:], ALU.add)
            step(tt(i2[:], gidx[:], i2[:], ALU.add))
            tt(one_e[:, 0], io(NE), b9(i1, NE), ALU.is_equal)
            step(tt(one_e[:, 1], io(NE), b9(i2, NE), ALU.is_equal))
            cp(tr_bf[:], cst[:, C_TR:C_TR + P])
            nc.vector.memset(on_bf[:], 1.0)
            tt(m_bf[:], one_e[:, 0], one_e[:, 1], ALU.add).then_inc(s_rv, 1)
            for k in range(2):
                ts(rhs_t[:, k, :, 0:NE], one_e[:, k], cst[:, C_PR:C_PR + 1], None, ALU.mult)
                tt(rhs_t[:, k, :, NE:2 * NE], one_e[:, k],
                   cst[:, C_TILE:C_TILE + T].unsqueeze(2).to_broadcast([P, T, NE]), ALU.mult)
                ts(rhs_t[:, k, :, 2 * NE:3 * NE], one_e[:, k], float(k + 1), None, ALU.mult)
            dve.wait_ge(s_rp, 1)
            cp(rank_s[:].rearrange("p t e -> p (t e)"), psZ[0][:, 0:T * NE])
            step(red(c9[9][:, 0:1], psZ[1][:, 0:NE], AX, ALU.max))
            cp(cnt_i[:], c9[9][:, 0:1])
            for k in range(2):
                step(tt(tmp_e[:], one_e[:, k], rank_s[:], ALU.mult))
                step(red(rk[:, k, :], tmp_e[:], AX, ALU.add))

            def one_hots(done):
                for k in range(2):
                    last = tt(oh_r[:, k], io(P), b9(rk[:, k, :], P), ALU.is_equal)
                last.then_inc(done, 1)

            def table_out(link, done):
                link(cp(tab[:], psG[:, 0:3 * NE]))
                a, b, c = tab[:, 0:NE], tab[:, NE:2 * NE], tab[:, 2 * NE:3 * NE]
                ts(tab2[:, 0, :], c, 0.0, OOB, ALU.is_equal, ALU.mult)
                link(stt(out=tab2[:, 1, :], in0=b, scalar=float(P), in1=a, op0=ALU.mult, op1=ALU.add))
                link(stt(out=tab2[:, 2, :], in0=tab2[:, 1, :], scalar=2.0, in1=c, op0=ALU.mult, op1=ALU.add))
                tt(idx_src[:], tab2[:, 1, :], tab2[:, 0, :], ALU.add)
                link(stt(out=tab2[:, 2, :], in0=tab2[:, 2, :], scalar=-1.0, in1=tab2[:, 0, :], op0=ALU.add, op1=ALU.add))
                cp(idx_dst[:], tab2[:, 2, :]).then_inc(done, 1)

            one_hots(s_rv)
            dve.wait_ge(s_sa, 2)
            step(red(gsum[:], g8[0][:, :, 0:4], AX, ALU.add))
            dve.wait_ge(s_sa, 3)
            step(ts(c9[8][:], c9[6][:], 1.0, None, ALU.add))
            step(tt(c9[8][:], c9[8][:], gsum[:], ALU.mult))
            step(nc.vector.reciprocal(w_of[:, 0, :], c9[8][:]))
            step(tt(w_of[:, 1, :], w_of[:, 0, :], c9[6][:], ALU.mult))
            dve.wait_ge(s_rp, 2)
            table_out(step, s_idx)
            dve.wait_ge(s_idx, 1)


            def col(ap, e):
                return ap[:, e:e + 1] if isinstance(e, int) else ap[:, bass.ds(e, 1)]

            def src_rows(e, k):
                if not (isinstance(e, int) and e < 4):
                    dve.wait_ge(s_ga[k], (e - k) * 4)
                cp(ic_src[:, k:k + 1], col(idx_src, e)).then_inc(s_isrc, 1)

            def dst_rows(e, k):
                if not (isinstance(e, int) and e < 4):
                    dve.wait_ge(s_sc4[k % 2], (e - k % 2 - 2) * 8)
                cp(ic_dst[:, k:k + 1], col(idx_dst, e)).then_inc(s_idst, 1)

            def into_hid(u):
                halves = lambda a: a.rearrange("p (q c) -> p q c", c=2)
                return tt(hid[:].rearrange("p (c q) -> p q c", c=2), halves(sg[:]), halves(u), ALU.mult)

            def g_out(e):
                dve.wait_ge(s_gTp, 2 * e + 2)
                if not (isinstance(e, int) and e == 0):
                    dve.wait_ge(s_gu, e)
                cp(xgT[:, 4:8, :].rearrange("p c t -> p (c t)"), psT[1][:]).then_inc(s_gTv, 1)

            def y_out(e, b):
                dve.wait_ge(s_dn, e + 1)
                if not (isinstance(e, int) and e < 2):
                    dve.wait_ge(s_sc4[b], (e - b) * 8)
                cp(y_t[b][:, 512:D], psS[:, 512:D]).then_inc(s_yv, 1)

            def stage4(e, k):
                b = k % 2
                dve.wait_ge(s_sg, e + 1)
                if not (isinstance(e, int) and e == 0):
                    dve.wait_ge(s_dTp, e)
                into_hid(psZ[b][:, FE:2 * FE]).then_inc(s_hid, 1)
                if not (isinstance(e, int) and e == NE - 1):
                    g_out(e + 1)
                if not (isinstance(e, int) and e == 0):
                    y_out(e - 1, 1 - b)
                if not (isinstance(e, int) and e >= NE - 4):
                    src_rows(e + 4, k)
                if not (isinstance(e, int) and e == NE - 1):
                    dst_rows(e + 1, (k + 1) % 4)

            for k in range(4):
                src_rows(k, k)
            dst_rows(0, 0)
            g_out(0)
            for k in range(4):
                stage4(k, k)
            with dve.Fori(4, NE - 7, 4) as e:
                for k in range(4):
                    stage4(e + k, k)
            for k in range(4):
                stage4(NE - 4 + k, k)
            y_out(NE - 1, 1)

            most = dve.value_load(cnt_i[0:1, 0:1], min_val=0, max_val=N_TOK)
            with dve.If(most > SLOTS):
                link = Chain(dve, o_step)
                with dve.Fori(0, N_CHUNK - 1) as m:
                    link.n = m * OV_LINKS
                    flat = rk[:].rearrange("p k t -> p (k t)")
                    link(ts(flat, flat, -float(SLOTS), None, ALU.add))
                    one_hots(o_oh)
                    dve.wait_ge(o_tab, m + 1)
                    table_out(link, o_idx)
                    dve.wait_ge(o_idx, m + 1)
                    settle(dve)
                    with dve.Fori(0, NE) as e:
                        n = m * NE + e
                        dve.wait_ge(o_free, n + 1)
                        cp(ic_src[:, 0:1], idx_src[:, bass.ds(e, 1)])
                        cp(ic_dst[:, 0:1], idx_dst[:, bass.ds(e, 1)]).then_inc(o_ic, 1)
                        dve.wait_ge(o_gTp, 2 * n + 2)
                        cp(xgT[:, 4:8, :].rearrange("p c t -> p (c t)"), psT[1][:]).then_inc(o_gTv, 1)
                        dve.wait_ge(o_sg, n + 1)
                        into_hid(psZ[0][:, FE:2 * FE]).then_inc(o_hid, 1)
                        dve.wait_ge(o_dn, n + 1)
                        cp(y_t[0][:, 512:D], psS[:, 512:D]).then_inc(o_y, 1)
            dve.wait_ge(o_done, 1)

            dve.wait_ge(s_fg, 16)

            def sum_rows(t):
                n = N_SAMPLE if t == T_P else P
                dve.wait_ge(s_yy[t % 4], (t // 4 + 1) * 16)
                step(stt(out=x1(t)[0:n], in0=yy[t % 4][0:n, 0, :], scalar=w_of[0:n, 0, t:t + 1], in1=x1(t)[0:n],
                         op0=ALU.mult, op1=ALU.add))
                stt(out=x1(t)[0:n], in0=yy[t % 4][0:n, 1, :], scalar=w_of[0:n, 1, t:t + 1], in1=x1(t)[0:n],
                    op0=ALU.mult, op1=ALU.add).then_inc(s_ysum, 1)

            def scale_rows(t):
                n = N_SAMPLE if t == T_P else P
                dve.wait_ge(s_fr, t + 1)
                dve.wait_ge(s_ysum, t + 1)
                stt(out=x1(t)[0:n], in0=x1(t)[0:n], scalar=fst[0:n, t % 2, 2:3], in1=fing[0:n], op0=ALU.mult,
                    op1=ALU.mult).then_inc(s_fo, 1)

            for t in range(T):
                sum_rows(t)
                if t > 0:
                    scale_rows(t - 1)
            scale_rows(T_P)

        @block.gpsimd
        def _(pool):
            link = Chain(pool, pool_step)
            ptt = nc.gpsimd.tensor_tensor
            nc.gpsimd.memset(small[:, 1:2], -0.5)
            nc.gpsimd.memset(small[:, 2:3], 1.0 / D)
            link(nc.gpsimd.memset(small[:, 3:4], EPS))

            def rsqrt(out, src, tmp, done, n=P, mean=True):
                if mean:
                    link(ptt(tmp, src, small[0:n, 2:3], ALU.mult))
                link(ptt(tmp, tmp if mean else src, small[0:n, 3:4], ALU.add))
                ptt(out, tmp, small[0:n, 1:2], ALU.pow).then_inc(done, 1)

            def row_scale(t):
                pool.wait_ge(s_sq, t + 1)
                rsqrt(st[:, 2:3], st[:, 0:1], st[:, 1:2], s_rstd)

            def ln_scale(t):
                pool.wait_ge(s_var, t + 1)
                rsqrt(st[:, 6:7], st[:, 4:5], st[:, 5:6], s_lnr, mean=False)

            row_scale(0)
            pool.wait_ge(s_ws, 16)
            nc.gpsimd.affine_select(out=ws_raw[:], in_=ws_raw[:], compare_op=ALU.is_ge, fill=0.0, base=0,
                                    pattern=[[0, NG], [-1, P]], channel_multiplier=1).then_inc(s_wmask, 1)
            n1 = link.n
            with pool.Fori(0, T_P) as t:
                link.n = 3 * t + n1
                row_scale(t + 1)
                ln_scale(t)
            link.n = n1 + 3 * T_P
            ln_scale(T_P)

            def h_scale(t):
                pool.wait_ge(s_sq2, t + 1)
                if not (isinstance(t, int) and t == 0):
                    pool.wait_ge(s_h, t)
                rsqrt(small[:, 10:11], small[:, 8:9], small[:, 9:10], s_r2)

            h_scale(0)
            n2 = link.n
            with pool.Fori(1, T) as t:
                link.n = 2 * t - 2 + n2
                h_scale(t)
            link.n = n2 + 2 * T_P

            def gather(k, done):
                nc.gpsimd.indirect_dma_start(xg[k][:], None, h_d, bass.IndirectOffsetOnAxis(ic_src[:, k:k + 1].bitcast(U32), 0),
                                             bounds_check=T * P - 1, oob_is_err=False).then_inc(done, 16)

            def scatter(k, b, done):
                nc.gpsimd.indirect_dma_start(y_d, bass.IndirectOffsetOnAxis(ic_dst[:, k:k + 1].bitcast(U32), 0), y_t[b][:], None,
                                             bounds_check=2 * T * P - 1, oob_is_err=False).then_inc(done, 16)

            def gather4(e, k):
                pool.wait_ge(s_isrc, e + 1)
                if not (isinstance(e, int) and e < 4):
                    pool.wait_ge(s_gTp, 2 * e - 6)
                settle(pool)
                gather(k, s_ga[k])

            def stage4(e, k):
                if not (isinstance(e, int) and e >= NE - 4):
                    gather4(e + 4, k)
                pool.wait_ge(s_idst, e + 1)
                pool.wait_ge(s_ya, e + 1)
                pool.wait_ge(s_yv, e + 1)
                settle(pool)
                scatter(k, k % 2, s_sc4[k % 2])

            pool.wait_ge(s_mTp, 2 * T)
            pool.wait_ge(s_op, 2 * T)
            for k in range(4):
                last = nc.gpsimd.memset(xg[k][:], 0.0)
            last.then_inc(s_zx, 1)
            pool.wait_ge(s_hst, 16 * T)
            pool.wait_ge(s_zx, 1)
            for k in range(4):
                gather4(k, k)
            for k in range(4):
                stage4(k, k)
            with pool.Fori(4, NE - 7, 4) as e:
                for k in range(4):
                    stage4(e + k, k)
            for k in range(4):
                stage4(NE - 4 + k, k)
            for b in range(2):
                pool.wait_ge(s_sc4[b], NE // 2 * 16)

            most = pool.value_load(cnt_i[0:1, 0:1], min_val=0, max_val=N_TOK)
            with pool.If(most > SLOTS):
                with pool.Fori(0, (N_CHUNK - 1) * NE) as n:
                    pool.sem_inc(o_free, 1)
                    pool.wait_ge(o_ic, n + 1)
                    settle(pool)
                    gather(0, o_ga)
                    pool.wait_ge(o_ya, n + 1)
                    pool.wait_ge(o_y, n + 1)
                    settle(pool)
                    scatter(0, 0, o_sc)
                    pool.wait_ge(o_sc, 16 * n + 16)
            pool.sem_inc(o_done, 1)

            def final_scale(t, b, n=P):
                pool.wait_ge(s_fsq, t + 1)
                if not (isinstance(t, int) and t < 2):
                    pool.wait_ge(s_fo, t - 1)
                rsqrt(fst[0:n, b, 2:3], fst[0:n, b, 0:1], fst[0:n, b, 1:2], s_fr, n)

            final_scale(0, 0)
            final_scale(1, 1)
            n6 = link.n
            with pool.Fori(2, T_P - 1, 2) as t:
                link.n = 2 * t - 4 + n6
                final_scale(t, 0)
                final_scale(t + 1, 1)
            link.n = n6 + 2 * T_P - 4
            final_scale(T_P, 0, N_SAMPLE)


def shape_constants():
    import numpy as np
    c = np.zeros((P, C_END), np.float32)
    r = np.arange(P)
    c[:, C_ID:C_ID + P] = np.eye(P)
    causal = np.where(r[None, :] <= r[:, None], 0.0, NEG)
    c[:, C_MF:C_MF + P] = NEG
    c[:, C_MF + P:C_MF + 2 * P] = causal
    c[:, C_MR:C_MR + P] = np.where(r[None, :] >= r[:, None], 0.0, NEG)
    c[:, C_MR + P:C_MR + 2 * P] = causal
    c[:, C_IO:C_IO + P] = r[None, :]
    c[:, C_TR:C_TR + P] = r[:, None] < r[None, :]
    c[:, C_PR] = r
    q = np.arange(64)
    c[q, C_SEL + (q % 32) // QPK] = 1.0
    c[N_SAMPLE:, C_INV + T_P] = 1000.0
    c[:, C_TILE:C_TILE + T] = np.arange(T)[None, :]
    inv_freq = (10000.0 ** (-np.arange(HD // 2) * 2.0 / HD)).astype(np.float32)
    for t in range(T):
        pos = (t * P + r if t < T_P else np.full(P, PAST)).astype(np.float32)
        angle = (pos[:, None] * inv_freq[None, :]).astype(np.float64)
        c[:, C_CS + t * HD:C_CS + t * HD + 32] = np.cos(angle)
        c[:, C_CS + t * HD + 32:C_CS + (t + 1) * HD] = np.sin(angle)
    return c


def kernel(**inputs):
    import numpy as np
    import concourse.bacc as bacc
    from concourse.bass_utils import run_bass_kernel_spmd

    a = {k: np.asarray(v) for k, v in inputs.items()}
    x_rows = np.zeros((T * P, D), a["x_prompt"].dtype)
    x_rows[:N_PROMPT] = a["x_prompt"].reshape(N_PROMPT, D)
    x_rows[N_PROMPT:N_TOK] = a["x_sample"].reshape(N_SAMPLE, D)
    sinks = a["attn_sinks"].reshape(NKV, 1, QPK)
    arrays = dict(
        x_rows=x_rows,
        cache_k=a["cache_swa_k"].reshape(N_SAMPLE, WIN, P),
        cache_v=a["cache_swa_v"].reshape(N_SAMPLE, WIN, P),
        mix_g=np.ascontiguousarray(a["norm_mix_g"].reshape(DC, P).T),
        w_in=a["w_in"].reshape(D, Z_COLS),
        sinks_b=a["attn_sinks"].reshape(1, NQ),
        sink_rows=np.ascontiguousarray(np.broadcast_to(sinks, (NKV, N_SAMPLE, QPK)).reshape(64, 1)),
        ln_g=a["gmlp_ln_g"].reshape(1, GW),
        ln_b=a["gmlp_ln_b"].reshape(1, GW),
        w_s=a["gmlp_w_s"].reshape(NG, P, P),
        b_sT=np.ascontiguousarray(a["gmlp_b_s"].reshape(NG, P).T),
        b_s=a["gmlp_b_s"].reshape(NG, P),
        w_out=a["w_out"].reshape(D, D),
        ffn_g=a["norm_ffn_g"].reshape(1, D),
        w_rg=a["router_group_w"].reshape(D, NGRP),
        b_r=np.concatenate([a["router_group_b"].reshape(1, NGRP), a["router_expert_b"].reshape(1, NE)], axis=1),
        w_re=a["router_expert_w"].reshape(D, NE),
        w_gate=a["expert_w_gate"].reshape(NE, D, FE),
        w_up=a["expert_w_up"].reshape(NE, D, FE),
        w_down=a["expert_w_down"].reshape(NE, FE, D),
        fin_g=a["final_norm_g"].reshape(1, D),
        consts=shape_constants(),
    )
    outs = dict(y_rows=(N_TOK, D), k_prompt=(P, P), v_prompt=(P, P), k_sample=(N_SAMPLE, P), v_sample=(N_SAMPLE, P),
                g_sample=(N_SAMPLE, GW))
    nc = bacc.Bacc("TRN2", target_bir_lowering=False, num_devices=1)
    aps = {n: nc.dram_tensor(n, v.shape, mybir.dt.from_np(v.dtype), kind="ExternalInput").ap() for n, v in arrays.items()}
    aps |= {n: nc.dram_tensor(n, s, F32, kind="ExternalOutput").ap() for n, s in outs.items()}
    build(nc, **aps)
    r = run_bass_kernel_spmd(nc, [arrays], core_ids=[0]).results[0]
    y = r["y_rows"]
    return (y[:N_PROMPT].reshape(1, N_PROMPT, D), y[N_PROMPT:].reshape(N_SAMPLE, 1, D),
            r["k_prompt"].reshape(1, 1, WIN, NKV, HD), r["v_prompt"].reshape(1, 1, WIN, NKV, HD),
            r["k_sample"].reshape(1, N_SAMPLE, 1, NKV, HD), r["v_sample"].reshape(1, N_SAMPLE, 1, NKV, HD),
            r["g_sample"].reshape(1, N_SAMPLE, 1, GW))
```

```python
from contextlib import ExitStack

import concourse.bass as bass
from concourse import mybir

F32 = mybir.dt.float32
F32R = mybir.dt.float32r
BF16 = mybir.dt.bfloat16
I32 = mybir.dt.int32
U32 = mybir.dt.uint32
ALU = mybir.AluOpType
ACT = mybir.ActivationFunctionType
AX = mybir.AxisListType.X

P = 128
D = 1024
DC = D // P
N_PROMPT = 1024
N_SAMPLE = 8
N_TOK = N_PROMPT + N_SAMPLE
T_P = N_PROMPT // P
T = T_P + 1
HD = 64
NQ = 8
NKV = 2
QPK = NQ // NKV
ATT = NQ * HD
GW = 512
NG = 8
Z_COLS = 1792
WIN = 128
NGRP = 4
EPG = 8
NE = 32
FE = 256
EPS = 1e-6
SCALE = HD ** -0.5
NEG = -1e30
SLOTS = 128
PAST = 8192
OV_LINKS = 5
N_CHUNK = -(-N_TOK // SLOTS)
OOB = 100000.0
Z_GROUPS = [(0, 512), (512, 256), (768, 512), (1280, 512)]
WI_COLS = [(0, 768), (768, 1792)]
N_WI = 2 * DC // 2
N_WO = 4
WO_STAGED = 2

C_ID = 0
C_MF = C_ID + P
C_MR = C_MF + 2 * P
C_IO = C_MR + 2 * P
C_TR = C_IO + P
C_PR = C_TR + P
C_SEL = C_PR + 1
C_INV = C_SEL + N_SAMPLE
C_TILE = C_INV + T
C_CS = C_TILE + T
C_END = C_CS + T * HD


class Region:

    def __init__(self, nc, base, start, end):
        self.nc, self.base, self.at, self.end = nc, base, start, end

    def take(self, name, shape, dt):
        n = 1
        for s in shape[1:]:
            n *= s
        size = -(-n * (2 if dt == BF16 else 4) // 32) * 32
        got = self.nc.alloc_sbuf_tensor_at(name, shape, dt, offset=self.base + self.at)
        self.at += size
        assert self.at <= self.end, (name, self.at, self.end)
        return got


class Chain:

    def __init__(self, eng, sem):
        self.eng, self.sem, self.n = eng, sem, 0

    def __call__(self, ins):
        ins.then_inc(self.sem, 1)
        self.n = self.n + 1
        self.eng.wait_ge(self.sem, self.n)


def build(nc, x_rows, cache_k, cache_v, mix_g, w_in, sinks_b, sink_rows, ln_g, ln_b, w_s, b_sT, b_s, w_out, ffn_g,
          w_rg, b_r, w_re, w_gate, w_up, w_down, fin_g, consts,
          y_rows, k_prompt, v_prompt, k_sample, v_sample, g_sample):
    mix_d = nc.dram_tensor("mix_d", [T * P, D], F32).ap()
    h_d = nc.dram_tensor("h_d", [T * P, D], F32).ap()
    y_d = nc.dram_tensor("y_d", [2 * T * P, D], F32).ap()

    ctx = ExitStack()
    with ctx:
        def bank(name, n=1):
            return ctx.enter_context(nc.psum_tensor(name, [P, n * 512], F32))

        def sem(name):
            return ctx.enter_context(nc.semaphore(name))

        psT = [bank("psT0"), bank("psT1")]
        psZ = [bank("psZ0"), bank("psZ1")]
        psS = bank("psS", 2)
        psO = bank("psO")
        psG = bank("psG")

        base = 16512
        r1 = Region(nc, base, 0, 114688)
        r2 = Region(nc, base, 114688, 147456)
        r3 = Region(nc, base, 147456, 212800)
        cst = r3.take("cst", [P, C_END], F32)
        w_of = r3.take("w_of", [P, 2, T], F32)
        small = r3.take("small", [P, 64], F32)
        wi_hi = r1.take("wi_hi", [P, DC, Z_COLS], F32R)
        wi_lo = r1.take("wi_lo", [P, DC, Z_COLS], F32R)
        wi_raw = Region(nc, base, r1.at - 4 * DC * Z_COLS, r1.at).take("wi_raw", [P, DC, Z_COLS], F32)
        wo_stage = [r2.take(f"wo_stage{n}", [P, 2 * D], F32) for n in range(WO_STAGED)]
        x_t = r2.take("x_t", [P, D], F32)
        q_ro = r2.take("q_ro", [P, ATT], F32)
        qT = r2.take("qT", [P, QPK, P], F32)
        a1 = r3.at
        mix_t = r3.take("mix_t", [P, D], F32)
        xT_hi = r3.take("xT_hi", [P, DC, P], F32R)
        xT_lo = r3.take("xT_lo", [P, DC, P], F32R)
        k_ro = r3.take("k_ro", [P, P], F32)
        kT = r3.take("kT", [P, 2 * P], F32)
        v_t = r3.take("v_t", [P, 2, P], F32)
        v_new = r3.take("v_new", [P, P], F32)
        u_t = r3.take("u_t", [P, GW], F32)
        vg_t = r3.take("vg_t", [P, GW], F32)
        vn_t = r3.take("vn_t", [P, GW], F32)
        s_at = r3.at
        s_t = [r3.take(f"s_t{g}", [P, QPK, 2 * P], F32) for g in range(2)]
        s_end = r3.at
        r_tmp = Region(nc, base, s_at, s_end)
        ws_raw = r_tmp.take("ws_raw", [P, NG, P], F32)
        kc_t = r_tmp.take("kc_t", [P, N_SAMPLE, P], F32)
        pT = r3.take("pT", [P, 2 * QPK, P], F32)
        lng = r3.take("lng", [P, GW], F32)
        lnb = r3.take("lnb", [P, GW], F32)
        wsT = r3.take("wsT", [P, NG, P], F32)
        rope_a = r3.take("rope_a", [P, ATT], F32)
        rope_b = r3.take("rope_b", [P, ATT], F32)
        junk = r3.take("junk", [P, D], BF16)
        kcT = r3.take("kcT", [P, N_SAMPLE, P], F32)
        csr = r3.take("csr", [P, HD], F32)
        sink_t = r3.take("sink_t", [P, NQ], F32)
        bsT = r3.take("bsT", [P, NG], F32)
        gmix = r3.take("gmix", [P, DC], F32)
        st = r3.take("st", [P, 64], F32)
        sinkr = r3.take("sinkr", [P, 1], F32)
        w00 = r3.take("w00", [P, NG], F32)
        b00 = r3.take("b00", [P, NG], F32)
        r_s = Region(nc, base, r2.at, 147456)
        vc_t = r_s.take("vc_t", [P, N_SAMPLE, P], F32)
        sT_s = r_s.take("sT_s", [P, NKV, 32], F32)
        prod = r_s.take("prod", [P, 64], F32)
        s_s = r_s.take("s_s", [64, 132], F32)
        pT_s = r_s.take("pT_s", [P, 64], F32)
        selp = r_s.take("selp", [64, N_SAMPLE], F32)
        d_s = r_s.take("d_s", [N_SAMPLE, 64], F32)
        oT_s = r_s.take("oT_s", [P, N_SAMPLE, QPK], F32)
        q1 = Region(nc, base, 0, 114688)
        wo_hi = q1.take("wo_hi", [P, DC, D], F32R)
        wo_lo = q1.take("wo_lo", [P, DC, D], F32R)
        wo_in = Region(nc, base, q1.at - 4 * DC * D, q1.at).take("wo_in", [P, DC, D], F32)
        x1a = Region(nc, base, 114688, 147456).take("x1a", [P, T_P, D], F32)
        s2 = Region(nc, base, a1, 212800)
        x1b = s2.take("x1b", [P, D], F32)
        at4 = s2.at
        m_t = [s2.take(f"m_t{b}", [P, D], F32) for b in range(2)]
        h_t = s2.take("h_t", [P, D], F32)
        hT = s2.take("hT", [P, DC, P], F32)
        at4_end = s2.at = s_at
        mT_hi = []
        mT_lo = []
        for b in range(2):
            mT_hi.append(s2.take(f"mT_hi{b}", [P, DC, P], F32R))
            mT_lo.append(s2.take(f"mT_lo{b}", [P, DC, P], F32R))
        at3, at3_end = s_at, s2.at
        ffg = s2.take("ffg", [P, D], F32)
        junk2 = s2.take("junk2", [P, D], BF16)
        w_r = s2.take("w_r", [P, DC, NGRP + NE], F32)
        b_rt = s2.take("b_rt", [P, NGRP + NE], F32)
        logits = s2.take("logits", [P, T, NGRP + NE], F32)
        s3 = Region(nc, base, s2.at, 212800)
        idx_src = s3.take("idx_src", [P, NE], I32)
        idx_dst = s3.take("idx_dst", [P, NE], I32)
        rk = s3.take("rk", [P, 2, T], F32)
        rhs_t = s3.take("rhs_t", [P, 2, T, 3 * NE], BF16)
        s3b = Region(nc, base, at3 + 8 * D, at3_end)
        one_e = s3b.take("one_e", [P, 2, T, NE], F32)
        m_bf = s3b.take("m_bf", [P, T, NE], BF16)
        rank_s = s3b.take("rank_s", [P, T, NE], F32)
        tmp_e = s3b.take("tmp_e", [P, T, NE], F32)
        g8 = [s3b.take(f"g8_{n}", [P, T, EPG], F32) for n in range(6)]
        c9 = [s3b.take(f"c9_{n}", [P, T], F32) for n in range(10)]
        tab = s3b.take("tab", [P, 3 * NE], F32)
        s3c = Region(nc, base, at3, at3 + 8 * D)
        oh_r = s3c.take("oh_r", [P, 2, T, P], BF16)
        tr_bf = s3c.take("tr_bf", [P, P], BF16)
        on_bf = s3c.take("on_bf", [P, P], BF16)
        tab2 = s3c.take("tab2", [P, 3, NE], F32)
        tmp_r = s3c.take("tmp_r", [P, 2, T, NE], F32)
        cnt_i = s3c.take("cnt_i", [P, 1], I32)
        wg = []
        wd = []
        wd_lo = []
        wd_hi = Region(nc, base, 57344, 65536).take("wd_hi", [P, 2, D], F32R)
        for n, at in enumerate([65536, 90112, 0, 24576]):
            e = Region(nc, base, at, at + 24576)
            wg.append(e.take(f"wg{n}", [P, 2, DC, FE], F32))
            wd.append(e.take(f"wd{n}", [P, 2, D], F32))
            wd_lo.append(Region(nc, base, e.at - 8 * D, e.at).take(f"wd_lo{n}", [P, 2, D], F32R))
        s4 = Region(nc, base, at4, at4_end)
        xg = [s4.take(f"xg{b}", [P, D], F32) for b in range(2)]
        xg += [Region(nc, base, at, at + 4 * D).take(f"xg{2 + n}", [P, D], F32) for n, at in enumerate([49152, 53248])]
        y_t = [s4.take(f"y_t{b}", [P, D], F32) for b in range(2)]
        y_t += [s3.take(f"y_t{b}", [P, D], F32) for b in (2, 3)]
        sg = s4.take("sg", [P, FE], F32)
        s4b = Region(nc, base, at3 + 8 * D, at3_end)
        hid = s4b.take("hid", [P, FE], F32)
        hidT_hi = s4b.take("hidT_hi", [P, 2, P], F32R)
        ic_src = s4b.take("ic_src", [P, 4], I32)
        ic_dst = s4b.take("ic_dst", [P, 4], I32)
        s4c = Region(nc, base, at3_end, at3_end + 4 * D + 2 * D)
        xgT = s4c.take("xgT", [P, DC, P], F32)
        hidT_lo = s4c.take("hidT_lo", [P, 2, P], F32R)
        hidT = Region(nc, base, s4c.at - 4 * 2 * P, s4c.at).take("hidT", [P, 2, P], F32)
        s6 = Region(nc, base, 90112, 114688)
        fing = s6.take("fing", [P, D], F32)
        junk3 = s6.take("junk3", [P, D], BF16)
        fst = s6.take("fst", [P, 2, 4], F32)
        s6y = Region(nc, base, 0, 57344)
        yy = [s6y.take(f"yy{b}", [P, 2, D], F32) for b in range(4)]

        ident = cst[:, C_ID:C_ID + P]

        def x1(t):
            if isinstance(t, int) and t == T_P:
                return x1b[:]
            return x1a[:, t, :] if isinstance(t, int) else x1a[:, bass.ds(t, 1), :].squeeze(1)

        def rows(ap, t, n=P):
            return ap[t * P:t * P + n, :] if isinstance(t, int) else ap[bass.ds(t * P, n), :]

        s_settled = sem("s_settled")
        s_id = sem("s_id")
        s_cst = sem("s_cst")
        s_msk = sem("s_msk")
        s_small = sem("s_small")
        s_gmix = sem("s_gmix")
        s_ws = sem("s_ws")
        s_kc = sem("s_kc")
        s_vc = sem("s_vc")
        s_wi = [sem(f"s_wi{n}") for n in range(N_WI)]
        s_wo = [sem(f"s_wo{n}") for n in range(N_WO)]
        s_x = sem("s_x")
        s_whi = sem("s_whi")
        s_wlo = sem("s_wlo")
        s_zero = sem("s_zero")
        s_wmask = sem("s_wmask")
        s_tset = sem("s_tset")
        s_eset_a = sem("s_eset_a")
        s_eset_v = sem("s_eset_v")
        s_sq = sem("s_sq")
        s_rstd = sem("s_rstd")
        s_xTp = sem("s_xTp")
        s_xh = sem("s_xh")
        s_xl = sem("s_xl")
        s_z = sem("s_z")
        s_qr = sem("s_qr")
        s_kr = sem("s_kr")
        s_qkTp = sem("s_qkTp")
        s_qT = sem("s_qT")
        s_kT = sem("s_kT")
        s_v = sem("s_v")
        s_vs = sem("s_vs")
        s_u = sem("s_u")
        s_vg = sem("s_vg")
        s_var = sem("s_var")
        s_lnr = sem("s_lnr")
        s_vn = sem("s_vn")
        s_sc = sem("s_sc")
        s_sm = sem("s_sm")
        s_nb = sem("s_nb")
        s_p = sem("s_p")
        s_pTp = sem("s_pTp")
        s_pTa = sem("s_pTa")
        s_pTv = sem("s_pTv")
        s_pv = sem("s_pv")
        s_gm = sem("s_gm")
        s_gmo = sem("s_gmo")
        s_att = sem("s_att")
        s_mix = sem("s_mix")
        s_mix_s = sem("s_mix_s")
        s_kvout = sem("s_kvout")
        dve_step = sem("dve_step")
        act_step = sem("act_step")
        pool_step = sem("pool_step")
        s_sp = sem("s_sp")
        s_sv = sem("s_sv")
        s_sa = sem("s_sa")
        s_ml = [sem(f"s_ml{b}") for b in range(2)]
        s_xr = [sem(f"s_xr{b}") for b in range(2)]
        s_p2 = sem("s_p2")
        s_mTp = sem("s_mTp")
        s_mh = sem("s_mh")
        s_mlo = sem("s_mlo")
        s_op = sem("s_op")
        s_x1 = sem("s_x1")
        s_sq2 = sem("s_sq2")
        s_r2 = sem("s_r2")
        s_h = sem("s_h")
        s_hst = sem("s_hst")
        s_hTp = sem("s_hTp")
        s_hTa = sem("s_hTa")
        s_hTv = sem("s_hTv")
        s_lg = sem("s_lg")
        s_lgo = sem("s_lgo")
        s_rv = sem("s_rv")
        s_ra = sem("s_ra")
        s_rp = sem("s_rp")
        s_idx = sem("s_idx")
        s_wg = [sem(f"s_wg{n}") for n in range(4)]
        s_wd = [sem(f"s_wd{n}") for n in range(4)]
        s_isrc = sem("s_isrc")
        s_idst = sem("s_idst")
        s_ga = [sem(f"s_ga{k}") for k in range(4)]
        s_gTp = sem("s_gTp")
        s_gTa = sem("s_gTa")
        s_gTv = sem("s_gTv")
        s_gu = sem("s_gu")
        s_sg = sem("s_sg")
        s_hid = sem("s_hid")
        s_dTp = sem("s_dTp")
        s_dTh = sem("s_dTh")
        s_dTl = sem("s_dTl")
        s_wdh = sem("s_wdh")
        s_wdl = sem("s_wdl")
        s_dn = sem("s_dn")
        s_ya = sem("s_ya")
        s_yv = sem("s_yv")
        s_sc4 = [sem(f"s_sc4_{k}") for k in range(4)]
        s_zx = sem("s_zx")
        o_idx = sem("o_idx")
        o_step = sem("o_step")
        o_free = sem("o_free")
        o_oh = sem("o_oh")
        o_tab = sem("o_tab")
        o_ic = sem("o_ic")
        o_w = sem("o_w")
        o_ga = sem("o_ga")
        o_gTp = sem("o_gTp")
        o_gTa = sem("o_gTa")
        o_gTv = sem("o_gTv")
        o_gu = sem("o_gu")
        o_sg = sem("o_sg")
        o_hid = sem("o_hid")
        o_dTp = sem("o_dTp")
        o_dT = sem("o_dT")
        o_dn = sem("o_dn")
        o_y = sem("o_y")
        o_ya = sem("o_ya")
        o_sc = sem("o_sc")
        o_done = sem("o_done")
        s_yy = [sem(f"s_yy{b}") for b in range(4)]
        s_fg = sem("s_fg")
        s_ysum = sem("s_ysum")
        s_fsq = sem("s_fsq")
        s_fr = sem("s_fr")
        s_fo = sem("s_fo")
        s_out = sem("s_out")

        block = ctx.enter_context(nc.Block())

        def settle(eng):
            eng.sem_inc(s_settled, 1)

        wo_r = w_out.rearrange("(c p) n -> p c n", p=P)

        def final_tile(i):
            if isinstance(i, int) and i == 0:
                return T_P, N_SAMPLE
            return i - 1, P

        def wi_piece(t, n):
            c0, c1 = WI_COLS[n // 4]
            return t[:, 2 * (n % 4):2 * (n % 4) + 2, c0:c1]

        def wo_raw(n):
            if n < WO_STAGED:
                return wo_stage[n][:].rearrange("p (c n) -> p c n", c=2)
            return wo_in[:, 2 * n:2 * n + 2, :]

        @block.sync
        def _(sp):
            wi_r = w_in.rearrange("(c p) n -> p c n", p=P)

            def load_wi(n):
                sp.dma_start(wi_piece(wi_raw, n), wi_piece(wi_r, n)).then_inc(s_wi[n], 16)

            def load_wo(n):
                sp.dma_start(wo_raw(n), wo_r[:, 2 * n:2 * n + 2, :]).then_inc(s_wo[n], 16)

            sp.dma_start(gmix[:], mix_g).then_inc(s_gmix, 16)
            load_wi(0)
            sp.dma_start(x_t[:], rows(x_rows, 0)).then_inc(s_x, 16)
            sp.dma_start(cst[:, 0:P], consts[:, 0:P]).then_inc(s_id, 16)
            for n in range(1, N_WI):
                load_wi(n)
                if n == 3:
                    sp.dma_start(cst[:, C_TR:], consts[:, C_TR:]).then_inc(s_cst, 16)
            sp.dma_start(cst[:, P:C_TR], consts[:, P:C_TR]).then_inc(s_msk, 16)
            sp.dma_start(ws_raw[:], w_s.rearrange("g t s -> t g s")).then_inc(s_ws, 16)
            sp.dma_start(kc_t[:], cache_k.rearrange("b s n -> s b n")).then_inc(s_kc, 16)
            sp.dma_start(sink_t[:], sinks_b.to_broadcast([P, NQ])).then_inc(s_small, 16)
            sp.dma_start(lng[:], ln_g.to_broadcast([P, GW])).then_inc(s_small, 16)
            sp.dma_start(lnb[:], ln_b.to_broadcast([P, GW])).then_inc(s_small, 16)
            sp.dma_start(bsT[:], b_sT).then_inc(s_small, 16)
            sp.dma_start(sinkr[0:64, :], sink_rows).then_inc(s_small, 16)
            with nc.allow_non_contiguous_dma(reason="eight elements"):
                sp.dma_start(w00[0:N_SAMPLE, :], w_s[:, 0:1, 0:1].rearrange("g a b -> (a b) g")
                             .to_broadcast([N_SAMPLE, NG])).then_inc(s_small, 16)
                sp.dma_start(b00[0:N_SAMPLE, :], b_s[:, 0:1].rearrange("g a -> a g")
                             .to_broadcast([N_SAMPLE, NG])).then_inc(s_small, 16)

            def stage1(t):
                if not (isinstance(t, int) and t == T_P):
                    sp.wait_ge(s_xTp, 2 * t + 2)
                    settle(sp)
                    sp.wait_ge(s_sq, t + 1)
                    sp.dma_start(x_t[:], rows(x_rows, t + 1)).then_inc(s_x, 16)
                if isinstance(t, int) and t == T_P - 1:
                    sp.wait_ge(s_kr, t + 1)
                    sp.dma_start(k_prompt, k_ro[:]).then_inc(s_kvout, 16)
                    sp.wait_ge(s_v, t + 1)
                    sp.dma_start(v_prompt, v_new[:]).then_inc(s_kvout, 16)
                if not (isinstance(t, int) and t == 0):
                    sp.wait_ge(s_att, 2 * t)
                    sp.wait_ge(s_gmo, t)
                    sp.dma_start(rows(mix_d, t - 1), mix_t[:]).then_inc(s_mix, 16)

            stage1(0)
            stage1(1)
            sp.dma_start(vc_t[:], cache_v.rearrange("b s n -> s b n")).then_inc(s_vc, 16)
            for n in range(WO_STAGED):
                load_wo(n)
            with sp.Fori(2, T_P - 1) as t:
                stage1(t)
            stage1(T_P - 1)
            stage1(T_P)
            sp.wait_ge(s_z, 4 * T)
            sp.wait_ge(s_mix, 16)
            sp.dma_start(m_t[0][:], rows(mix_d, 0)).then_inc(s_ml[0], 16)
            for n in range(WO_STAGED, N_WO):
                load_wo(n)
            sp.wait_ge(s_kr, T)
            sp.dma_start(k_sample, k_ro[0:N_SAMPLE, :]).then_inc(s_kvout, 16)
            sp.wait_ge(s_v, T)
            sp.dma_start(v_sample, v_new[0:N_SAMPLE, :]).then_inc(s_kvout, 16)
            sp.wait_ge(s_gm, T_P)
            sp.dma_start(ffg[:], ffn_g.to_broadcast([P, D])).then_inc(s_p2, 16)
            sp.dma_start(w_r[:, :, 0:NGRP], w_rg.rearrange("(p c) n -> p c n", c=DC)).then_inc(s_p2, 16)
            sp.dma_start(w_r[:, :, NGRP:], w_re.rearrange("(p c) n -> p c n", c=DC)).then_inc(s_p2, 16)
            sp.dma_start(b_rt[:], b_r.to_broadcast([P, NGRP + NE])).then_inc(s_p2, 16)
            sp.wait_ge(s_vn, T)
            sp.dma_start(g_sample, vn_t[0:N_SAMPLE, :]).then_inc(s_kvout, 16)
            sp.wait_ge(s_wlo, N_WI + 1)
            sp.dma_start(x1(0), rows(x_rows, 0)).then_inc(s_xr[0], 16)

            def load_gate_up(e, k, done):
                for j, w in enumerate((w_gate, w_up)):
                    src = w[e] if isinstance(e, int) else w[bass.ds(e, 1)].squeeze(0)
                    sp.dma_start(wg[k][:, j], src.rearrange("(p c) f -> p c f", c=DC)).then_inc(done, 16)

            def load_down(e, k, done):
                src = w_down[e] if isinstance(e, int) else w_down[bass.ds(e, 1)].squeeze(0)
                sp.dma_start(wd[k][:], src.rearrange("(p c) n -> p c n", c=2)).then_inc(done, 16)

            def load_expert(e):
                load_gate_up(e, e, s_wg[e])
                load_down(e, e, s_wd[e])

            def stage2(t, b):
                if not (isinstance(t, int) and t == T_P):
                    if not (isinstance(t, int) and t == 0):
                        sp.wait_ge(s_mTp, 2 * t)
                    sp.dma_start(m_t[1 - b][:], rows(mix_d, t + 1)).then_inc(s_ml[1 - b], 16)
                    sp.dma_start(x1(t + 1), rows(x_rows, t + 1)).then_inc(s_xr[1 - b], 16)
                if not (isinstance(t, int) and t == 0):
                    store_h(t - 1)

            def store_h(t):
                sp.wait_ge(s_h, t + 1)
                sp.dma_start(rows(h_d, t), h_t[:]).then_inc(s_hst, 16)

            stage2(0, 0)
            load_expert(0)
            sp.wait_ge(s_wlo, N_WI + N_WO)
            with sp.Fori(1, T_P - 2, 2) as t:
                stage2(t, 1)
                stage2(t + 1, 0)
            sp.wait_ge(s_mix_s, 16)
            stage2(T_P - 1, 1)
            load_expert(1)
            stage2(T_P, 0)
            sp.wait_ge(s_op, 2 * T)
            load_gate_up(2, 2, s_wg[2])
            store_h(T_P)
            load_down(2, 2, s_wd[2])
            load_expert(3)

            def stage4(e, k):
                sp.wait_ge(s_gu, e - 3)
                load_gate_up(e, k, s_wg[k])
                sp.wait_ge(s_dn, e - 3)
                load_down(e, k, s_wd[k])

            with sp.Fori(4, NE - 3, 4) as e:
                for k in range(4):
                    stage4(e + k, k)
            sp.wait_ge(s_dn, NE - 2)
            sp.dma_start(fing[:], fin_g.to_broadcast([P, D])).then_inc(s_fg, 16)
            sp.wait_ge(s_dn, NE)

            sp.wait_ge(s_idx, 1)
            most = sp.value_load(cnt_i[0:1, 0:1], min_val=0, max_val=N_TOK)
            with sp.If(most > SLOTS):
                with sp.Fori(0, N_CHUNK - 1) as m:
                    with sp.Fori(0, NE) as e:
                        sp.wait_ge(o_ic, m * NE + e + 1)
                        load_gate_up(e, 0, o_w)
                        load_down(e, 0, o_w)
            sp.wait_ge(o_done, 1)

            def load_y(i):
                t, n = final_tile(i)
                src = y_d.rearrange("(r k) n -> r (k n)", k=2)
                sp.dma_start(yy[i % 4][0:n].rearrange("p k n -> p (k n)"), rows(src, t, n)).then_inc(s_yy[i % 4], 16)

            for i in range(4):
                load_y(i)
            for i in range(T + 1):
                if i + 4 < T:
                    sp.wait_ge(s_ysum, i + 1)
                    load_y(i + 4)
                if i > 0:
                    t, n = final_tile(i - 1)
                    sp.wait_ge(s_fo, i)
                    sp.dma_start(rows(y_rows, t, n), x1(t)[0:n]).then_inc(s_out, 16)
            sp.wait_ge(s_out, 16 * T)

        @block.tensor
        def _(pe):
            def transposes(src, n, bank_):
                for j in range(n):
                    last = nc.tensor.transpose(bank_[:, j * P:(j + 1) * P], src(j), ident)
                return last

            def set_up():
                pe.wait_ge(s_wmask, 1)
                for b in range(2):
                    if b == 0:
                        pe.wait_ge(s_xh, 2)
                        pe.wait_ge(s_xl, 2)
                    transposes(lambda j: ws_raw[:, 4 * b + j, :], 4, psT[b]).then_inc(s_tset, 1)
                pe.wait_ge(s_kc, 16)
                for b in range(2):
                    pe.wait_ge(s_eset_a if b == 0 else s_eset_v, 1)
                    transposes(lambda j: kc_t[:, 4 * b + j, :], 4, psT[b]).then_inc(s_tset, 1)

            def t_x(t):
                pe.wait_ge(s_x, 16 * (t + 1))
                for b in range(2):
                    if isinstance(t, int) and t == 1 and b == 0:
                        pe.wait_ge(s_eset_a, 2)
                    elif not (isinstance(t, int) and t == 0):
                        pe.wait_ge(s_pTa if b == 0 else s_kT, 2 * t - 2 if b == 0 else t)
                    transposes(lambda j: x_t[:, (4 * b + j) * P:(4 * b + j + 1) * P], 4, psT[b]).then_inc(s_xTp, 1)

            def z_group(t, g):
                c0, n = Z_GROUPS[g]
                if g == 0:
                    pe.wait_ge(s_xh, 2 * t + 2)
                    pe.wait_ge(s_xl, 2 * t + 2)
                if g == 2:
                    pe.wait_ge(s_qr, t + 1)
                elif g == 3:
                    pe.wait_ge(s_kr, t + 1)
                    pe.wait_ge(s_v, t + 1)
                elif not (isinstance(t, int) and t == 0):
                    pe.wait_ge(s_u if g == 0 else s_vg, t)
                k = 0
                for c in range(DC):
                    if isinstance(t, int) and t == 0 and g % 2 == 0 and c % 2 == 0:
                        pe.wait_ge(s_whi, 2 * g + c // 2 + 1)
                        pe.wait_ge(s_wlo, 2 * g + c // 2 + 1)
                    for a, w in ((xT_hi, wi_hi), (xT_lo, wi_hi), (xT_hi, wi_lo)):
                        last = nc.tensor.matmul(psZ[g % 2][:, 0:n], a[:, c, :], w[:, c, c0:c0 + n],
                                                start=(k == 0), stop=(k == 3 * DC - 1))
                        k += 1
                last.then_inc(s_z, 1)

            def t_qk(t):
                pe.wait_ge(s_qr, t + 1)
                if not (isinstance(t, int) and t == 0):
                    pe.wait_ge(s_gmo, t)
                transposes(lambda j: q_ro[:, j * P:(j + 1) * P], 4, psG).then_inc(s_qkTp, 1)
                pe.wait_ge(s_kr, t + 1)
                if not (isinstance(t, int) and t == 0):
                    pe.wait_ge(s_pTv, 2 * t)
                else:
                    pe.wait_ge(s_eset_v, 2)
                transposes(lambda j: k_ro[:], 1, psT[1]).then_inc(s_qkTp, 1)

            def scores(t, g):
                if g == 0:
                    pe.wait_ge(s_qT, t + 1)
                    pe.wait_ge(s_kT, t + 1)
                    if not (isinstance(t, int) and t == 0):
                        pe.wait_ge(s_sm, 2 * t)
                else:
                    pe.wait_ge(s_sm, 2 * t + 1)
                rows_ = slice(g * HD, (g + 1) * HD)
                for c in range(QPK):
                    last = nc.tensor.matmul(psS[:, c * 256:(c + 1) * 256], qT[rows_, c, :], kT[rows_, :],
                                            start=True, stop=True, skip_group_check=True)
                last.then_inc(s_sc, 1)

            def t_p(t, g):
                pe.wait_ge(s_p, 2 * t + g + 1)
                for b in range(2):
                    if g == 1:
                        pe.wait_ge(s_pTa if b == 0 else s_pTv, 2 * t + 1)
                    transposes(lambda j: s_t[g][:, 2 * b + j // 2, (j % 2) * P:(j % 2 + 1) * P], 4, psT[b])\
                        .then_inc(s_pTp, 1)

            def pv(t, g):
                pe.wait_ge(s_pTa, 2 * t + g + 1)
                pe.wait_ge(s_pTv, 2 * t + g + 1)
                if g == 0:
                    pe.wait_ge(s_vs, t + 1)
                    if not (isinstance(t, int) and t == 0):
                        pe.wait_ge(s_att, 2 * t)
                else:
                    pe.wait_ge(s_att, 2 * t + 1)
                for c in range(QPK):
                    for k in range(2):
                        last = nc.tensor.matmul(psO[:, (g * QPK + c) * HD:(g * QPK + c + 1) * HD],
                                                pT[:, 2 * c + k, :], v_t[:, k, g * HD:(g + 1) * HD],
                                                start=(k == 0), stop=(k == 1), skip_group_check=True)
                last.then_inc(s_pv, 1)

            def gm(t):
                pe.wait_ge(s_vn, t + 1)
                pe.wait_ge(s_qT, t + 1)
                for g in range(NG):
                    last = nc.tensor.matmul(psG[:, g * HD:(g + 1) * HD], wsT[:, g, :], vn_t[:, g * HD:(g + 1) * HD],
                                            start=True, stop=True, skip_group_check=True)
                last.then_inc(s_gm, 1)

            def stage1(t):
                before = not (isinstance(t, int) and t == 0)
                sample = isinstance(t, int) and t == T_P
                z_group(t, 0)
                if before:
                    gm(t - 1)
                z_group(t, 1)
                if before:
                    t_p(t - 1, 0)
                    scores(t - 1, 1)
                    pv(t - 1, 0)
                z_group(t, 2)
                if before:
                    t_p(t - 1, 1)
                else:
                    set_up()
                z_group(t, 3)
                t_qk(t)
                if before:
                    pv(t - 1, 1)
                if not sample:
                    t_x(t + 1)
                    scores(t, 0)

            pe.wait_ge(s_id, 16)
            t_x(0)
            stage1(0)
            stage1(1)
            with pe.Fori(2, T_P - 1) as t:
                stage1(t)
            stage1(T_P - 1)
            stage1(T_P)

            def sample_scores():
                pe.wait_ge(s_qT, T)
                pe.wait_ge(s_kT, T)
                pe.wait_ge(s_sm, 2 * T_P)
                for g in range(NKV):
                    r = slice(g * HD, (g + 1) * HD)
                    for b in range(N_SAMPLE):
                        last = nc.tensor.matmul(psS[:, 512 * g + 4 * b:512 * g + 4 * b + 4], kcT[r, b, :], qT[r, :, b],
                                                start=True, stop=True, skip_group_check=True)
                last.then_inc(s_sp, 1)
                pe.wait_ge(s_sv, 1)
                nc.tensor.matmul(psG[0:64, 128:129], prod[:], small[:, 0:1], start=True, stop=True).then_inc(s_sp, 1)

            def sample_rows():
                pe.wait_ge(s_sv, 2)
                nc.tensor.transpose(psO[0:64, 0:P], sT_s[:].rearrange("p g r -> p (g r)"), ident).then_inc(s_sp, 1)

            def sample_weights():
                pe.wait_ge(s_sv, 6)
                nc.tensor.transpose(psS[:, 0:64], s_s[:, 0:P], ident[0:64, 0:64]).then_inc(s_sp, 1)
                nc.tensor.matmul(psG[0:N_SAMPLE, 0:64], selp[:], ident[0:64, 0:64], start=True, stop=True)\
                    .then_inc(s_sp, 1)

            def sample_values():
                pe.wait_ge(s_sv, 8)
                pe.wait_ge(s_vc, 16)
                pe.wait_ge(s_v, T)
                nc.tensor.matmul(psO[:, 0:64], v_new[0:N_SAMPLE, :], d_s[:], start=True, stop=False, skip_group_check=True)
                for b in range(N_SAMPLE):
                    o = psO[:, 0:64].rearrange("p (g r) -> p g r", g=NKV)[:, :, 4 * b:4 * b + 4]
                    q = pT_s[:].rearrange("p (g r) -> p g r", g=NKV)[:, :, 4 * b:4 * b + 4]
                    last = nc.tensor.matmul(o, vc_t[:, b, :], q, start=False, stop=(b == N_SAMPLE - 1),
                                            skip_group_check=True)
                last.then_inc(s_sp, 1)

            def sample_out():
                pe.wait_ge(s_sv, 9)
                for c in range(QPK):
                    last = nc.tensor.transpose(psS[0:N_SAMPLE, 512 + c * P:512 + (c + 1) * P], oT_s[:, :, c], ident)
                last.then_inc(s_sp, 1)

            def t_m(t, b):
                pe.wait_ge(s_ml[b], (t - b + 2) * 8)
                for k in range(2):
                    if isinstance(t, int) and t == 0:
                        pe.wait_ge(s_pTa if k == 0 else s_kT, 2 * T_P if k == 0 else T)
                    else:
                        pe.wait_ge(s_mh, 2 * t - 1 + k)
                        pe.wait_ge(s_mlo, 2 * t - 1 + k)
                    transposes(lambda j: m_t[b][:, (4 * k + j) * P:(4 * k + j + 1) * P], 4, psT[k]).then_inc(s_mTp, 1)

            def out_half(t, b, h):
                if h == 0:
                    pe.wait_ge(s_mh, 2 * t + 2)
                    pe.wait_ge(s_mlo, 2 * t + 2)
                if isinstance(t, int) and t == 0:
                    pe.wait_ge(s_u if h == 0 else s_vg, T)
                else:
                    pe.wait_ge(s_x1, 2 * t - 1 + h)
                k = 0
                for c in range(DC):
                    if isinstance(t, int) and t == 0 and h == 0 and c % 2 == 0:
                        pe.wait_ge(s_whi, N_WI + c // 2 + 1)
                        pe.wait_ge(s_wlo, N_WI + c // 2 + 1)
                    for a, w in ((mT_hi, wo_hi), (mT_lo, wo_hi), (mT_hi, wo_lo)):
                        last = nc.tensor.matmul(psZ[h][:], a[b][:, c, :], w[:, c, h * 512:(h + 1) * 512],
                                                start=(k == 0), stop=(k == 3 * DC - 1))
                        k += 1
                last.then_inc(s_op, 1)

            def t_h(t):
                pe.wait_ge(s_h, t + 1)
                if isinstance(t, int) and t == 0:
                    pe.wait_ge(s_sv, 10)
                if not (isinstance(t, int) and t == 0):
                    pe.wait_ge(s_hTa, t)
                    pe.wait_ge(s_hTv, t)
                for j in range(DC):
                    last = nc.tensor.transpose(psS[:, j * P:(j + 1) * P], h_t[:, j * P:(j + 1) * P], ident)
                last.then_inc(s_hTp, 1)

            def route(t):
                pe.wait_ge(s_hTa, t + 1)
                pe.wait_ge(s_hTv, t + 1)
                if isinstance(t, int) and t == 0:
                    pe.wait_ge(s_p2, 64)
                else:
                    pe.wait_ge(s_lgo, t)
                for c in range(DC):
                    last = nc.tensor.matmul(psG[:, 0:NGRP + NE], hT[:, c, :], w_r[:, c, :],
                                            start=(c == 0), stop=(c == DC - 1))
                last.then_inc(s_lg, 1)

            def stage2(t, b):
                first = isinstance(t, int) and t == 0
                out_half(t, b, 0)
                if not (isinstance(t, int) and t == T_P):
                    t_m(t + 1, 1 - b)
                if first:
                    sample_weights()
                else:
                    t_h(t - 1)
                out_half(t, b, 1)
                if first:
                    sample_values()
                    sample_out()
                else:
                    route(t - 1)

            sample_scores()
            t_m(0, 0)
            sample_rows()
            stage2(0, 0)
            with pe.Fori(1, T_P - 2, 2) as t:
                stage2(t, 1)
                stage2(t + 1, 0)
            stage2(T_P - 1, 1)
            stage2(T_P, 0)
            t_h(T_P)
            route(T_P)

            pe.wait_ge(s_rv, 2)
            mm = lambda out, a, b, **k: nc.tensor.matmul(out, a, b, skip_group_check=True, **k)
            mm(psZ[0][:, 0:T * NE], tr_bf[:], m_bf[:].rearrange("p t e -> p (t e)"), start=True, stop=False)
            for j in range(T - 1):
                last = mm(psZ[0][:, (j + 1) * NE:T * NE].rearrange("p (t e) -> p t e", e=NE), on_bf[:],
                          m_bf[:, j:j + 1, :].to_broadcast([P, T - 1 - j, NE]), start=False, stop=(j == T - 2))
            for j in range(T):
                last = mm(psZ[1][:, 0:NE], on_bf[:], m_bf[:, j, :], start=(j == 0), stop=(j == T - 1))
            last.then_inc(s_rp, 1)

            def table(ready, before, done):
                for k in range(2):
                    pe.wait_ge(ready, before + k + 1)
                    for t in range(T):
                        last = mm(psG[:, 0:3 * NE], oh_r[:, k, t, :], rhs_t[:, k, t, :],
                                  start=(t == 0 and k == 0), stop=(t == T - 1 and k == 1))
                last.then_inc(done, 1)

            table(s_rv, 2, s_rp)

            def t_g(slot, done):
                for k in range(2):
                    transposes(lambda j: xg[slot][:, (4 * k + j) * P:(4 * k + j + 1) * P], 4, psT[k]).then_inc(done, 1)

            def gate_up(z, w, done):
                for c in range(DC):
                    last = nc.tensor.matmul(psZ[z][:], xgT[:, c, :], w[:, :, c, :], start=(c == 0), stop=(c == DC - 1))
                last.then_inc(done, 1)

            def t_hid(done):
                transposes(lambda j: hid[:, j * P:(j + 1) * P], 2, psO).then_inc(done, 1)

            def down(w, done):
                for h in range(2):
                    for c in range(2):
                        last = nc.tensor.matmul(psS[:, h * 512:(h + 1) * 512], hidT[:, c, :],
                                                w[:, c, h * 512:(h + 1) * 512], start=(c == 0), stop=(c == 1))
                last.then_inc(done, 1)

            def down_split(k, done):
                for h in range(2):
                    n = 0
                    for c in range(2):
                        for a, w in ((hidT_hi, wd_hi), (hidT_lo, wd_hi), (hidT_hi, wd_lo[k])):
                            last = nc.tensor.matmul(psS[:, h * 512:(h + 1) * 512], a[:, c, :], w[:, c, h * 512:(h + 1) * 512],
                                                    start=(n == 0), stop=(n == 5))
                            n += 1
                last.then_inc(done, 1)

            def first_g(e, k):
                pe.wait_ge(s_ga[k], (e - k + 4) * 4)
                if not (isinstance(e, int) and e == 0):
                    pe.wait_ge(s_gTa, e)
                    pe.wait_ge(s_gTv, e)
                t_g(k, s_gTp)

            def last_d(e, k):
                pe.wait_ge(s_dTh, e + 1)
                if not (isinstance(e, int) and e == 0):
                    pe.wait_ge(s_ya, e)
                    pe.wait_ge(s_yv, e)
                if isinstance(e, int) and e == NE - 1:
                    pe.wait_ge(s_wd[k], NE // 4 * 16)
                    down(wd[k], s_dn)
                else:
                    pe.wait_ge(s_dTl, e + 1)
                    pe.wait_ge(s_wdh, e + 1)
                    pe.wait_ge(s_wdl, e + 1)
                    down_split(k, s_dn)

            def stage4(e, k):
                b = k % 2
                pe.wait_ge(s_gTa, e + 1)
                pe.wait_ge(s_gTv, e + 1)
                pe.wait_ge(s_wg[k], (e - k + 4) * 8)
                if not (isinstance(e, int) and e < 2):
                    pe.wait_ge(s_hid, e - 1)
                gate_up(b, wg[k][:], s_gu)
                if not (isinstance(e, int) and e == NE - 1):
                    first_g(e + 1, (k + 1) % 4)
                if not (isinstance(e, int) and e == 0):
                    last_d(e - 1, (k + 3) % 4)
                pe.wait_ge(s_hid, e + 1)
                t_hid(s_dTp)

            first_g(0, 0)
            for k in range(4):
                stage4(k, k)
            with pe.Fori(4, NE - 7, 4) as e:
                for k in range(4):
                    stage4(e + k, k)
            for k in range(4):
                stage4(NE - 4 + k, k)
            last_d(NE - 1, 3)

            pe.wait_ge(s_idx, 1)
            most = pe.value_load(cnt_i[0:1, 0:1], min_val=0, max_val=N_TOK)
            with pe.If(most > SLOTS):
                with pe.Fori(0, N_CHUNK - 1) as m:
                    table(o_oh, m * 2, o_tab)
                    with pe.Fori(0, NE) as e:
                        n = m * NE + e
                        pe.wait_ge(o_ga, 16 * n + 16)
                        t_g(0, o_gTp)
                        pe.wait_ge(o_gTa, n + 1)
                        pe.wait_ge(o_gTv, n + 1)
                        pe.wait_ge(o_w, 48 * n + 48)
                        gate_up(0, wg[0][:], o_gu)
                        pe.wait_ge(o_hid, n + 1)
                        t_hid(o_dTp)
                        pe.wait_ge(o_dT, n + 1)
                        down(wd[0], o_dn)

        @block.scalar
        def _(act):
            act.wait_ge(s_gmix, 16)

            def split(n):
                act.wait_ge(s_wi[n], 16)
                for c in range(2):
                    g = 2 * (n % 4) + c
                    last = nc.scalar.activation(wi_piece(wi_hi, n)[:, c, :], wi_piece(wi_raw, n)[:, c, :],
                                                ACT.Copy, scale=gmix[:, g:g + 1])
                last.then_inc(s_whi, 1)

            def copy(out, in_):
                return nc.scalar.activation(out, in_, ACT.Copy)

            def set_up():
                act.wait_ge(s_tset, 1)
                copy(wsT[:, 0:4, :].rearrange("p g t -> p (g t)"), psT[0][:]).then_inc(s_eset_a, 1)
                act.wait_ge(s_tset, 3)
                copy(kcT[:, 0:4, :].rearrange("p g t -> p (g t)"), psT[0][:]).then_inc(s_eset_a, 1)

            def square(t):
                act.wait_ge(s_x, 16 * (t + 1))
                if not (isinstance(t, int) and t == 0):
                    act.wait_ge(s_rstd, t)
                    act.wait_ge(s_sq, t)
                nc.scalar.activation(junk[:], x_t[:], ACT.Square, accum_out=st[:, 0:1]).then_inc(s_sq, 1)

            def x_hi(t):
                for b in range(2):
                    act.wait_ge(s_xTp, 2 * t + b + 1)
                    if not (isinstance(t, int) and t == 0):
                        act.wait_ge(s_z, 4 * t)
                    copy(xT_hi[:, 4 * b:4 * b + 4, :].rearrange("p c t -> p (c t)"), psT[b][:]).then_inc(s_xh, 1)

            def exps(t, g):
                act.wait_ge(s_nb, 2 * t + g + 1)
                for c in range(QPK):
                    h = g * QPK + c
                    nc.scalar.activation(s_t[g][:, c, :], s_t[g][:, c, :], ACT.Exp, bias=st[:, 8 + h:9 + h],
                                         accum_out=st[:, 16 + h:17 + h])
                nc.scalar.activation(st[:, 32 + 4 * g:36 + 4 * g], st[:, 24 + 4 * g:28 + 4 * g], ACT.Exp).then_inc(s_p, 1)

            def p_out(t, g):
                act.wait_ge(s_pTp, 4 * t + 2 * g + 1)
                if g == 1:
                    act.wait_ge(s_pv, 2 * t + 1)
                elif not (isinstance(t, int) and t == 0):
                    act.wait_ge(s_pv, 2 * t)
                copy(pT[:, 0:4, :].rearrange("p j t -> p (j t)"), psT[0][:]).then_inc(s_pTa, 1)

            def values(t):
                act.wait_ge(s_rstd, t + 1)
                act.wait_ge(s_kr, t + 1)
                if isinstance(t, int) and t == T_P:
                    act.wait_ge(s_kvout, 32)
                if not (isinstance(t, int) and t == 0):
                    act.wait_ge(s_vs, t)
                nc.scalar.activation(v_new[:], psZ[1][:, P:2 * P], ACT.Copy, scale=st[:, 2:3]).then_inc(s_v, 1)

            def shift(t):
                if isinstance(t, int) and t == 0:
                    act.wait_ge(s_zero, 1)
                else:
                    act.wait_ge(s_pv, 2 * t)
                    copy(v_t[:, 0, :], v_t[:, 1, :]).then_inc(act_step, 1)
                    act.wait_ge(act_step, t)
                act.wait_ge(s_v, t + 1)
                copy(v_t[:, 1, :], v_new[:]).then_inc(s_vs, 1)

            def gelu_u(t):
                act.wait_ge(s_z, 4 * t + 3)
                if not (isinstance(t, int) and t == 0):
                    act.wait_ge(s_gmo, t)
                nc.scalar.activation(u_t[:], psZ[0][:], ACT.Gelu, scale=st[:, 2:3]).then_inc(s_u, 1)

            def gelu_v(t):
                act.wait_ge(s_z, 4 * t + 4)
                if not (isinstance(t, int) and t == 0):
                    act.wait_ge(s_vn, t)
                nc.scalar.activation(vg_t[:], psZ[1][:], ACT.Gelu, scale=st[:, 2:3]).then_inc(s_vg, 1)

            def q_out(t):
                act.wait_ge(s_qkTp, 2 * t + 1)
                if not (isinstance(t, int) and t == 0):
                    act.wait_ge(s_sc, 2 * t)
                copy(qT[:].rearrange("p c t -> p (c t)"), psG[:]).then_inc(s_qT, 1)

            def stage1(t):
                before = not (isinstance(t, int) and t == 0)
                sample = isinstance(t, int) and t == T_P
                if before:
                    exps(t - 1, 0)
                    p_out(t - 1, 0)
                else:
                    for n in range(4, N_WI):
                        split(n)
                values(t)
                if before:
                    exps(t - 1, 1)
                    p_out(t - 1, 1)
                else:
                    set_up()
                gelu_u(t)
                q_out(t)
                gelu_v(t)
                if not sample:
                    x_hi(t + 1)
                    shift(t)
                    square(t + 1)

            split(0)
            x_hi(0)
            split(1)
            square(0)
            split(2)
            split(3)
            stage1(0)
            stage1(1)
            with act.Fori(2, T_P - 1) as t:
                stage1(t)
            stage1(T_P - 1)
            stage1(T_P)

            def sample_exps():
                act.wait_ge(s_sv, 4)
                nc.scalar.activation(s_s[:, 0:129], s_s[:, 0:129], ACT.Exp, bias=st[0:64, 40:41], scale=SCALE,
                                     accum_out=st[0:64, 42:43])
                nc.scalar.activation(st[0:64, 43:44], st[0:64, 41:42], ACT.Exp).then_inc(s_sa, 1)

            def split_out(n):
                act.wait_ge(s_z, 4 * T)
                act.wait_ge(s_wo[n], 16)
                copy(wo_hi[:, 2 * n:2 * n + 2, :], wo_raw(n)).then_inc(s_whi, 1)

            def m_hi(t, b):
                for k in range(2):
                    act.wait_ge(s_mTp, 2 * t + k + 1)
                    if not (isinstance(t, int) and t < 2):
                        act.wait_ge(s_op, 2 * t - 2)
                    copy(mT_hi[b][:, 4 * k:4 * k + 4, :].rearrange("p c t -> p (c t)"), psT[k][:]).then_inc(s_mh, 1)

            def square2(t):
                act.wait_ge(s_x1, 2 * t + 2)
                if not (isinstance(t, int) and t == 0):
                    act.wait_ge(s_r2, t)
                    act.wait_ge(s_sq2, t)
                nc.scalar.activation(junk2[:], x1(t), ACT.Square, accum_out=small[:, 8:9]).then_inc(s_sq2, 1)

            def h_out(t):
                act.wait_ge(s_hTp, t + 1)
                if not (isinstance(t, int) and t == 0):
                    act.wait_ge(s_lg, t)
                copy(hT[:, 0:4, :].rearrange("p c t -> p (c t)"), psS[:, 0:512]).then_inc(s_hTa, 1)

            def choice_exps(a, b, done):
                act.wait_ge(s_ra, done + 1)
                nc.scalar.activation(g8[0][:, a:b, 0:4], g8[0][:, a:b, 0:4], ACT.Exp).then_inc(s_sa, 1)
                act.wait_ge(s_ra, done + 2)
                nc.scalar.activation(c9[6][:, a:b], c9[6][:, a:b], ACT.Exp).then_inc(s_sa, 1)

            def stage2(t, b):
                if not (isinstance(t, int) and t == T_P):
                    m_hi(t + 1, 1 - b)
                if not (isinstance(t, int) and t == 0):
                    h_out(t - 1)
                if isinstance(t, int) and t == T_P:
                    choice_exps(0, T - 2, 0)
                square2(t)

            split_out(0)
            split_out(1)
            m_hi(0, 0)
            split_out(2)
            split_out(3)
            sample_exps()
            stage2(0, 0)
            with act.Fori(1, T_P - 2, 2) as t:
                stage2(t, 1)
                stage2(t + 1, 0)
            stage2(T_P - 1, 1)
            stage2(T_P, 0)
            h_out(T_P)

            choice_exps(T - 2, T, 2)

            def g_out(e):
                act.wait_ge(s_gTp, 2 * e + 1)
                if not (isinstance(e, int) and e == 0):
                    act.wait_ge(s_gu, e)
                copy(xgT[:, 0:4, :].rearrange("p c t -> p (c t)"), psT[0][:]).then_inc(s_gTa, 1)

            def silu(e, b):
                act.wait_ge(s_gu, e + 1)
                if not (isinstance(e, int) and e == 0):
                    act.wait_ge(s_hid, e)
                nc.scalar.activation(sg[:], psZ[b][:, 0:FE], ACT.Silu).then_inc(s_sg, 1)

            def hid_out(e):
                act.wait_ge(s_dTp, e + 1)
                if not (isinstance(e, int) and e == 0):
                    act.wait_ge(s_dn, e)
                dst = hidT if isinstance(e, int) and e == NE - 1 else hidT_hi
                copy(dst[:].rearrange("p c t -> p (c t)"), psO[:, 0:256]).then_inc(s_dTh, 1)

            def down_hi(e, k):
                act.wait_ge(s_wd[k], (e - k + 4) * 4)
                if not (isinstance(e, int) and e == 0):
                    act.wait_ge(s_dn, e)
                copy(wd_hi[:], wd[k][:]).then_inc(s_wdh, 1)

            def y_out(e, k):
                act.wait_ge(s_dn, e + 1)
                if not (isinstance(e, int) and e < 4):
                    act.wait_ge(s_sc4[k], (e - k) * 4)
                copy(y_t[k][:, 0:512], psS[:, 0:512]).then_inc(s_ya, 1)

            def stage4(e, k):
                b = k % 2
                silu(e, b)
                if not (isinstance(e, int) and e == NE - 1):
                    g_out(e + 1)
                if not (isinstance(e, int) and e == 0):
                    y_out(e - 1, (k + 3) % 4)
                hid_out(e)
                if not (isinstance(e, int) and e == NE - 1):
                    down_hi(e, k)

            g_out(0)
            for k in range(4):
                stage4(k, k)
            with act.Fori(4, NE - 7, 4) as e:
                for k in range(4):
                    stage4(e + k, k)
            for k in range(4):
                stage4(NE - 4 + k, k)
            y_out(NE - 1, 3)

            act.wait_ge(s_idx, 1)
            most = act.value_load(cnt_i[0:1, 0:1], min_val=0, max_val=N_TOK)
            with act.If(most > SLOTS):
                with act.Fori(0, (N_CHUNK - 1) * NE) as n:
                    act.wait_ge(o_gTp, 2 * n + 1)
                    copy(xgT[:, 0:4, :].rearrange("p c t -> p (c t)"), psT[0][:]).then_inc(o_gTa, 1)
                    act.wait_ge(o_gu, n + 1)
                    nc.scalar.activation(sg[:], psZ[0][:, 0:FE], ACT.Silu).then_inc(o_sg, 1)
                    act.wait_ge(o_dTp, n + 1)
                    copy(hidT[:].rearrange("p c t -> p (c t)"), psO[:, 0:256]).then_inc(o_dT, 1)
                    act.wait_ge(o_dn, n + 1)
                    copy(y_t[0][:, 0:512], psS[:, 0:512]).then_inc(o_ya, 1)
            act.wait_ge(o_done, 1)

            def sq_final(i, b):
                t, n = final_tile(i)
                act.wait_ge(s_ysum, i + 1)
                if not (isinstance(i, int) and i == 0):
                    act.wait_ge(s_fsq, i)
                if not (isinstance(i, int) and i < 2):
                    act.wait_ge(s_fr, i - 1)
                nc.scalar.activation(junk3[0:n], x1(t)[0:n], ACT.Square, accum_out=fst[0:n, b, 0:1]).then_inc(s_fsq, 1)

            sq_final(0, 0)
            sq_final(1, 1)
            with act.Fori(2, T_P - 1, 2) as i:
                sq_final(i, 0)
                sq_final(i + 1, 1)
            sq_final(T_P, 0)

        @block.vector
        def _(dve):
            step = Chain(dve, dve_step)
            tt = nc.vector.tensor_tensor
            ts = nc.vector.tensor_scalar
            stt = nc.vector.scalar_tensor_tensor
            cp = nc.vector.tensor_copy
            nc.vector.memset(kT[:], 0.0)
            nc.vector.memset(v_t[:], 0.0)
            nc.vector.memset(small[:, 0:1], 1.0).then_inc(s_zero, 1)
            dve.wait_ge(s_zero, 1)
            dve.wait_ge(s_gmix, 16)

            def split(n):
                dve.wait_ge(s_wi[n], 16)
                dve.wait_ge(s_whi, n + 1)
                for c in range(2):
                    g = 2 * (n % 4) + c
                    last = stt(out=wi_piece(wi_lo, n)[:, c, :], in0=wi_piece(wi_raw, n)[:, c, :], scalar=gmix[:, g:g + 1],
                               in1=wi_piece(wi_hi, n)[:, c, :].bitcast(F32), op0=ALU.mult, op1=ALU.subtract)
                last.then_inc(s_wlo, 1)

            def x_lo(t):
                for b in range(2):
                    dve.wait_ge(s_xh, 2 * t + b + 1)
                    dst = slice(4 * b, 4 * b + 4)
                    tt(xT_lo[:, dst, :].rearrange("p c t -> p (c t)"), psT[b][:],
                       xT_hi[:, dst, :].rearrange("p c t -> p (c t)").bitcast(F32), ALU.subtract).then_inc(s_xl, 1)

            def set_up():
                dve.wait_ge(s_tset, 2)
                cp(wsT[:, 4:8, :].rearrange("p g t -> p (g t)"), psT[1][:]).then_inc(s_eset_v, 1)
                dve.wait_ge(s_tset, 4)
                cp(kcT[:, 4:8, :].rearrange("p g t -> p (g t)"), psT[1][:]).then_inc(s_eset_v, 1)

            def rope(src, n, dst):
                cos = csr[:, 0:32].unsqueeze(1).unsqueeze(1).to_broadcast([P, n, 2, 32])
                sin = csr[:, 32:64].unsqueeze(1).unsqueeze(1).to_broadcast([P, n, 2, 32])
                a = rope_a[:, 0:n * HD].rearrange("p (h two d) -> p h two d", two=2, d=32)
                b = rope_b[:, 0:n * HD].rearrange("p (h two d) -> p h two d", two=2, d=32)
                src4 = src.rearrange("p (h two d) -> p h two d", two=2, d=32)
                tt(a, src4, cos, ALU.mult)
                step(tt(b, src4, sin, ALU.mult))
                tt(dst[0], a[:, :, 0, :], b[:, :, 1, :], ALU.subtract)
                return tt(dst[1], a[:, :, 1, :], b[:, :, 0, :], ALU.add)

            def rope_q(t):
                dve.wait_ge(s_rstd, t + 1)
                cs = cst[:, C_CS + t * HD:C_CS + t * HD + HD] if isinstance(t, int) else cst[:, bass.ds(t * HD + C_CS, HD)]
                step(ts(csr[:], cs, st[:, 2:3], None, ALU.mult))
                dve.wait_ge(s_z, 4 * t + 1)
                if not (isinstance(t, int) and t == 0):
                    dve.wait_ge(s_qkTp, 2 * t)
                q = q_ro[:].rearrange("p (c k two d) -> p k c two d", k=2, two=2, d=32)
                for k in range(2):
                    last = rope(psZ[0][:, k * 256:(k + 1) * 256], QPK, (q[:, k, :, 0, :], q[:, k, :, 1, :]))
                    if k == 0:
                        step(last)
                last.then_inc(s_qr, 1)

            def rope_k(t):
                dve.wait_ge(s_z, 4 * t + 2)
                dve.wait_ge(s_qr, t + 1)
                if isinstance(t, int) and t == T_P:
                    dve.wait_ge(s_kvout, 32)
                k = k_ro[:].rearrange("p (k two d) -> p k two d", two=2, d=32)
                rope(psZ[1][:, 0:P], NKV, (k[:, :, 0, :], k[:, :, 1, :])).then_inc(s_kr, 1)

            def softmax(t, g):
                dve.wait_ge(s_sc, 2 * t + g + 1)
                if not (isinstance(t, int) and t == 0):
                    dve.wait_ge(s_pTp, 4 * t - 2 + 2 * g)
                    dve.wait_ge(s_att, 2 * t - 1 + g)
                first = isinstance(t, int) and t == 0
                c = C_MF if first else C_MR
                mask = cst[:, c:c + 2 * P].unsqueeze(1).to_broadcast([P, QPK, 2 * P])
                stt(out=s_t[g][:], in0=psS[:].rearrange("p (c s) -> p c s", c=QPK), scalar=SCALE, in1=mask,
                    op0=ALU.mult, op1=ALU.add).then_inc(s_sm, 1)
                dve.wait_ge(s_sm, 2 * t + g + 1)
                mx = st[:, 44 + 4 * g:48 + 4 * g]
                sink = sink_t[:, 4 * g:4 * g + 4]
                step(nc.vector.tensor_reduce(mx, s_t[g][:], AX, ALU.max))
                step(tt(mx, mx, sink, ALU.max))
                ts(st[:, 8 + 4 * g:12 + 4 * g], mx, -1.0, None, ALU.mult)
                tt(st[:, 24 + 4 * g:28 + 4 * g], sink, mx, ALU.subtract).then_inc(s_nb, 1)

            def p_out(t, g):
                dve.wait_ge(s_pTp, 4 * t + 2 * g + 2)
                if g == 1:
                    dve.wait_ge(s_pv, 2 * t + 1)
                elif not (isinstance(t, int) and t == 0):
                    dve.wait_ge(s_pv, 2 * t)
                cp(pT[:, 4:8, :].rearrange("p j t -> p (j t)"), psT[1][:]).then_inc(s_pTv, 1)

            def att_out(t, g):
                dve.wait_ge(s_p, 2 * t + g + 1)
                r = st[:, 52 + 4 * g:56 + 4 * g]
                step(tt(r, st[:, 16 + 4 * g:20 + 4 * g], st[:, 32 + 4 * g:36 + 4 * g], ALU.add))
                step(nc.vector.reciprocal(r, r))
                dve.wait_ge(s_pv, 2 * t + g + 1)
                w = QPK * HD
                tt(mix_t[:, g * w:(g + 1) * w].rearrange("p (c d) -> p c d", c=QPK),
                   psO[:, g * w:(g + 1) * w].rearrange("p (c d) -> p c d", c=QPK),
                   r.unsqueeze(2).to_broadcast([P, QPK, HD]), ALU.mult).then_inc(s_att, 1)

            def gm_out(t):
                dve.wait_ge(s_gm, t + 1)
                dve.wait_ge(s_u, t + 1)
                if not (isinstance(t, int) and t == 0):
                    dve.wait_ge(s_mix, 16 * t)
                half = mix_t[:, ATT:D]
                step(tt(half.rearrange("p (g d) -> p g d", g=NG), psG[:].rearrange("p (g d) -> p g d", g=NG),
                        bsT[:].unsqueeze(2).to_broadcast([P, NG, HD]), ALU.add))
                tt(half, half, u_t[:], ALU.mult).then_inc(s_gmo, 1)

            def norm_v(t):
                dve.wait_ge(s_vg, t + 1)
                step(nc.vector.bn_stats(rope_a[:, 0:6], vg_t[:]))
                settle(dve)
                nc.vector.bn_aggr(st[:, 3:5], rope_a[:, 0:6]).then_inc(s_var, 1)
                dve.wait_ge(s_var, t + 1)
                if not (isinstance(t, int) and t == 0):
                    dve.wait_ge(s_gm, t)
                step(stt(out=vn_t[:], in0=vg_t[:], scalar=st[:, 3:4], in1=lng[:], op0=ALU.subtract, op1=ALU.mult))
                dve.wait_ge(s_lnr, t + 1)
                stt(out=vn_t[:], in0=vn_t[:], scalar=st[:, 6:7], in1=lnb[:], op0=ALU.mult, op1=ALU.add).then_inc(s_vn, 1)

            def k_out(t):
                dve.wait_ge(s_qkTp, 2 * t + 2)
                if not (isinstance(t, int) and t == 0):
                    dve.wait_ge(s_sc, 2 * t)
                    dve.wait_ge(s_kT, t)
                    step(cp(kT[:, 0:P], kT[:, P:2 * P]))
                cp(kT[:, P:2 * P], psT[1][:, 0:P]).then_inc(s_kT, 1)

            def stage1(t):
                before = not (isinstance(t, int) and t == 0)
                sample = isinstance(t, int) and t == T_P
                if before:
                    softmax(t - 1, 0)
                else:
                    dve.wait_ge(s_cst, 16)
                rope_q(t)
                if before:
                    gm_out(t - 1)
                    p_out(t - 1, 0)
                    softmax(t - 1, 1)
                    att_out(t - 1, 0)
                else:
                    split(4)
                    split(5)
                rope_k(t)
                if before:
                    p_out(t - 1, 1)
                else:
                    split(6)
                    split(7)
                    set_up()
                    dve.wait_ge(s_small, 16 * 7)
                    dve.wait_ge(s_msk, 16)
                k_out(t)
                if before:
                    att_out(t - 1, 1)
                if not sample:
                    x_lo(t + 1)
                norm_v(t)

            split(0)
            x_lo(0)
            split(1)
            split(2)
            split(3)
            stage1(0)
            n1 = step.n
            stage1(1)
            per = step.n - n1
            n2 = step.n
            with dve.Fori(2, T_P - 1) as t:
                step.n = (t - 2) * per + n2
                stage1(t)
            step.n = n2 + (T_P - 3) * per
            stage1(T_P - 1)
            stage1(T_P)

            def sample_products():
                dve.wait_ge(s_qT, T)
                dve.wait_ge(s_kT, T)
                step(nc.vector.memset(prod[:], 0.0))
                for g in range(NKV):
                    r = slice(g * HD, (g + 1) * HD)
                    last = tt(prod[r, 32 * g:32 * g + 32].rearrange("p (b c) -> p b c", c=QPK),
                              qT[r, :, 0:N_SAMPLE].rearrange("p c b -> p b c"),
                              kT[r, P:P + N_SAMPLE].unsqueeze(2).to_broadcast([HD, N_SAMPLE, QPK]), ALU.mult)
                last.then_inc(s_sv, 1)

            def sample_cache_scores():
                dve.wait_ge(s_sp, 1)
                cp(sT_s[:], psS[:].rearrange("p (g r) -> p g r", g=NKV)[:, :, 0:32]).then_inc(s_sv, 1)

            def sample_gmlp():
                dve.wait_ge(s_mix, 16 * T_P)
                step(nc.vector.memset(mix_t[:], 0.0))
                dve.wait_ge(s_vn, T)
                dve.wait_ge(s_u, T)
                v3 = vn_t[0:N_SAMPLE, :].rearrange("p (g d) -> p g d", g=NG)
                m3 = mix_t[0:N_SAMPLE, ATT:D].rearrange("p (g d) -> p g d", g=NG)
                step(tt(m3, v3, w00[0:N_SAMPLE, :].unsqueeze(2).to_broadcast([N_SAMPLE, NG, HD]), ALU.mult))
                step(tt(m3, m3, b00[0:N_SAMPLE, :].unsqueeze(2).to_broadcast([N_SAMPLE, NG, HD]), ALU.add))
                step(tt(mix_t[0:N_SAMPLE, ATT:D], mix_t[0:N_SAMPLE, ATT:D], u_t[0:N_SAMPLE, :], ALU.mult))

            def sample_maxima():
                dve.wait_ge(s_sp, 3)
                cp(s_s[:, 0:P], psO[0:64, 0:P])
                cp(s_s[:, P:P + 1], psG[0:64, 128:129]).then_inc(s_sv, 1)
                dve.wait_ge(s_sv, 3)
                step(nc.vector.tensor_reduce(st[0:64, 44:45], s_s[:, 0:P + 1], AX, ALU.max))
                step(ts(st[0:64, 44:45], st[0:64, 44:45], SCALE, sinkr[0:64, :], ALU.mult, ALU.max))
                ts(st[0:64, 40:41], st[0:64, 44:45], -1.0, None, ALU.mult)
                tt(st[0:64, 41:42], sinkr[0:64, :], st[0:64, 44:45], ALU.subtract).then_inc(s_sv, 1)

            def sample_weights():
                dve.wait_ge(s_sa, 1)
                step(tt(st[0:64, 45:46], st[0:64, 42:43], st[0:64, 43:44], ALU.add))
                step(nc.vector.reciprocal(st[0:64, 45:46], st[0:64, 45:46]))
                ts(s_s[:, 0:P + 1], s_s[:, 0:P + 1], st[0:64, 45:46], None, ALU.mult).then_inc(s_sv, 1)
                dve.wait_ge(s_sv, 5)
                ts(selp[:], cst[0:64, C_SEL:C_SEL + N_SAMPLE], s_s[:, P:P + 1], None, ALU.mult).then_inc(s_sv, 1)

            def sample_weights_out():
                dve.wait_ge(s_sp, 4)
                cp(pT_s[:], psS[:, 0:64]).then_inc(s_sv, 1)
                dve.wait_ge(s_sp, 5)
                cp(d_s[:], psG[0:N_SAMPLE, 0:64]).then_inc(s_sv, 1)

            def sample_values_out():
                dve.wait_ge(s_sp, 6)
                for g in range(NKV):
                    r = slice(g * HD, (g + 1) * HD)
                    last = cp(oT_s[r, :, :].rearrange("p b c -> p (b c)"), psO[r, 32 * g:32 * g + 32])
                last.then_inc(s_sv, 1)

            def sample_rows_out():
                dve.wait_ge(s_sp, 7)
                cp(mix_t[0:N_SAMPLE, 0:ATT].rearrange("p (k c d) -> p c k d", k=NKV, c=QPK),
                   psS[0:N_SAMPLE, 512:1024].rearrange("p (c k d) -> p c k d", k=NKV, c=QPK)).then_inc(s_sv, 1)

            def split_out(n):
                dve.wait_ge(s_whi, N_WI + n + 1)
                dve.wait_ge(s_wo[n], 16)
                tt(wo_lo[:, 2 * n:2 * n + 2, :], wo_raw(n), wo_hi[:, 2 * n:2 * n + 2, :].bitcast(F32), ALU.subtract)\
                    .then_inc(s_wlo, 1)

            red = nc.vector.tensor_reduce

            gmax, gidx, m1, m2, i1, i2 = c9[0], c9[2], c9[3], c9[4], c9[5], c9[7]

            def over(x, a, b, n):
                return x[:, a:b].unsqueeze(2).to_broadcast([P, b - a, n])

            def numbers(a, b, n):
                return cst[:, C_IO:C_IO + n].unsqueeze(1).to_broadcast([P, b - a, n])

            def first_of(eq, a, b, n, idx, onehot):
                step(stt(out=eq, in0=eq, scalar=-64.0, in1=numbers(a, b, n), op0=ALU.mult, op1=ALU.add))
                step(red(idx[:, a:b], eq, AX, ALU.min))
                step(stt(out=onehot, in0=numbers(a, b, n), scalar=-64.0, in1=over(idx, a, b, n), op0=ALU.add,
                         op1=ALU.is_equal))

            def choose_group(a, b):
                t = slice(a, b)
                lg, oh = logits[:, t, 0:NGRP], g8[1][:, t, 0:4]
                step(red(gmax[:, t], lg, AX, ALU.max))
                tt(g8[0][:, t, 0:4], lg, over(gmax, a, b, 4), ALU.subtract).then_inc(s_ra, 1)
                step(tt(oh, lg, over(gmax, a, b, 4), ALU.is_equal))
                first_of(oh, a, b, 4, gidx, oh)
                le = logits[:, t, NGRP:].rearrange("p t (g e) -> p t g e", g=NGRP)
                for g in range(NGRP):
                    o = g8[1][:, t, g:g + 1].to_broadcast([P, b - a, EPG])
                    last = tt(tmp_e[:, t, g * EPG:(g + 1) * EPG], le[:, :, g, :], o, ALU.mult)
                step(last)
                step(red(g8[2][:, t, :], tmp_e[:, t, :].rearrange("p t (g e) -> p t e g", g=NGRP), AX, ALU.add))

            def choose_experts(a, b):
                t = slice(a, b)
                esel, e2, eq, oh = g8[2][:, t, :], g8[3][:, t, :], g8[4][:, t, :], g8[5][:, t, :]
                step(red(m1[:, t], esel, AX, ALU.max))
                step(tt(eq, esel, over(m1, a, b, 8), ALU.is_equal))
                first_of(eq, a, b, 8, i1, oh)
                step(stt(out=e2, in0=oh, scalar=NEG, in1=esel, op0=ALU.mult, op1=ALU.add))
                step(red(m2[:, t], e2, AX, ALU.max))
                step(tt(eq, e2, over(m2, a, b, 8), ALU.is_equal))
                first_of(eq, a, b, 8, i2, oh)
                tt(c9[6][:, t], m2[:, t], m1[:, t], ALU.subtract).then_inc(s_ra, 1)
                step(stt(out=gidx[:, t], in0=gidx[:, t], scalar=float(EPG), in1=cst[:, C_INV + a:C_INV + b], op0=ALU.mult,
                         op1=ALU.add))
                tt(i1[:, t], gidx[:, t], i1[:, t], ALU.add)
                step(tt(i2[:, t], gidx[:, t], i2[:, t], ALU.add))
                tt(one_e[:, 0, t, :], numbers(a, b, NE), over(i1, a, b, NE), ALU.is_equal)
                step(tt(one_e[:, 1, t, :], numbers(a, b, NE), over(i2, a, b, NE), ALU.is_equal))
                tt(m_bf[:, t, :], one_e[:, 0, t, :], one_e[:, 1, t, :], ALU.add).then_inc(s_rv, 1)

            def table_columns(a, b):
                t = slice(a, b)
                for k in range(2):
                    ts(rhs_t[:, k, t, 0:NE], one_e[:, k, t, :], cst[:, C_PR:C_PR + 1], None, ALU.mult)
                    tt(rhs_t[:, k, t, NE:2 * NE], one_e[:, k, t, :],
                       cst[:, C_TILE + a:C_TILE + b].unsqueeze(2).to_broadcast([P, b - a, NE]), ALU.mult)
                    ts(rhs_t[:, k, t, 2 * NE:3 * NE], one_e[:, k, t, :], float(k + 1), None, ALU.mult)

            def m_lo(t, b):
                for k in range(2):
                    dve.wait_ge(s_mh, 2 * t + k + 1)
                    dst = slice(4 * k, 4 * k + 4)
                    tt(mT_lo[b][:, dst, :].rearrange("p c t -> p (c t)"), psT[k][:],
                       mT_hi[b][:, dst, :].rearrange("p c t -> p (c t)").bitcast(F32), ALU.subtract).then_inc(s_mlo, 1)

            def residual(t, b, h):
                if h == 0:
                    dve.wait_ge(s_xr[b], (t - b + 2) * 8)
                dve.wait_ge(s_op, 2 * t + h + 1)
                part = x1(t)[:, h * 512:(h + 1) * 512]
                tt(part, part, psZ[h][:], ALU.add).then_inc(s_x1, 1)

            def h_rows(t):
                dve.wait_ge(s_r2, t + 1)
                dve.wait_ge(s_x1, 2 * t + 2)
                if not (isinstance(t, int) and t == 0):
                    dve.wait_ge(s_hst, 16 * t)
                    dve.wait_ge(s_hTp, t)
                stt(out=h_t[:].rearrange("p (c q) -> p q c", c=DC), in0=x1(t).rearrange("p (q c) -> p q c", c=DC),
                    scalar=small[:, 10:11], in1=ffg[:].rearrange("p (q c) -> p q c", c=DC), op0=ALU.mult, op1=ALU.mult)\
                    .then_inc(s_h, 1)

            def h_out(t):
                dve.wait_ge(s_hTp, t + 1)
                if not (isinstance(t, int) and t == 0):
                    dve.wait_ge(s_lg, t)
                cp(hT[:, 4:8, :].rearrange("p c t -> p (c t)"), psS[:, 512:1024]).then_inc(s_hTv, 1)

            def logits_out(t):
                dve.wait_ge(s_lg, t + 1)
                dst = logits[:, t, :] if isinstance(t, int) else logits[:, bass.ds(t, 1), :].squeeze(1)
                tt(dst, psG[:, 0:NGRP + NE], b_rt[:], ALU.add).then_inc(s_lgo, 1)

            def stage2(t, b):
                first = isinstance(t, int) and t == 0
                if not (isinstance(t, int) and t == T_P):
                    m_lo(t + 1, 1 - b)
                last = isinstance(t, int) and t == T_P
                if last:
                    dve.wait_ge(s_lgo, T - 2)
                    dve.wait_ge(s_op, 2 * T_P)
                    choose_group(0, T - 2)
                if not first:
                    h_out(t - 1)
                if last:
                    choose_experts(0, T - 2)
                residual(t, b, 0)
                if first:
                    sample_weights_out()
                    sample_gmlp()
                residual(t, b, 1)
                if first:
                    sample_values_out()
                    sample_rows_out()
                    dve.wait_ge(s_p2, 64)
                    dve.wait_ge(s_kvout, 5 * 16)
                else:
                    logits_out(t - 1)
                h_rows(t)
                if last:
                    table_columns(0, T - 2)

            sample_products()
            sample_cache_scores()
            split_out(0)
            m_lo(0, 0)
            split_out(1)
            sample_maxima()
            split_out(2)
            split_out(3)
            sample_weights()
            stage2(0, 0)
            with dve.Fori(1, T_P - 2, 2) as t:
                stage2(t, 1)
                stage2(t + 1, 0)
            stage2(T_P - 1, 1)
            stage2(T_P, 0)
            h_out(T_P)
            logits_out(T_P)

            dve.wait_ge(s_lgo, T)
            dve.wait_ge(s_op, 2 * T)
            cp(tr_bf[:], cst[:, C_TR:C_TR + P])
            nc.vector.memset(on_bf[:], 1.0)
            choose_group(T - 2, T)
            choose_experts(T - 2, T)
            table_columns(T - 2, T)
            dve.wait_ge(s_rp, 1)
            cp(rank_s[:].rearrange("p t e -> p (t e)"), psZ[0][:, 0:T * NE])
            step(red(c9[9][:, 0:1], psZ[1][:, 0:NE], AX, ALU.max))
            cp(cnt_i[:], c9[9][:, 0:1])
            step(tt(tmp_r[:], one_e[:], rank_s[:].unsqueeze(1).to_broadcast([P, 2, T, NE]), ALU.mult))
            step(red(rk[:], tmp_r[:], AX, ALU.add))

            def one_hots(done):
                for k in range(2):
                    tt(oh_r[:, k], cst[:, C_IO:C_IO + P].unsqueeze(1).to_broadcast([P, T, P]),
                       rk[:, k, :].unsqueeze(2).to_broadcast([P, T, P]), ALU.is_equal).then_inc(done, 1)

            def table_out(link, done):
                link(cp(tab[:], psG[:, 0:3 * NE]))
                a, b, c = tab[:, 0:NE], tab[:, NE:2 * NE], tab[:, 2 * NE:3 * NE]
                ts(tab2[:, 0, :], c, 0.0, OOB, ALU.is_equal, ALU.mult)
                link(stt(out=tab2[:, 1, :], in0=b, scalar=float(P), in1=a, op0=ALU.mult, op1=ALU.add))
                link(stt(out=tab2[:, 2, :], in0=tab2[:, 1, :], scalar=2.0, in1=c, op0=ALU.mult, op1=ALU.add))
                tt(idx_src[:], tab2[:, 1, :], tab2[:, 0, :], ALU.add)
                link(stt(out=tab2[:, 2, :], in0=tab2[:, 2, :], scalar=-1.0, in1=tab2[:, 0, :], op0=ALU.add, op1=ALU.add))
                cp(idx_dst[:], tab2[:, 2, :]).then_inc(done, 1)

            one_hots(s_rv)
            dve.wait_ge(s_sa, 5)
            gsum = c9[1]
            step(red(gsum[:], g8[0][:, :, 0:4], AX, ALU.add))
            step(ts(c9[8][:], c9[6][:], 1.0, None, ALU.add))
            step(tt(c9[8][:], c9[8][:], gsum[:], ALU.mult))
            step(nc.vector.reciprocal(w_of[:, 0, :], c9[8][:]))
            step(tt(w_of[:, 1, :], w_of[:, 0, :], c9[6][:], ALU.mult))
            dve.wait_ge(s_rp, 2)
            table_out(step, s_idx)
            dve.wait_ge(s_idx, 1)


            def col(ap, e):
                return ap[:, e:e + 1] if isinstance(e, int) else ap[:, bass.ds(e, 1)]

            def src_rows(e, k):
                if not (isinstance(e, int) and e < 4):
                    dve.wait_ge(s_ga[k], (e - k) * 4)
                cp(ic_src[:, k:k + 1], col(idx_src, e)).then_inc(s_isrc, 1)

            def dst_rows(e, k):
                if not (isinstance(e, int) and e < 4):
                    dve.wait_ge(s_sc4[k], (e - k) * 4)
                cp(ic_dst[:, k:k + 1], col(idx_dst, e)).then_inc(s_idst, 1)

            def into_hid(u):
                halves = lambda a: a.rearrange("p (q c) -> p q c", c=2)
                return tt(hid[:].rearrange("p (c q) -> p q c", c=2), halves(sg[:]), halves(u), ALU.mult)

            def g_out(e):
                dve.wait_ge(s_gTp, 2 * e + 2)
                if not (isinstance(e, int) and e == 0):
                    dve.wait_ge(s_gu, e)
                cp(xgT[:, 4:8, :].rearrange("p c t -> p (c t)"), psT[1][:]).then_inc(s_gTv, 1)

            def hid_lo(e):
                dve.wait_ge(s_dTh, e + 1)
                tt(hidT_lo[:].rearrange("p c t -> p (c t)"), psO[:, 0:256],
                   hidT_hi[:].rearrange("p c t -> p (c t)").bitcast(F32), ALU.subtract).then_inc(s_dTl, 1)

            def down_lo(e, k):
                dve.wait_ge(s_wd[k], (e - k + 4) * 4)
                dve.wait_ge(s_wdh, e + 1)
                tt(wd_lo[k][:], wd[k][:], wd_hi[:].bitcast(F32), ALU.subtract).then_inc(s_wdl, 1)

            def y_out(e, k):
                dve.wait_ge(s_dn, e + 1)
                if not (isinstance(e, int) and e < 4):
                    dve.wait_ge(s_sc4[k], (e - k) * 4)
                cp(y_t[k][:, 512:D], psS[:, 512:D]).then_inc(s_yv, 1)

            def stage4(e, k):
                b = k % 2
                dve.wait_ge(s_sg, e + 1)
                if not (isinstance(e, int) and e == 0):
                    dve.wait_ge(s_dTp, e)
                into_hid(psZ[b][:, FE:2 * FE]).then_inc(s_hid, 1)
                if not (isinstance(e, int) and e == NE - 1):
                    g_out(e + 1)
                if not (isinstance(e, int) and e == 0):
                    y_out(e - 1, (k + 3) % 4)
                if not (isinstance(e, int) and e == NE - 1):
                    hid_lo(e)
                if not (isinstance(e, int) and e >= NE - 5):
                    src_rows(e + 5, (k + 1) % 4)
                if not (isinstance(e, int) and e == NE - 1):
                    down_lo(e, k)
                dst_rows(e, k)

            for k in range(4):
                src_rows(k, k)
            g_out(0)
            src_rows(4, 0)
            for k in range(4):
                stage4(k, k)
            with dve.Fori(4, NE - 11, 4) as e:
                for k in range(4):
                    stage4(e + k, k)
            for e in range(NE - 8, NE):
                stage4(e, e % 4)
            y_out(NE - 1, 3)

            most = dve.value_load(cnt_i[0:1, 0:1], min_val=0, max_val=N_TOK)
            with dve.If(most > SLOTS):
                link = Chain(dve, o_step)
                with dve.Fori(0, N_CHUNK - 1) as m:
                    link.n = m * OV_LINKS
                    flat = rk[:].rearrange("p k t -> p (k t)")
                    link(ts(flat, flat, -float(SLOTS), None, ALU.add))
                    one_hots(o_oh)
                    dve.wait_ge(o_tab, m + 1)
                    table_out(link, o_idx)
                    dve.wait_ge(o_idx, m + 1)
                    settle(dve)
                    with dve.Fori(0, NE) as e:
                        n = m * NE + e
                        dve.wait_ge(o_free, n + 1)
                        cp(ic_src[:, 0:1], idx_src[:, bass.ds(e, 1)])
                        cp(ic_dst[:, 0:1], idx_dst[:, bass.ds(e, 1)]).then_inc(o_ic, 1)
                        dve.wait_ge(o_gTp, 2 * n + 2)
                        cp(xgT[:, 4:8, :].rearrange("p c t -> p (c t)"), psT[1][:]).then_inc(o_gTv, 1)
                        dve.wait_ge(o_sg, n + 1)
                        into_hid(psZ[0][:, FE:2 * FE]).then_inc(o_hid, 1)
                        dve.wait_ge(o_dn, n + 1)
                        cp(y_t[0][:, 512:D], psS[:, 512:D]).then_inc(o_y, 1)
            dve.wait_ge(o_done, 1)


            def sum_rows(i):
                t, n = final_tile(i)
                dve.wait_ge(s_yy[i % 4], (i // 4 + 1) * 16)
                step(stt(out=x1(t)[0:n], in0=yy[i % 4][0:n, 0, :], scalar=w_of[0:n, 0, t:t + 1], in1=x1(t)[0:n],
                         op0=ALU.mult, op1=ALU.add))
                stt(out=x1(t)[0:n], in0=yy[i % 4][0:n, 1, :], scalar=w_of[0:n, 1, t:t + 1], in1=x1(t)[0:n],
                    op0=ALU.mult, op1=ALU.add).then_inc(s_ysum, 1)

            def scale_rows(i):
                t, n = final_tile(i)
                dve.wait_ge(s_fr, i + 1)
                dve.wait_ge(s_ysum, i + 1)
                dve.wait_ge(s_fg, 16)
                stt(out=x1(t)[0:n], in0=x1(t)[0:n], scalar=fst[0:n, i % 2, 2:3], in1=fing[0:n], op0=ALU.mult,
                    op1=ALU.mult).then_inc(s_fo, 1)

            for i in range(T):
                sum_rows(i)
                if i > 0:
                    scale_rows(i - 1)
            scale_rows(T_P)

        @block.gpsimd
        def _(pool):
            link = Chain(pool, pool_step)
            ptt = nc.gpsimd.tensor_tensor
            nc.gpsimd.memset(small[:, 1:2], -0.5)
            nc.gpsimd.memset(small[:, 2:3], 1.0 / D)
            link(nc.gpsimd.memset(small[:, 3:4], EPS))

            def rsqrt(out, src, tmp, done, n=P, mean=True):
                if mean:
                    link(ptt(tmp, src, small[0:n, 2:3], ALU.mult))
                link(ptt(tmp, tmp if mean else src, small[0:n, 3:4], ALU.add))
                ptt(out, tmp, small[0:n, 1:2], ALU.pow).then_inc(done, 1)

            def row_scale(t):
                pool.wait_ge(s_sq, t + 1)
                rsqrt(st[:, 2:3], st[:, 0:1], st[:, 1:2], s_rstd)

            def ln_scale(t):
                pool.wait_ge(s_var, t + 1)
                rsqrt(st[:, 6:7], st[:, 4:5], st[:, 5:6], s_lnr, mean=False)

            row_scale(0)
            pool.wait_ge(s_ws, 16)
            nc.gpsimd.affine_select(out=ws_raw[:], in_=ws_raw[:], compare_op=ALU.is_ge, fill=0.0, base=0,
                                    pattern=[[0, NG], [-1, P]], channel_multiplier=1).then_inc(s_wmask, 1)
            n1 = link.n
            with pool.Fori(0, T_P) as t:
                link.n = 3 * t + n1
                row_scale(t + 1)
                ln_scale(t)
            link.n = n1 + 3 * T_P
            ln_scale(T_P)

            def h_scale(t):
                pool.wait_ge(s_sq2, t + 1)
                if not (isinstance(t, int) and t == 0):
                    pool.wait_ge(s_h, t)
                rsqrt(small[:, 10:11], small[:, 8:9], small[:, 9:10], s_r2)

            h_scale(0)
            pool.wait_ge(s_sv, 10)
            nc.gpsimd.dma_start(rows(mix_d, T_P), mix_t[:]).then_inc(s_mix_s, 16)
            n2 = link.n
            with pool.Fori(1, T) as t:
                link.n = 2 * t - 2 + n2
                h_scale(t)
            link.n = n2 + 2 * T_P

            def gather(k, done):
                nc.gpsimd.indirect_dma_start(xg[k][:], None, h_d, bass.IndirectOffsetOnAxis(ic_src[:, k:k + 1].bitcast(U32), 0),
                                             bounds_check=T * P - 1, oob_is_err=False).then_inc(done, 16)

            def scatter(k, done):
                nc.gpsimd.indirect_dma_start(y_d, bass.IndirectOffsetOnAxis(ic_dst[:, k:k + 1].bitcast(U32), 0), y_t[k][:], None,
                                             bounds_check=2 * T * P - 1, oob_is_err=False).then_inc(done, 16)

            def gather4(e, k):
                pool.wait_ge(s_isrc, e + 1)
                if not (isinstance(e, int) and e < 4):
                    pool.wait_ge(s_gTp, 2 * e - 6)
                settle(pool)
                gather(k, s_ga[k])

            def stage4(e, k):
                if not (isinstance(e, int) and e >= NE - 5):
                    gather4(e + 5, (k + 1) % 4)
                pool.wait_ge(s_idst, e + 1)
                pool.wait_ge(s_ya, e + 1)
                pool.wait_ge(s_yv, e + 1)
                settle(pool)
                scatter(k, s_sc4[k])

            pool.wait_ge(s_mTp, 2 * T)
            pool.wait_ge(s_op, 2 * T)
            for k in range(4):
                last = nc.gpsimd.memset(xg[k][:], 0.0)
            last.then_inc(s_zx, 1)
            pool.wait_ge(s_hst, 16 * T)
            pool.wait_ge(s_zx, 1)
            for k in range(4):
                gather4(k, k)
            gather4(4, 0)
            for k in range(4):
                stage4(k, k)
            with pool.Fori(4, NE - 11, 4) as e:
                for k in range(4):
                    stage4(e + k, k)
            for e in range(NE - 8, NE):
                stage4(e, e % 4)
            most = pool.value_load(cnt_i[0:1, 0:1], min_val=0, max_val=N_TOK)
            for k in range(4):
                pool.wait_ge(s_sc4[k], NE // 4 * 16)

            with pool.If(most > SLOTS):
                with pool.Fori(0, (N_CHUNK - 1) * NE) as n:
                    pool.sem_inc(o_free, 1)
                    pool.wait_ge(o_ic, n + 1)
                    settle(pool)
                    gather(0, o_ga)
                    pool.wait_ge(o_ya, n + 1)
                    pool.wait_ge(o_y, n + 1)
                    settle(pool)
                    scatter(0, o_sc)
                    pool.wait_ge(o_sc, 16 * n + 16)
            pool.sem_inc(o_done, 1)

            def final_scale(i, b):
                n = final_tile(i)[1]
                pool.wait_ge(s_fsq, i + 1)
                if not (isinstance(i, int) and i < 2):
                    pool.wait_ge(s_fo, i - 1)
                rsqrt(fst[0:n, b, 2:3], fst[0:n, b, 0:1], fst[0:n, b, 1:2], s_fr, n)

            final_scale(0, 0)
            final_scale(1, 1)
            n6 = link.n
            with pool.Fori(2, T_P - 1, 2) as i:
                link.n = 2 * i - 4 + n6
                final_scale(i, 0)
                final_scale(i + 1, 1)
            link.n = n6 + 2 * T_P - 4
            final_scale(T_P, 0)


def shape_constants():
    import numpy as np
    c = np.zeros((P, C_END), np.float32)
    r = np.arange(P)
    c[:, C_ID:C_ID + P] = np.eye(P)
    causal = np.where(r[None, :] <= r[:, None], 0.0, NEG)
    c[:, C_MF:C_MF + P] = NEG
    c[:, C_MF + P:C_MF + 2 * P] = causal
    c[:, C_MR:C_MR + P] = np.where(r[None, :] >= r[:, None], 0.0, NEG)
    c[:, C_MR + P:C_MR + 2 * P] = causal
    c[:, C_IO:C_IO + P] = r[None, :]
    c[:, C_TR:C_TR + P] = r[:, None] < r[None, :]
    c[:, C_PR] = r
    q = np.arange(64)
    c[q, C_SEL + (q % 32) // QPK] = 1.0
    c[:, C_INV:C_INV + T] = (EPG + 1) * 64.0
    c[N_SAMPLE:, C_INV + T_P] += 1000.0
    c[:, C_TILE:C_TILE + T] = np.arange(T)[None, :]
    inv_freq = (10000.0 ** (-np.arange(HD // 2) * 2.0 / HD)).astype(np.float32)
    for t in range(T):
        pos = (t * P + r if t < T_P else np.full(P, PAST)).astype(np.float32)
        angle = (pos[:, None] * inv_freq[None, :]).astype(np.float64)
        c[:, C_CS + t * HD:C_CS + t * HD + 32] = np.cos(angle)
        c[:, C_CS + t * HD + 32:C_CS + (t + 1) * HD] = np.sin(angle)
    return c


def kernel(**inputs):
    import numpy as np
    import concourse.bacc as bacc
    from concourse.bass_utils import run_bass_kernel_spmd

    a = {k: np.asarray(v) for k, v in inputs.items()}
    x_rows = np.zeros((T * P, D), a["x_prompt"].dtype)
    x_rows[:N_PROMPT] = a["x_prompt"].reshape(N_PROMPT, D)
    x_rows[N_PROMPT:N_TOK] = a["x_sample"].reshape(N_SAMPLE, D)
    sinks = a["attn_sinks"].reshape(NKV, 1, QPK)
    arrays = dict(
        x_rows=x_rows,
        cache_k=a["cache_swa_k"].reshape(N_SAMPLE, WIN, P),
        cache_v=a["cache_swa_v"].reshape(N_SAMPLE, WIN, P),
        mix_g=np.ascontiguousarray(a["norm_mix_g"].reshape(DC, P).T),
        w_in=a["w_in"].reshape(D, Z_COLS),
        sinks_b=a["attn_sinks"].reshape(1, NQ),
        sink_rows=np.ascontiguousarray(np.broadcast_to(sinks, (NKV, N_SAMPLE, QPK)).reshape(64, 1)),
        ln_g=a["gmlp_ln_g"].reshape(1, GW),
        ln_b=a["gmlp_ln_b"].reshape(1, GW),
        w_s=a["gmlp_w_s"].reshape(NG, P, P),
        b_sT=np.ascontiguousarray(a["gmlp_b_s"].reshape(NG, P).T),
        b_s=a["gmlp_b_s"].reshape(NG, P),
        w_out=a["w_out"].reshape(D, D),
        ffn_g=a["norm_ffn_g"].reshape(1, D),
        w_rg=a["router_group_w"].reshape(D, NGRP),
        b_r=np.concatenate([a["router_group_b"].reshape(1, NGRP), a["router_expert_b"].reshape(1, NE)], axis=1),
        w_re=a["router_expert_w"].reshape(D, NE),
        w_gate=a["expert_w_gate"].reshape(NE, D, FE),
        w_up=a["expert_w_up"].reshape(NE, D, FE),
        w_down=a["expert_w_down"].reshape(NE, FE, D),
        fin_g=a["final_norm_g"].reshape(1, D),
        consts=shape_constants(),
    )
    outs = dict(y_rows=(N_TOK, D), k_prompt=(P, P), v_prompt=(P, P), k_sample=(N_SAMPLE, P), v_sample=(N_SAMPLE, P),
                g_sample=(N_SAMPLE, GW))
    nc = bacc.Bacc("TRN2", target_bir_lowering=False, num_devices=1)
    aps = {n: nc.dram_tensor(n, v.shape, mybir.dt.from_np(v.dtype), kind="ExternalInput").ap() for n, v in arrays.items()}
    aps |= {n: nc.dram_tensor(n, s, F32, kind="ExternalOutput").ap() for n, s in outs.items()}
    build(nc, **aps)
    r = run_bass_kernel_spmd(nc, [arrays], core_ids=[0]).results[0]
    y = r["y_rows"]
    return (y[:N_PROMPT].reshape(1, N_PROMPT, D), y[N_PROMPT:].reshape(N_SAMPLE, 1, D),
            r["k_prompt"].reshape(1, 1, WIN, NKV, HD), r["v_prompt"].reshape(1, 1, WIN, NKV, HD),
            r["k_sample"].reshape(1, N_SAMPLE, 1, NKV, HD), r["v_sample"].reshape(1, N_SAMPLE, 1, NKV, HD),
            r["g_sample"].reshape(1, N_SAMPLE, 1, GW))
```
